# Optimizing a Trainium2 kernel written in Bass

```python
import math
import jax, jax.numpy as jnp
from jax import lax
import numpy as np

D_MODEL = 1024
BATCH = 1
SEQ = 1024
DEPTH = 2

GRID_W = 64
CTX_LEN = 256
N_MIXERS = 2
N_HEADS = 8
KV_HEADS = 2
GROUP = N_HEADS // KV_HEADS
HEAD_DIM = D_MODEL // N_HEADS
Q_DIM = N_HEADS * HEAD_DIM
KV_DIM = KV_HEADS * HEAD_DIM
AXIS_DIM = HEAD_DIM // 2
AXIS_PAIRS = AXIS_DIM // 2
ROPE_THETA = 10000.0
Q_BLOCK = 128
ATTN_SCALE = 1.0 / math.sqrt(HEAD_DIM)
POOL_WINDOWS = (2, 4, 8, 16)
POOL_GROUPS = len(POOL_WINDOWS)
POOL_CH = D_MODEL // POOL_GROUPS
D_FF = 2816
CONV_W = 3
N_MOD = 6
EPS = 1e-6


def rmsnorm(x, g):
    xf = x.astype(jnp.float32)
    y = xf * lax.rsqrt(jnp.mean(xf * xf, axis=-1, keepdims=True) + EPS)
    return y.astype(x.dtype) * g

def modulate(h, shift, scale):
    return h * (1.0 + scale) + shift

def axial_rope_tables(rows, cols):
    r = jnp.repeat(jnp.arange(rows, dtype=jnp.float32), cols)
    cc = jnp.tile(jnp.arange(cols, dtype=jnp.float32), rows)
    inv = ROPE_THETA ** (-jnp.arange(AXIS_PAIRS, dtype=jnp.float32) / AXIS_PAIRS)
    ang = jnp.stack([r[:, None] * inv, cc[:, None] * inv], axis=1)
    return jnp.cos(ang), jnp.sin(ang)

def apply_axial_rope(x, cos, sin):
    B, L, H, _ = x.shape
    xa = x.reshape(B, L, H, 2, 2, AXIS_PAIRS)
    x1, x2 = xa[..., 0, :], xa[..., 1, :]
    c = cos[None, :, None]
    s = sin[None, :, None]
    out = jnp.stack([x1 * c - x2 * s, x2 * c + x1 * s], axis=-2)
    return out.reshape(B, L, H, HEAD_DIM).astype(x.dtype)

def qkv_proj(h, w_qkv, g_q, g_k):
    B, L, _ = h.shape
    qkv = h @ w_qkv
    q = qkv[..., :Q_DIM].reshape(B, L, N_HEADS, HEAD_DIM)
    k = qkv[..., Q_DIM:Q_DIM + KV_DIM].reshape(B, L, KV_HEADS, HEAD_DIM)
    v = qkv[..., Q_DIM + KV_DIM:].reshape(B, L, KV_HEADS, HEAD_DIM)
    return rmsnorm(q, g_q), rmsnorm(k, g_k), v

def kv_proj(h, w_qkv, g_k):
    B, L, _ = h.shape
    kv = h @ w_qkv[:, Q_DIM:]
    k = kv[..., :KV_DIM].reshape(B, L, KV_HEADS, HEAD_DIM)
    v = kv[..., KV_DIM:].reshape(B, L, KV_HEADS, HEAD_DIM)
    return rmsnorm(k, g_k), v

def gqa_block(qblk, k, v):
    s = jnp.einsum('bqkgd,bskd->bkgqs', qblk, k, preferred_element_type=jnp.float32) * ATTN_SCALE
    p = jax.nn.softmax(s, axis=-1).astype(v.dtype)
    return jnp.einsum('bkgqs,bskd->bqkgd', p, v)

def latent_attention(q, k_all, v_all):
    B, L, _, _ = q.shape
    nblk = L // Q_BLOCK
    qb = q.reshape(B, nblk, Q_BLOCK, KV_HEADS, GROUP, HEAD_DIM).transpose(1, 0, 2, 3, 4, 5)
    o = lax.map(lambda qblk: gqa_block(qblk, k_all, v_all), qb)
    return o.transpose(1, 0, 2, 3, 4, 5).reshape(B, L, Q_DIM)

def context_attention(q, k, v):
    B, L, _, _ = q.shape
    o = gqa_block(q.reshape(B, L, KV_HEADS, GROUP, HEAD_DIM), k, v)
    return o.reshape(B, L, Q_DIM)

def multiscale_pool_mix(h, w_pool, b_pool, pool_scale):
    B, L, _ = h.shape
    hg = h.reshape(B, L, POOL_GROUPS, POOL_CH)
    csum = jnp.concatenate(
        [jnp.zeros((B, 1, POOL_GROUPS, POOL_CH), jnp.float32),
         jnp.cumsum(hg.astype(jnp.float32), axis=1)], axis=1)
    t = jnp.arange(L)
    means = []
    for g, w in enumerate(POOL_WINDOWS):
        lo = jnp.clip(t - w // 2, 0, L)
        hi = jnp.clip(t + (w - w // 2), 0, L)
        cnt = (hi - lo).astype(jnp.float32)
        cg = csum[:, :, g]
        s = jnp.take(cg, hi, axis=1) - jnp.take(cg, lo, axis=1)
        means.append(s / cnt[None, :, None])
    pooled = jnp.stack(means, axis=2).astype(h.dtype) - hg
    y = jnp.einsum('blgc,gce->blge', pooled, w_pool) + b_pool
    return y.reshape(B, L, D_MODEL) * pool_scale

def conv_ffn(h, w_up, conv_w, conv_b, w_down):
    u = h @ w_up
    gate, val = u[..., :D_FF], u[..., D_FF:]
    gp = jnp.pad(gate, ((0, 0), (1, 1), (0, 0)))
    gate = gp[:, :-2] * conv_w[0] + gp[:, 1:-1] * conv_w[1] + gp[:, 2:] * conv_w[2] + conv_b
    return (jax.nn.silu(gate) * val) @ w_down

def first_inputs(seed: int = 0) -> dict:
    key = jax.random.key(seed)
    ks = jax.random.split(key, 32)
    f32 = jnp.float32
    n_attn = (DEPTH + N_MIXERS - 1) // N_MIXERS
    n_pool = DEPTH // N_MIXERS
    nrm = lambda k, shape, s: jax.random.normal(k, shape, f32) * s
    gain = lambda k, shape: 1.0 + 0.05 * jax.random.normal(k, shape, f32)
    return {
        "x": nrm(ks[0], (BATCH, SEQ, D_MODEL), 1.0),
        "c": nrm(ks[1], (BATCH, D_MODEL), 1.0),
        "ctx": nrm(ks[2], (BATCH, CTX_LEN, D_MODEL), 1.0),
        "c_ctx": nrm(ks[3], (D_MODEL,), 1.0),
        "w_mod": nrm(ks[4], (DEPTH, D_MODEL, N_MOD * D_MODEL), 0.5 * D_MODEL ** -0.5),
        "b_mod": nrm(ks[5], (DEPTH, N_MOD * D_MODEL), 0.02),
        "g_pre_mix": gain(ks[6], (DEPTH, D_MODEL)),
        "g_post_mix": gain(ks[7], (DEPTH, D_MODEL)),
        "g_pre_ffn": gain(ks[8], (DEPTH, D_MODEL)),
        "g_post_ffn": gain(ks[9], (DEPTH, D_MODEL)),
        "w_qkv": nrm(ks[10], (n_attn, D_MODEL, Q_DIM + 2 * KV_DIM), D_MODEL ** -0.5),
        "g_q": gain(ks[11], (n_attn, HEAD_DIM)),
        "g_k": gain(ks[12], (n_attn, HEAD_DIM)),
        "w_o": nrm(ks[13], (n_attn, Q_DIM, D_MODEL), Q_DIM ** -0.5),
        "w_pool": nrm(ks[14], (n_pool, POOL_GROUPS, POOL_CH, POOL_CH), POOL_CH ** -0.5),
        "b_pool": nrm(ks[15], (n_pool, POOL_GROUPS, POOL_CH), 0.02),
        "pool_scale": gain(ks[16], (n_pool, D_MODEL)),
        "w_up": nrm(ks[17], (DEPTH, D_MODEL, 2 * D_FF), D_MODEL ** -0.5),
        "conv_w": nrm(ks[18], (DEPTH, CONV_W, D_FF), CONV_W ** -0.5),
        "conv_b": nrm(ks[19], (DEPTH, D_FF), 0.02),
        "w_down": nrm(ks[20], (DEPTH, D_FF, D_MODEL), D_FF ** -0.5),
    }

def first_block(x, c, ctx, c_ctx, w_mod, b_mod, g_pre_mix, g_post_mix, g_pre_ffn, g_post_ffn,
              w_qkv, g_q, g_k, w_o, w_pool, b_pool, pool_scale, w_up, conv_w, conv_b, w_down):
    B, L, _ = x.shape
    ROWS = L // GRID_W
    cos, sin = axial_rope_tables(ROWS, GRID_W)
    sc = jax.nn.silu(c)
    sc_ctx = jax.nn.silu(c_ctx)
    for i in range(DEPTH):
        mixer = i % N_MIXERS
        j = i // N_MIXERS
        update_ctx = any(jj % N_MIXERS == 0 for jj in range(i + 1, DEPTH))
        m = (sc @ w_mod[i] + b_mod[i]).reshape(B, N_MOD, D_MODEL)[:, :, None, :]
        mc = (sc_ctx @ w_mod[i] + b_mod[i]).reshape(N_MOD, D_MODEL)
        shift_m, scale_m, gate_m, shift_f, scale_f, gate_f = [m[:, k] for k in range(N_MOD)]
        cshift_m, cscale_m, cgate_m, cshift_f, cscale_f, cgate_f = [mc[k] for k in range(N_MOD)]

        h = modulate(rmsnorm(x, g_pre_mix[i]), shift_m, scale_m)
        hc = modulate(rmsnorm(ctx, g_pre_mix[i]), cshift_m, cscale_m)
        if mixer == 0:
            q, k, v = qkv_proj(h, w_qkv[j], g_q[j], g_k[j])
            q = apply_axial_rope(q, cos, sin)
            k = apply_axial_rope(k, cos, sin)
            if update_ctx:
                qc, kc, vc = qkv_proj(hc, w_qkv[j], g_q[j], g_k[j])
            else:
                kc, vc = kv_proj(hc, w_qkv[j], g_k[j])
            k_all = jnp.concatenate([kc, k], axis=1)
            v_all = jnp.concatenate([vc, v], axis=1)
            y = latent_attention(q, k_all, v_all) @ w_o[j]
            if update_ctx:
                yc = context_attention(qc, kc, vc) @ w_o[j]
        else:
            y = multiscale_pool_mix(h, w_pool[j], b_pool[j], pool_scale[j])
            if update_ctx:
                yc = multiscale_pool_mix(hc, w_pool[j], b_pool[j], pool_scale[j])
        x = x + gate_m * rmsnorm(y, g_post_mix[i])
        if update_ctx:
            ctx = ctx + cgate_m * rmsnorm(yc, g_post_mix[i])

        h = modulate(rmsnorm(x, g_pre_ffn[i]), shift_f, scale_f)
        x = x + gate_f * rmsnorm(conv_ffn(h, w_up[i], conv_w[i], conv_b[i], w_down[i]), g_post_ffn[i])
        if update_ctx:
            hc = modulate(rmsnorm(ctx, g_pre_ffn[i]), cshift_f, cscale_f)
            ctx = ctx + cgate_f * rmsnorm(conv_ffn(hc, w_up[i], conv_w[i], conv_b[i], w_down[i]), g_post_ffn[i])
    return x


DEPTH_2 = 1

D_MIX = D_MODEL
D_LRU = D_MIX // 2
LRU_HEADS = 8
LRU_HEAD_DIM = D_LRU // LRU_HEADS
LRU_CONV = 4
LRU_C = 8.0
D_RET = D_MIX - D_LRU
RET_HEADS = 4
RET_HEAD_DIM = D_RET // RET_HEADS
RET_CHUNK = 128
ROPE_BASE = 10000.0
D_IN = 2 * D_LRU + 4 * D_RET
SPLITS = (D_LRU, 2 * D_LRU, 2 * D_LRU + D_RET, 2 * D_LRU + 2 * D_RET, 2 * D_LRU + 3 * D_RET)
D_FF_2 = 3 * D_MODEL
FFN_CONV = 3
NORM_EPS = 1e-6


def rms_norm(x, gain):
    xf = x.astype(jnp.float32)
    y = xf * lax.rsqrt(jnp.mean(xf * xf, axis=-1, keepdims=True) + NORM_EPS)
    return (y * gain.astype(jnp.float32)).astype(x.dtype)

def causal_depthwise_conv(x, w, b):
    width, ch = w.shape
    y = lax.conv_general_dilated(
        x, w[:, None, :].astype(x.dtype), window_strides=(1,),
        padding=[(width - 1, 0)], dimension_numbers=("NWC", "WIO", "NWC"),
        feature_group_count=ch)
    return y + b.astype(x.dtype)

def _linear_recurrence_combine(left, right):
    a1, b1 = left
    a2, b2 = right
    return a1 * a2, a2 * b1 + b2

def rg_lru(x, wa, ba, wx, bx, lam):
    bsz, slen, _ = x.shape
    xf = x.astype(jnp.float32)
    xh = xf.reshape(bsz, slen, LRU_HEADS, LRU_HEAD_DIM)
    r = jax.nn.sigmoid(jnp.einsum("bshi,hij->bshj", xh, wa.astype(jnp.float32)).reshape(bsz, slen, D_LRU)
                       + ba.astype(jnp.float32))
    i = jax.nn.sigmoid(jnp.einsum("bshi,hij->bshj", xh, wx.astype(jnp.float32)).reshape(bsz, slen, D_LRU)
                       + bx.astype(jnp.float32))
    log_a = -LRU_C * r * jax.nn.softplus(-lam.astype(jnp.float32))
    a = jnp.exp(log_a)
    inp = jnp.sqrt(-jnp.expm1(2.0 * log_a)) * (i * xf)
    _, h = lax.associative_scan(_linear_recurrence_combine, (a, inp), axis=1)
    return h

def rotary(x, cos, sin):
    half = x.shape[-1] // 2
    x1, x2 = x[..., :half], x[..., half:]
    return jnp.concatenate([x1 * cos - x2 * sin, x2 * cos + x1 * sin], axis=-1)

def retention_chunkwise(q, k, v):
    bsz, slen, nh, dk = q.shape
    dv = v.shape[-1]
    c = RET_CHUNK
    n = slen // c
    log_g = jnp.log1p(-jnp.exp2(-5.0 - jnp.arange(nh, dtype=jnp.float32)))
    q = q.reshape(bsz, n, c, nh, dk)
    k = (k * (dk ** -0.5)).reshape(bsz, n, c, nh, dk)
    v = v.reshape(bsz, n, c, nh, dv)
    idx = jnp.arange(c, dtype=jnp.float32)
    diff = idx[:, None] - idx[None, :]
    decay_in = jnp.where(diff[None] >= 0, jnp.exp(jnp.maximum(diff, 0.0)[None] * log_g[:, None, None]), 0.0)
    scores = jnp.einsum("bnihd,bnjhd->bnhij", q, k) * decay_in[None, None]
    inner = jnp.einsum("bnhij,bnjhe->bnihe", scores, v)
    zeta = jnp.exp((c - 1 - idx)[None, :] * log_g[:, None])
    kv = jnp.einsum("bnjhd,bnjhe,hj->nbhde", k, v, zeta)
    g_chunk = jnp.exp(c * log_g)[None, :, None, None]

    def step(state, kv_n):
        return state * g_chunk + kv_n, state

    init = jnp.zeros((bsz, nh, dk, dv), jnp.float32)
    _, prev = lax.scan(step, init, kv)
    xi = jnp.exp((idx + 1.0)[None, :] * log_g[:, None])
    cross = jnp.einsum("bnihd,nbhde,hi->bnihe", q, prev, xi)
    return (inner + cross).reshape(bsz, slen, nh, dv)

def head_group_norm(o, gain):
    mu = jnp.mean(o, axis=-1, keepdims=True)
    var = jnp.mean(jnp.square(o - mu), axis=-1, keepdims=True)
    return (o - mu) * lax.rsqrt(var + NORM_EPS) * gain.astype(jnp.float32).reshape(RET_HEADS, RET_HEAD_DIM)

def second_inputs(seed: int = 0) -> dict:
    key = jax.random.key(seed)
    ks = jax.random.split(key, 20)
    f32 = jnp.float32

    def nrm(k, shape, fan_in):
        return jax.random.normal(k, shape, f32) * (fan_in ** -0.5)

    def gain(k, shape):
        return 1.0 + 0.05 * jax.random.normal(k, shape, f32)

    def bias(k, shape):
        return 0.02 * jax.random.normal(k, shape, f32)

    a0 = jax.random.uniform(ks[9], (DEPTH_2, D_LRU), f32, minval=0.9, maxval=0.999)
    return {
        "x": jax.random.normal(ks[0], (BATCH, SEQ, D_MODEL), f32),
        "norm1_gain": gain(ks[1], (DEPTH_2, D_MODEL)),
        "w_in": nrm(ks[2], (DEPTH_2, D_MODEL, D_IN), D_MODEL),
        "lru_conv_w": nrm(ks[3], (DEPTH_2, LRU_CONV, D_LRU), LRU_CONV),
        "lru_conv_b": bias(ks[4], (DEPTH_2, D_LRU)),
        "lru_gate_a_w": nrm(ks[5], (DEPTH_2, LRU_HEADS, LRU_HEAD_DIM, LRU_HEAD_DIM), LRU_HEAD_DIM),
        "lru_gate_a_b": bias(ks[6], (DEPTH_2, D_LRU)),
        "lru_gate_x_w": nrm(ks[7], (DEPTH_2, LRU_HEADS, LRU_HEAD_DIM, LRU_HEAD_DIM), LRU_HEAD_DIM),
        "lru_gate_x_b": bias(ks[8], (DEPTH_2, D_LRU)),
        "lru_lambda": jnp.log(a0) - jnp.log1p(-a0),
        "lru_norm_gain": gain(ks[10], (DEPTH_2, D_LRU)),
        "ret_norm_gain": gain(ks[11], (DEPTH_2, D_RET)),
        "w_out": nrm(ks[12], (DEPTH_2, D_MIX, D_MODEL), D_MIX),
        "norm2_gain": gain(ks[13], (DEPTH_2, D_MODEL)),
        "ffn_up_w": nrm(ks[14], (DEPTH_2, D_MODEL, 2 * D_FF_2), D_MODEL),
        "ffn_conv_w": nrm(ks[15], (DEPTH_2, FFN_CONV, 2 * D_FF_2), FFN_CONV),
        "ffn_conv_b": bias(ks[16], (DEPTH_2, 2 * D_FF_2)),
        "ffn_down_w": nrm(ks[17], (DEPTH_2, D_FF_2, D_MODEL), D_FF_2),
        "final_norm_gain": gain(ks[18], (D_MODEL,)),
    }

def second_block(x, norm1_gain, w_in, lru_conv_w, lru_conv_b, lru_gate_a_w, lru_gate_a_b,
              lru_gate_x_w, lru_gate_x_b, lru_lambda, lru_norm_gain, ret_norm_gain, w_out,
              norm2_gain, ffn_up_w, ffn_conv_w, ffn_conv_b, ffn_down_w, final_norm_gain):
    bsz, slen, _ = x.shape
    dt = x.dtype
    pos = jnp.arange(slen, dtype=jnp.float32)
    inv_freq = ROPE_BASE ** (-jnp.arange(0, RET_HEAD_DIM, 2, dtype=jnp.float32) / RET_HEAD_DIM)
    ang = pos[:, None] * inv_freq[None, :]
    cos = jnp.cos(ang)[:, None, :]
    sin = jnp.sin(ang)[:, None, :]

    h = x
    for l in range(DEPTH_2):
        u = rms_norm(h, norm1_gain[l])
        proj = u @ w_in[l].astype(dt)
        x_lru, g_lru, q, k, v, g_ret = jnp.split(proj, SPLITS, axis=-1)

        xc = causal_depthwise_conv(x_lru, lru_conv_w[l], lru_conv_b[l])
        hl = rg_lru(xc, lru_gate_a_w[l], lru_gate_a_b[l], lru_gate_x_w[l], lru_gate_x_b[l], lru_lambda[l])
        y_lru = rms_norm(hl.astype(dt) * jax.nn.gelu(g_lru), lru_norm_gain[l])

        qh = rotary(q.astype(jnp.float32).reshape(bsz, slen, RET_HEADS, RET_HEAD_DIM), cos, sin)
        kh = rotary(k.astype(jnp.float32).reshape(bsz, slen, RET_HEADS, RET_HEAD_DIM), cos, sin)
        vh = v.astype(jnp.float32).reshape(bsz, slen, RET_HEADS, RET_HEAD_DIM)
        o = head_group_norm(retention_chunkwise(qh, kh, vh), ret_norm_gain[l]).reshape(bsz, slen, D_RET)
        y_ret = o.astype(dt) * jax.nn.silu(g_ret)

        mixed = jnp.concatenate([y_lru, y_ret], axis=-1)
        h = h + mixed @ w_out[l].astype(dt)

        u = rms_norm(h, norm2_gain[l])
        up = causal_depthwise_conv(u @ ffn_up_w[l].astype(dt), ffn_conv_w[l], ffn_conv_b[l])
        a_branch, v_branch = jnp.split(up, 2, axis=-1)
        h = h + (jax.nn.gelu(a_branch) * v_branch) @ ffn_down_w[l].astype(dt)

    return rms_norm(h, final_norm_gain)


def setup_inputs(seed=0):
    out = dict(first_inputs(seed))
    for name, value in second_inputs(seed + 1).items():
        if name != "x":
            out[name + "_2"] = value
    return out


def reference(
    x, c, ctx, c_ctx, w_mod, b_mod, g_pre_mix, g_post_mix, g_pre_ffn, g_post_ffn, w_qkv, g_q,
    g_k, w_o, w_pool, b_pool, pool_scale, w_up, conv_w, conv_b, w_down, norm1_gain_2, w_in_2,
    lru_conv_w_2, lru_conv_b_2, lru_gate_a_w_2, lru_gate_a_b_2, lru_gate_x_w_2, lru_gate_x_b_2,
    lru_lambda_2, lru_norm_gain_2, ret_norm_gain_2, w_out_2, norm2_gain_2, ffn_up_w_2,
    ffn_conv_w_2, ffn_conv_b_2, ffn_down_w_2, final_norm_gain_2,
):
    x = first_block(
        x, c, ctx, c_ctx, w_mod, b_mod, g_pre_mix, g_post_mix, g_pre_ffn, g_post_ffn, w_qkv,
        g_q, g_k, w_o, w_pool, b_pool, pool_scale, w_up, conv_w, conv_b, w_down,
    )
    return second_block(
        x, norm1_gain_2, w_in_2, lru_conv_w_2, lru_conv_b_2, lru_gate_a_w_2, lru_gate_a_b_2,
        lru_gate_x_w_2, lru_gate_x_b_2, lru_lambda_2, lru_norm_gain_2, ret_norm_gain_2, w_out_2,
        norm2_gain_2, ffn_up_w_2, ffn_conv_w_2, ffn_conv_b_2, ffn_down_w_2, final_norm_gain_2,
    )


_drawn_inputs = setup_inputs


def setup_inputs(seed=0):
    import zlib

    import numpy as np

    out = dict(_drawn_inputs(seed))
    spreads = {}
    factors = {'g_pre_mix': 2.913,
     'g_q': 8.0,
     'g_k': 8.0,
     'b_pool': 12.231,
     'pool_scale': 9.053,
     'conv_b': 5.725,
     'lru_gate_a_b_2': 32.295,
     'lru_gate_x_b_2': 8.0,
     'ret_norm_gain_2': 3.316,
     'ffn_conv_b_2': 4.953,
     'lru_norm_gain_2': 3.049,
     'norm2_gain_2': 3.426}
    for name, (base, spread) in spreads.items():
        noise = np.random.default_rng([zlib.crc32(name.encode()), seed]).standard_normal(out[name].shape)
        drawn = base * np.exp(spread * noise) if base else spread * noise
        out[name] = __import__('jax').numpy.asarray(drawn.astype(out[name].dtype))
    for name, factor in factors.items():
        out[name] = (out[name] * factor).astype(out[name].dtype)
    return out
```

```python
import math

import numpy as np

import concourse.bass as bass
from concourse import mybir

F32 = mybir.dt.float32
F32R = mybir.dt.float32r
ALU = mybir.AluOpType
ACT = mybir.ActivationFunctionType
AX_X = mybir.AxisListType.X

P = 128
D = 1024
KD = D // P
T = 1024
HALF = 512
TT = T // P
CTX = 256
KEYS = CTX + T
HEADS, KV, GROUP = 8, 2, 4
FF1, FF2 = 2816 // P, 3072 // P
RET_HEADS = 4
EPS = 1e-6
ATT_SCALE = 1.0 / math.sqrt(P)
RET_SCALE = float(P) ** -0.5
RET_DECAY = [float(np.log1p(-np.exp2(np.float32(-5.0 - h)))) for h in range(RET_HEADS)]
LRU_C = 8.0

BASE = 16512
CONST = 0
W_RAW = 7936
W_HI = W_RAW + 2 * 4096
W_LO = W_HI + 2 * 4096
YX = W_LO + 2 * 4096
XN = YX + 16384
A0 = XN + 65536
END = A0 + 24 * 4096


class Counters:

    def __init__(self, nc):
        self.nc, self.sems, self.reached = nc, {}, {}

    def __getitem__(self, name):
        if name not in self.sems:
            self.sems[name] = self.nc.alloc_semaphore(name)
            self.reached.setdefault(name, 0)
        return self.sems[name]

    def take(self, name, total):
        self[name]
        before = self.reached[name]
        self.reached[name] = before + total
        return before


class Memory:

    def __init__(self, nc):
        self.nc, self.small = nc, CONST

        def at(name, offset, shape, dtype=F32):
            return nc.alloc_sbuf_tensor_at(name, shape, dtype, offset=BASE + offset)

        self.at = at
        self.w_raw = at("w_raw", W_RAW, [P, 2, 8, P])
        self.w_hi = at("w_hi", W_HI, [P, 2, 8, P], F32R)
        self.w_lo = at("w_lo", W_LO, [P, 2, 8, P], F32R)
        self.xn_hi = at("xn_hi", XN, [P, KD, T], F32R)
        self.xn_lo = at("xn_lo", XN + 32768, [P, KD, T], F32R)
        self.ring = at("ring", XN, [P, 32, HALF], F32R)
        self.a = at("a", A0, [P, 24, T])
        self.a_lo = [at(f"a_lo{i}", A0 + 32768 * i, [P, 8, T], F32R) for i in range(3)]
        self.x = self.a[:, 8:16, :]
        self.yx = at("yx", YX, [P, KD, HALF])
        self.xnc_hi = at("xnc_hi", YX, [P, KD, CTX], F32R)
        self.xnc_lo = at("xnc_lo", YX + 8192, [P, KD, CTX], F32R)
        self.ps = nc.alloc_psum_tensor("ps", [P, 8, 512], F32)

    def vec(self, name, shape):
        n = 4 * int(np.prod(shape[1:]))
        t = self.at(name, self.small, shape)
        self.small += (n + 31) // 32 * 32
        assert self.small <= W_RAW, self.small
        return t


def stand_alone(eng, c):
    eng.sem_inc(c[f"waits_passed_{str(eng.engine).split('.')[-1].lower()}"], 1)


class WeightStream:

    def __init__(self, c, m, units):
        assert units % 2 == 0
        self.c, self.m = c, m
        self.raw0 = [c.take(f"w_raw{s}", 16 * units // 2) for s in (0, 1)]
        self.hi0 = c.take("w_hi", units)
        self.lo0 = c.take("w_lo", units)
        self.done0 = c.take("unit_done", units)

    def load(self, sp, u, slot, src):
        kc = src.shape[1]
        sp.wait_ge(self.c["w_lo"], self.lo0 + u + 1)
        sp.dma_start(self.m.w_raw[:, slot, 0:kc, :], src).then_inc(self.c[f"w_raw{slot}"], 16)

    def split(self, pool, u, pair, slot, kc):
        raw = self.m.w_raw[:, slot, 0:kc, :]
        hi = self.m.w_hi[:, slot, 0:kc, :]
        pool.wait_ge(self.c[f"w_raw{slot}"], 16 * pair + self.raw0[slot] + 16)
        pool.wait_ge(self.c["unit_done"], self.done0 + u + 1)
        stand_alone(pool, self.c)
        pool.tensor_scalar(hi, raw, 1.0, 1.0, ALU.mult, ALU.mult).then_inc(self.c["w_hi"], 1)
        pool.wait_ge(self.c["w_hi"], self.hi0 + u + 1)
        pool.tensor_tensor(self.m.w_lo[:, slot, 0:kc, :], raw, hi.bitcast(F32),
                           ALU.subtract).then_inc(self.c["w_lo"], 1)

    def ready(self, pe, u):
        pe.wait_ge(self.c["w_lo"], self.lo0 + u + 3)

    def products(self, pe, slot, out, k, hi, lo, start, stop):
        w_hi, w_lo = self.m.w_hi[:, slot, k, :], self.m.w_lo[:, slot, k, :]
        pe.matmul(out, w_hi, hi, start=start, stop=False)
        pe.matmul(out, w_hi, lo, start=False, stop=False)
        return pe.matmul(out, w_lo, hi, start=False, stop=stop)

    def finished(self, eng, u):
        eng.wait_ge(self.c["unit_done"], self.done0 + u + 3)


class RootMeanSquare:

    def __init__(self, c, m, name, groups, chunks, tiles, count, source, squares, stat, turned,
                 broadcast, small):
        self.c, self.m = c, m
        self.groups, self.chunks, self.tiles, self.count = groups, chunks, tiles, count
        self.source, self.squares = source, squares
        self.stat, self.turned, self.broadcast = stat, turned, broadcast
        self.cols = groups * tiles
        self.sd = m.rms_sd[:, small:small + self.cols]
        self.rs = m.rms_rs[:, small:small + self.cols]
        self.row = m.rms_row[small // 4] if self.cols <= 4 else m.rms_rows
        n = groups * chunks
        self.n = n
        self.sq0 = c.take("rms_squared", n)
        self.sum0 = c.take("rms_summed", n)
        self.sd0 = c.take("rms_root", 1)
        self.rc0 = c.take("rms_inverse", 1)
        self.tr0 = c.take("rms_turned", 1)
        self.row0 = c.take("rms_row", 1)
        self.rb0 = c.take("rms_broadcast", groups)
        self.free0 = c.take("rms_broadcast_used", groups if groups > len(broadcast) else 0)

    def act_squares(self, act, before=None):
        slots = len(self.squares)
        for i in range(self.n):
            if before:
                before(i)
            if i >= slots:
                act.wait_ge(self.c["rms_summed"], self.sum0 + i - slots + 1)
            src, out = self.source(i), self.squares[i % slots]
            if len(src.shape) == 3:
                out = out.rearrange("p (a t) -> p a t", a=src.shape[1])
            act.activation(out, src, ACT.Square).then_inc(self.c["rms_squared"], 1)

    def pe_sums(self, pe):
        for i in range(self.n):
            pe.wait_ge(self.c["rms_squared"], self.sq0 + i + 1)
            g, k = divmod(i, self.chunks)
            for t in range(self.tiles):
                col = g * self.tiles + t
                last = pe.matmul(self.stat[:, col:col + 1],
                                 self.squares[i % len(self.squares)][:, t * P:(t + 1) * P],
                                 self.m.ones[:, 0:1], start=(k == 0 and t == 0),
                                 stop=(k == self.chunks - 1), skip_group_check=True)
            last.then_inc(self.c["rms_summed"], 1)

    def act_root(self, act):
        act.wait_ge(self.c["rms_summed"], self.sum0 + self.n)
        act.activation(self.sd, self.stat[:, 0:self.cols], ACT.Sqrt, bias=self.m.eps[:, 0:1],
                       scale=1.0 / self.count).then_inc(self.c["rms_root"], 1)

    def dve_inverse(self, dve):
        dve.wait_ge(self.c["rms_root"], self.sd0 + 1)
        dve.reciprocal(self.rs, self.sd).then_inc(self.c["rms_inverse"], 1)

    def pe_turn(self, pe):
        pe.wait_ge(self.c["rms_inverse"], self.rc0 + 1)
        pe.transpose(self.turned[0:self.cols, 0:P], self.rs, self.m.ident[:]
                     ).then_inc(self.c["rms_turned"], 1)

    def dve_row(self, dve):
        dve.wait_ge(self.c["rms_turned"], self.tr0 + 1)
        dve.tensor_copy(self.row[0:self.cols, :], self.turned[0:self.cols, 0:P]
                        ).then_inc(self.c["rms_row"], 1)

    def pe_broadcast(self, pe, g):
        banks = len(self.broadcast)
        if g == 0:
            pe.wait_ge(self.c["rms_row"], self.row0 + 1)
        if g >= banks:
            pe.wait_ge(self.c["rms_broadcast_used"], self.free0 + g - banks + 1)
        out = self.broadcast[g % banks]
        for t in range(self.tiles):
            col = g * self.tiles + t
            last = pe.matmul(out[:, t * P:(t + 1) * P],
                             self.m.ident[0:self.cols, col:col + 1].to_broadcast([self.cols, P]),
                             self.row[0:self.cols, :], start=True, stop=True)
        last.then_inc(self.c["rms_broadcast"], 1)

    def ready(self, eng, g):
        eng.wait_ge(self.c["rms_broadcast"], self.rb0 + g + 1)
        return self.broadcast[g % len(self.broadcast)][:, 0:self.tiles * P]

    def used(self, last):
        return last.then_inc(self.c["rms_broadcast_used"], 1)


class PreNorm:

    def __init__(self, c, m, name, parts, split=True):
        self.c, self.m, self.parts, self.split = c, m, parts, split
        n = KD * len(parts)
        self.x0, self.aff0 = c.take("pre_scaled", n), c.take("pre_shifted", n)
        self.h0, self.l0 = c.take("pre_hi", n if split else 0), c.take("pre_lo", n if split else 0)
        self.rms = [
            RootMeanSquare(c, m, f"{name}{j}", 1, KD, p["tiles"], D, p["source"], p["squares"],
                           p["stat"], p["turned"], [p["bank"]], p["small"])
            for j, p in enumerate(parts)]

    def act(self, act):
        for j, (p, rms) in enumerate(zip(self.parts, self.rms)):
            rms.act_squares(act)
            rms.act_root(act)
            for k in range(KD):
                i = j * KD + k
                act.wait_ge(self.c["pre_scaled"], self.x0 + i + 1)
                act.activation(p["work"](k), p["work"](k), ACT.Identity, bias=p["shift"](k),
                               scale=p["scale"](k)).then_inc(self.c["pre_shifted"], 1)

    def pe_sums(self, pe, j):
        self.rms[j].pe_sums(pe)

    def pe_spread(self, pe, j):
        self.rms[j].pe_turn(pe)
        self.rms[j].pe_broadcast(pe, 0)

    def pool(self, pool):
        for j, p in enumerate(self.parts):
            for k in range(KD):
                i = j * KD + k
                pool.wait_ge(self.c["pre_shifted"], self.aff0 + i + 1)
                pool.tensor_scalar(p["hi"](k), p["work"](k), 1.0, 1.0, ALU.mult, ALU.mult
                                   ).then_inc(self.c["pre_hi"], 1)

    def dve(self, dve):
        for j, (p, rms) in enumerate(zip(self.parts, self.rms)):
            rms.dve_inverse(dve)
            rms.dve_row(dve)
            bank = rms.ready(dve, 0)
            for k in range(KD):
                last = dve.tensor_tensor(p["work"](k), p["source"](k), bank, ALU.mult)
                last.then_inc(self.c["pre_scaled"], 1)
            if self.split:
                for k in range(KD):
                    i = j * KD + k
                    dve.wait_ge(self.c["pre_hi"], self.h0 + i + 1)
                    dve.tensor_tensor(p["lo"](k), p["work"](k), p["hi"](k).bitcast(F32),
                                      ALU.subtract).then_inc(self.c["pre_lo"], 1)

    def ready(self, eng, part, k=KD - 1):
        eng.wait_ge(self.c["pre_lo"], self.l0 + part * KD + k + 1)


def halves_parts(m, scale, shift, work=0, squares=8):
    def part(h):
        s = slice(h * HALF, (h + 1) * HALF)
        return dict(
            source=lambda k: m.x[:, k, s], work=lambda k: m.a[:, work + k, s],
            hi=lambda k: m.xn_hi[:, k, s], lo=lambda k: m.xn_lo[:, k, s],
            scale=scale, shift=shift, tiles=4, stat=m.ps[:, 4, 8 * h:8 * h + 8],
            turned=m.ps[:, 5, h * P:(h + 1) * P], bank=m.ps[:, 6 + h, :], small=4 * h,
            squares=[m.a[:, 16 + i, s] for i in range(squares)])
    return [part(0), part(1)]


def load_vectors(nc, c, m, ins):
    lists = [
        ("b_mod", ins["b_mod"].rearrange("l (k p) -> (l k) p", p=P)),
        ("c", ins["c"].rearrange("b (k p) -> (b k) p", p=P)),
        ("c_ctx", ins["c_ctx"].rearrange("(k p) -> k p", p=P)),
        ("g_pre_mix", ins["g_pre_mix"].rearrange("l (k p) -> (l k) p", p=P)),
        ("g_post_mix", ins["g_post_mix"].rearrange("l (k p) -> (l k) p", p=P)),
        ("g_pre_ffn", ins["g_pre_ffn"].rearrange("l (k p) -> (l k) p", p=P)),
        ("g_post_ffn", ins["g_post_ffn"].rearrange("l (k p) -> (l k) p", p=P)),
        ("b_pool", ins["b_pool"].rearrange("j g (k p) -> (j g k) p", p=P)),
        ("pool_scale", ins["pool_scale"].rearrange("j (k p) -> (j k) p", p=P)),
        ("g_q", ins["g_q"]), ("g_k", ins["g_k"]),
        ("norm1", ins["norm1_gain_2"].rearrange("j (k p) -> (j k) p", p=P)),
        ("norm2", ins["norm2_gain_2"].rearrange("j (k p) -> (j k) p", p=P)),
        ("final", ins["final_norm_gain_2"].rearrange("(k p) -> k p", p=P)),
        ("conv_w0", ins["conv_w"][0].rearrange("w (k p) -> (w k) p", p=P)),
        ("conv_w1", ins["conv_w"][1].rearrange("w (k p) -> (w k) p", p=P)),
        ("conv_b", ins["conv_b"].rearrange("l (k p) -> (l k) p", p=P)),
        ("lru_conv_w", ins["lru_conv_w_2"].rearrange("j w (k p) -> (j w k) p", p=P)),
        ("lru_conv_b", ins["lru_conv_b_2"].rearrange("j (k p) -> (j k) p", p=P)),
        ("gate_a_b", ins["lru_gate_a_b_2"].rearrange("j (k p) -> (j k) p", p=P)),
        ("gate_x_b", ins["lru_gate_x_b_2"].rearrange("j (k p) -> (j k) p", p=P)),
        ("lambda", ins["lru_lambda_2"].rearrange("j (k p) -> (j k) p", p=P)),
        ("lru_norm", ins["lru_norm_gain_2"].rearrange("j (k p) -> (j k) p", p=P)),
        ("ret_norm", ins["ret_norm_gain_2"].rearrange("j (k p) -> (j k) p", p=P)),
        ("ffn_w0", ins["ffn_conv_w_2"][0, 0].rearrange("(k p) -> k p", p=P)),
        ("ffn_w1", ins["ffn_conv_w_2"][0, 1].rearrange("(k p) -> k p", p=P)),
        ("ffn_w2", ins["ffn_conv_w_2"][0, 2].rearrange("(k p) -> k p", p=P)),
        ("ffn_b", ins["ffn_conv_b_2"].rearrange("j (k p) -> (j k) p", p=P)),
    ]
    fill, place = [], {}
    for name, ap in sorted(lists, key=lambda x: -x[1].shape[0]):
        n = ap.shape[0]
        tile = next((i for i, f in enumerate(fill) if f + n <= P), len(fill))
        if tile == len(fill):
            fill.append(0)
        place[name] = (tile, fill[tile], n)
        fill[tile] += n
    tiles = len(fill)
    m.vt = m.vec("vt", [P, tiles * P])
    m.col = {name: tile * P + at for name, (tile, at, n) in place.items()}
    m.ident = m.vec("ident", [P, P])
    m.mod = m.vec("mod", [P, 2, 48, 2])
    m.silu_c = m.vec("silu_c", [P, KD, 2])
    m.eps = m.vec("eps", [P, 1])
    m.ones = m.vec("ones", [P, 1])
    m.rms_sd = m.vec("rms_sd", [P, 96])
    m.rms_rs = m.vec("rms_rs", [P, 96])
    rms_row = m.vec("rms_row", [P, 3, P])
    m.rms_row = [rms_row[:, r, :] for r in range(3)]
    m.rms_rows = rms_row[:, 0, :]
    m.coef = m.vec("coef", [P, 2, 4, KD])
    m.coef_ctx = m.vec("coef_ctx", [P, KD])

    rows_in = m.at("vector_rows", YX, [P, tiles, P])
    x_rows = m.at("x_rows", A0, [P, TT, D])
    ctx_rows = m.at("ctx_rows", A0 + 16 * 4096, [P, 2, D])
    m.ctx_cm = m.at("ctx_cm", A0 + 21 * 4096, [P, KD, CTX])
    wm = m.at("w_mod_slots", XN, [P, 4, KD, HALF])
    x_tiles = ins["x"].rearrange("b (t p) d -> (b t) p d", p=P)
    ctx_tiles = ins["ctx"].rearrange("b (t p) d -> (b t) p d", p=P)
    w_mod = ins["w_mod"].rearrange("l (k p) n -> l p k n", p=P)
    groups = [(x_rows, t, g, m.x) for t in range(TT) for g in (0, 1)]
    groups += [(ctx_rows, t, g, m.ctx_cm) for t in range(2) for g in (0, 1)]

    with nc.Block() as block:
        @block.sync
        def _(sp):
            sp.dma_start(m.ident[:], ins["k_ident"]).then_inc(c["ident_in"], 16)
            for name, ap in lists:
                tile, at, n = place[name]
                sp.dma_start(rows_in[at:at + n, tile, :], ap).then_inc(c["rows_in"], 16)
            for s in range(4):
                sp.dma_start(wm[:, s], w_mod[0, :, :, s * HALF:(s + 1) * HALF]
                             ).then_inc(c[f"mod_in{s}"], 16)
            for t in range(TT):
                sp.dma_start(x_rows[:, t, :], x_tiles[t]).then_inc(c["x_in"], 16)
            for t in range(2):
                sp.dma_start(ctx_rows[:, t, :], ctx_tiles[t]).then_inc(c["x_in"], 16)

            def pieces(layer, i, s):
                sp.wait_ge(c["mod_out"], 4 * i + 12 * layer + s - 3)
                sp.dma_start(wm[:, s], w_mod[layer, :, :, bass.ds(i * 4 * HALF + s * HALF, HALF)]
                             ).then_inc(c[f"mod_in{s}"], 16)

            with sp.Fori(1, 3) as i:
                for s in range(4):
                    pieces(0, i, s)
            with sp.Fori(0, 3) as i:
                for s in range(4):
                    pieces(1, i, s)

        @block.gpsimd
        def _(pool):
            pool.memset(m.eps[:], EPS).then_inc(c["consts"], 1)
            pool.memset(m.ones[:], 1.0).then_inc(c["consts"], 1)
            for name in ("w_lo", "unit_done", "down_used", "at_exp", "at_lo"):
                pool.sem_inc(c[name], 2)
            for name in ("up_out", "at_copied"):
                pool.sem_inc(c[name], 1)

        @block.tensor
        def _(pe):
            pe.wait_ge(c["ident_in"], 16)
            pe.wait_ge(c["rows_in"], 16 * len(lists))
            pe.wait_ge(c["consts"], 2)
            for s in range(tiles):
                last = pe.transpose(m.ps[:, s // 4, (s % 4) * P:(s % 4) * P + fill[s]],
                                    rows_in[0:fill[s], s, :], m.ident[0:fill[s], 0:fill[s]])
            last.then_inc(c["vt_turned"], 1)
            pe.wait_ge(c["x_in"], 16 * (TT + 2))
            for i, (src, t, g, dst) in enumerate(groups):
                if i >= 2:
                    pe.wait_ge(c["x_copied"], i - 1)
                for q in range(4):
                    k = 4 * g + q
                    last = pe.transpose(m.ps[:, 2 + i % 2, q * P:(q + 1) * P],
                                        src[:, t, k * P:(k + 1) * P], m.ident[:])
                last.then_inc(c["x_turned"], 1)
            pe.wait_ge(c["silu_c"], 2)

            def piece(i, s):
                pe.wait_ge(c[f"mod_in{s}"], 16 * i + 16)
                out = m.ps[:, 4 + s, 0:8]
                for q in range(4):
                    for k in range(KD):
                        last = pe.matmul(out[:, 2 * q:2 * q + 2],
                                         wm[:, s, k, q * P:(q + 1) * P], m.silu_c[:, k, :],
                                         start=(k == 0), stop=(k == KD - 1))
                last.then_inc(c["mod_out"], 1)

            for s in range(4):
                piece(0, s)
            with pe.Fori(1, 6) as i:
                for s in range(4):
                    pe.wait_ge(c["mod_read"], 4 * i + s - 3)
                    piece(i, s)

        @block.scalar
        def _(act):
            act.wait_ge(c["vt_copied"], tiles)
            for v, name in enumerate(("c", "c_ctx")):
                act.activation(m.silu_c[:, :, v], m.vt[:, m.col[name]:m.col[name] + KD],
                               ACT.Silu).then_inc(c["silu_c"], 1)
            for i, (src, t, g, dst) in enumerate(groups):
                act.wait_ge(c["x_turned"], i + 1)
                act.activation(dst[:, 4 * g:4 * g + 4, t * P:(t + 1) * P],
                               m.ps[:, 2 + i % 2, :].rearrange("p (q t) -> p q t", q=4),
                               ACT.Copy).then_inc(c["x_copied"], 1)

        @block.vector
        def _(dve):
            dve.wait_ge(c["vt_turned"], 1)
            for s in range(tiles):
                dve.tensor_copy(m.vt[:, s * P:s * P + fill[s]],
                                m.ps[:, s // 4, (s % 4) * P:(s % 4) * P + fill[s]]
                                ).then_inc(c["vt_copied"], 1)
            mod = m.mod[:].rearrange("p l q v -> p (l q) v")

            dve.wait_ge(c["vt_copied"], tiles)
            with dve.Fori(0, 6) as i:
                for s in range(4):
                    dve.wait_ge(c["mod_out"], 4 * i + s + 1)
                    bias = m.vt[:, bass.ds(i * 16 + (m.col["b_mod"] + 4 * s), 4)]
                    dve.tensor_tensor(mod[:, bass.ds(i * 16 + 4 * s, 4), :],
                                      m.ps[:, 4 + s, 0:8].rearrange("p (q v) -> p q v", v=2),
                                      bias.unsqueeze(2).to_broadcast([P, 4, 2]),
                                      ALU.add).then_inc(c["mod_read"], 1)
            dve.wait_ge(c["mod_read"], 24)
            for layer in range(2):
                for j, (what, gain) in enumerate(((1, "g_pre_mix"), (2, "g_post_mix"),
                                                  (4, "g_pre_ffn"), (5, "g_post_ffn"))):
                    col = m.col[gain] + KD * layer
                    dve.scalar_tensor_tensor(
                        out=m.coef[:, layer, j, :], in0=m.mod[:, layer, 8 * what:8 * what + 8, 0],
                        scalar=1.0 if j % 2 == 0 else 0.0, in1=m.vt[:, col:col + KD],
                        op0=ALU.add, op1=ALU.mult).then_inc(c["coef"], 1)
            dve.scalar_tensor_tensor(
                out=m.coef_ctx[:], in0=m.mod[:, 0, 8:16, 1], scalar=1.0,
                in1=m.vt[:, m.col["g_pre_mix"]:m.col["g_pre_mix"] + KD], op0=ALU.add,
                op1=ALU.mult).then_inc(c["coef"], 1)


def mod_col(m, layer, what, k, v=0):
    return m.mod[:, layer, 8 * what + k, v:v + 1]


def vcol(m, name, k):
    return m.vt[:, m.col[name] + k:m.col[name] + k + 1]


def weight_units(w, start, count):
    v = w.rearrange("(k p) n -> p k n", p=P)
    return lambda u: v[:, :, bass.ds(u * P + start, P)]


def unit_half(ws, m, pe, slot, half, pre=None):
    s = slice(half * HALF, (half + 1) * HALF)
    for k in range(KD):
        if pre:
            pre.ready(pe, half, k)
        last = ws.products(pe, slot, m.ps[:, 2 * slot + half, :], k, m.xn_hi[:, k, s],
                           m.xn_lo[:, k, s], k == 0, k == KD - 1)
    return last


def first_units(c, ws, m, pe, pre):
    pre.pe_sums(pe, 0)
    pre.pe_spread(pe, 0)
    ws.ready(pe, 0)
    unit_half(ws, m, pe, 0, 0, pre)
    pre.pe_sums(pe, 1)
    ws.ready(pe, 1)
    unit_half(ws, m, pe, 1, 0)
    pre.pe_spread(pe, 1)
    unit_half(ws, m, pe, 0, 1, pre).then_inc(c["unit_done"], 1)
    unit_half(ws, m, pe, 1, 1).then_inc(c["unit_done"], 1)
    for j in range(2, len(pre.parts)):
        pre.pe_sums(pe, j)
        pre.pe_spread(pe, j)


def project_stage(nc, c, m, name, pre, w, units, ctx_from, dest, ctx_dest):
    ws = WeightStream(c, m, units)
    f0 = c.take("project_copied", units)
    n_ctx = units - ctx_from
    cf0 = c.take("ctx_copied", n_ctx)
    src = weight_units(w, 0, units)
    loop = ctx_from // 2

    with nc.Block() as block:
        @block.sync
        def _(sp):
            with sp.Fori(0, units // 2) as i:
                for b in range(2):
                    ws.load(sp, 2 * i + b, b, src(2 * i + b))

        @block.gpsimd
        def _(pool):
            for b in range(2):
                ws.split(pool, b, 0, b, KD)
            pre.pool(pool)
            with pool.Fori(1, units // 2) as i:
                for b in range(2):
                    ws.split(pool, 2 * i + b, i, b, KD)

        @block.tensor
        def _(pe):
            first_units(c, ws, m, pe, pre)

            def unit(u, b, with_ctx):
                ws.ready(pe, u)
                pe.wait_ge(c["project_copied"], f0 + u - 1)
                for h in range(2):
                    last = unit_half(ws, m, pe, b, h)
                if with_ctx:
                    if u == ctx_from:
                        pre.ready(pe, 2)
                    else:
                        pe.wait_ge(c["ctx_copied"], cf0 + u - ctx_from)
                    for k in range(KD):
                        last = ws.products(pe, b, m.ps[:, 4, 0:CTX], k, m.xnc_hi[:, k, :],
                                           m.xnc_lo[:, k, :], k == 0, k == KD - 1)
                last.then_inc(c["unit_done"], 1)

            with pe.Fori(1, loop) as i:
                for b in range(2):
                    unit(2 * i + b, b, False)
            for u in range(ctx_from, units):
                unit(u, u % 2, True)

        @block.scalar
        def _(act):
            pre.act(act)

            def copy(u, b):
                ws.finished(act, u)
                stand_alone(act, c)
                act.activation(dest(u), m.ps[:, 2 * b:2 * b + 2, :].rearrange("p b t -> p (b t)"),
                               ACT.Copy).then_inc(c["project_copied"], 1)

            with act.Fori(0, loop) as i:
                for b in range(2):
                    copy(2 * i + b, b)
            for u in range(ctx_from, units):
                copy(u, u % 2)
                act.activation(ctx_dest(u), m.ps[:, 4, 0:CTX], ACT.Copy
                               ).then_inc(c["ctx_copied"], 1)

        @block.vector
        def _(dve):
            pre.dve(dve)


def ffn_up_stage(nc, c, m, name, pre, w, ff, conv_w, conv_b, causal, x_store):
    ws = WeightStream(c, m, 2 * ff)
    out0 = c.take("up_out", ff)
    steps = 2 if causal else 1
    i0 = c.take("up_centre", steps * ff)
    s0 = c.take("up_side", 2 * steps * ff)
    act0 = c.take("up_act", ff)
    wv = w.rearrange("(k p) n -> p k n", p=P)
    work = m.at(f"{name}_work", YX, [P, 4, T])
    gate_work, value_work = work[:, 0, :], work[:, 1, :]
    banks = m.ps[:].rearrange("p b t -> p (b t)")
    gate_ps, value_ps = banks[:, 0:T], banks[:, T:2 * T]
    if causal:
        centre, sides = 2, [(slice(0, T - 2), slice(2, T), 0), (slice(0, T - 1), slice(1, T), 1)]
    else:
        centre, sides = 1, [(slice(0, T - 1), slice(1, T), 0), (slice(1, T), slice(0, T - 1), 2)]

    with nc.Block() as block:
        @block.sync
        def _(sp):
            with sp.Fori(0, ff) as j:
                for b in range(2):
                    ws.load(sp, 2 * j + b, b, wv[:, :, bass.ds(j * P + b * ff * P, P)])

        @block.gpsimd
        def _(pool):
            for b in range(2):
                ws.split(pool, b, 0, b, KD)
            pre.pool(pool)
            with pool.Fori(1, ff) as j:
                for b in range(2):
                    ws.split(pool, 2 * j + b, j, b, KD)

        @block.tensor
        def _(pe):
            first_units(c, ws, m, pe, pre)
            with pe.Fori(1, ff) as j:
                for b in range(2):
                    ws.ready(pe, 2 * j + b)
                    if causal or b == 0:
                        pe.wait_ge(c["up_side"], 2 * steps * j + s0 - 2 * steps + 2 * b + 2)
                    else:
                        pe.wait_ge(c["up_out"], out0 + j + 1)
                    for h in range(2):
                        last = unit_half(ws, m, pe, b, h)
                    last.then_inc(c["unit_done"], 1)

        @block.scalar
        def _(act):
            pre.act(act)
            with act.Fori(0, ff) as j:
                ws.finished(act, 2 * j)
                act.wait_ge(c["up_out"], out0 + j + 1)
                stand_alone(act, c)
                act.activation(gate_work, gate_ps, ACT.Identity, bias=conv_b(j),
                               scale=conv_w(centre, j)).then_inc(c["up_centre"], 1)
                if causal:
                    ws.finished(act, 2 * j + 1)
                    stand_alone(act, c)
                    act.activation(value_work, value_ps, ACT.Identity, bias=conv_b(j + ff),
                                   scale=conv_w(centre, j + ff)).then_inc(c["up_centre"], 1)
                act.wait_ge(c["up_side"], 2 * steps * j + s0 + 2)
                act.activation(gate_work, gate_work, ACT.Gelu_apprx_tanh if causal else ACT.Silu
                               ).then_inc(c["up_act"], 1)

        @block.vector
        def _(dve):
            pre.dve(dve)

            def neighbours(j, part, target, source, chunk):
                dve.wait_ge(c["up_centre"], steps * j + i0 + part + 1)
                for n, (src, dst, tap) in enumerate(sides):
                    if n:
                        dve.wait_ge(c["up_side"], 2 * steps * j + s0 + 2 * part + 1)
                    last = dve.scalar_tensor_tensor(
                        out=target[:, dst], in0=source[:, src], scalar=conv_w(tap, chunk),
                        in1=target[:, dst], op0=ALU.mult, op1=ALU.add)
                    last.then_inc(c["up_side"], 1)

            with dve.Fori(0, ff) as j:
                neighbours(j, 0, gate_work, gate_ps, j)
                if causal:
                    neighbours(j, 1, value_work, value_ps, j + ff)
                    dve.wait_ge(c["up_side"], 2 * steps * j + s0 + 4)
                dve.wait_ge(c["up_act"], act0 + j + 1)
                if causal:
                    dve.tensor_tensor(m.a[:, bass.ds(j, 1), :].rearrange("p o t -> p (o t)"),
                                      gate_work, value_work, ALU.mult
                                      ).then_inc(c["up_out"], 1)
                else:
                    ws.finished(dve, 2 * j + 1)
                    dve.tensor_tensor(m.a[:, bass.ds(j, 1), :].rearrange("p o t -> p (o t)"),
                                      gate_work, value_ps, ALU.mult
                                      ).then_inc(c["up_out"], 1)


def down_stage(nc, c, m, name, chunks, groups, source, kmap, evac, post, x_dram, x_load, x_store):
    ng = len(groups)
    units = 2 * KD * ng
    ws = WeightStream(c, m, units)
    h0, l0 = c.take("down_hi", 2 * chunks), c.take("down_lo", 2 * chunks)
    f0 = c.take("down_used", 2 * KD)
    xl0 = c.take("x_loaded", 32 if x_load else 0)
    xs0 = c.take("x_stored", 32 if x_store else 0)
    rx0 = c.take("x_scaled", 2 * KD if post else 0)
    nx0 = c.take("x_new", 2 * KD)
    pairs = KD // 2
    per = 2 * ng

    def y(half, n):
        return m.yx[:, n, :] if half == 0 else m.a[:, n, 0:HALF]

    def x(half, k):
        return m.x[:, k, half * HALF:(half + 1) * HALF]

    def slot(half, k):
        return m.ring[:, (half * chunks + k) % 32, :]

    def lo(half, k):
        return m.a_lo[k // 8][:, k % 8, half * HALF:(half + 1) * HALF]

    def full(half, k):
        return m.a[:, k, half * HALF:(half + 1) * HALF]

    rms = []
    if post:
        for h in range(2):
            squares = [m.a[:, 16 + i, h * HALF:(h + 1) * HALF] for i in range(6)]
            rms.append(RootMeanSquare(c, m, f"{name}{h}", 1, KD, 4, D,
                                      (lambda hh: lambda k: y(hh, k))(h), squares,
                                      m.ps[:, 4, 8 * h:8 * h + 8], m.ps[:, 5, h * P:(h + 1) * P],
                                      [m.ps[:, 6 + h, :]], 4 * h))

    with nc.Block() as block:
        @block.sync
        def _(sp):
            def pair(half, i):
                for b in range(2):
                    for g in range(ng):
                        n = b * ng + g
                        ws.load(sp, per * i + half * KD * ng + n, n % 2, source(i, b, g))

            with sp.Fori(0, pairs) as i:
                pair(0, i)
            pair(1, 0)
            if x_load:
                ws.finished(sp, units // 2 - 1)
                sp.dma_start(m.x[:, :, 0:HALF], x_dram[:, :, 0:HALF]).then_inc(c["x_loaded"], 16)
            with sp.Fori(1, pairs) as i:
                pair(1, i)
            if x_load:
                ws.finished(sp, units - 1)
                sp.wait_ge(c["x_loaded"], xl0 + 16)
                sp.dma_start(m.x[:, :, HALF:T], x_dram[:, :, HALF:T]).then_inc(c["x_loaded"], 16)
            if x_store:
                for h in range(2):
                    if x_load:
                        sp.wait_ge(c["x_loaded"], xl0 + 32)
                    sp.wait_ge(c["x_new"], nx0 + (h + 1) * KD)
                    s = slice(h * HALF, (h + 1) * HALF)
                    sp.dma_start(x_dram[:, :, s], m.x[:, :, s]).then_inc(c["x_stored"], 16)
                sp.wait_ge(c["x_stored"], xs0 + 32)

        @block.gpsimd
        def _(pool):
            def pair(half, i):
                for b in range(2):
                    for g in range(ng):
                        n = b * ng + g
                        ws.split(pool, per * i + half * KD * ng + n,
                                 ng * i + half * KD * ng // 2 + n // 2, n % 2, groups[g])

            for half in range(2):
                with pool.Fori(0, pairs) as i:
                    pair(half, i)

        @block.tensor
        def _(pe):
            def pair(half, i, waits):
                for b in range(2):
                    pe.wait_ge(c["down_used"], 2 * i + f0 + half * KD + b + 1)
                    k = 0
                    first = kmap(i, b)
                    for g in range(ng):
                        n = b * ng + g
                        ws.ready(pe, per * i + half * KD * ng + n)
                        for q in range(groups[g]):
                            kk = first + k
                            if waits:
                                pe.wait_ge(c["down_lo"], l0 + half * chunks + kk + 1)
                            last = ws.products(pe, n % 2, m.ps[:, b, :], q, slot(half, kk),
                                               lo(half, kk), k == 0, k == sum(groups) - 1)
                            k += 1
                        last.then_inc(c["unit_done"], 1)

            looped = sum(groups) == chunks
            pair(0, 0, True)
            if looped:
                with pe.Fori(1, pairs) as i:
                    pair(0, i, False)
            else:
                for i in range(1, pairs):
                    pair(0, i, True)
            pair(1, 0, True)
            if post:
                rms[0].pe_sums(pe)
            pair(1, 1, not looped)
            if post:
                rms[0].pe_turn(pe)
            pair(1, 2, not looped)
            if post:
                rms[0].pe_broadcast(pe, 0)
            pair(1, 3, not looped)
            if post:
                rms[1].pe_sums(pe)
                rms[1].pe_turn(pe)
                rms[1].pe_broadcast(pe, 0)

        @block.scalar
        def _(act):
            def splits(half):
                for k in range(chunks):
                    if half and chunks + k >= 32:
                        ws.finished(act, units // 2 - 1)
                    act.activation(slot(half, k), full(half, k), ACT.Copy
                                   ).then_inc(c["down_hi"], 1)

            def copies(half, i):
                for b in range(2):
                    ws.finished(act, per * i + half * KD * ng + b * ng + ng - 1)
                    stand_alone(act, c)
                    if half == 0:
                        dst = m.yx[:, bass.ds(2 * i + b, 1), :].rearrange("p o t -> p (o t)")
                    else:
                        dst = y(1, 2 * i + b)
                    if evac is None:
                        act.activation(dst, m.ps[:, b, :], ACT.Copy).then_inc(c["down_used"], 1)
                    else:
                        scale, bias = evac
                        act.activation(dst, m.ps[:, b, :], ACT.Identity, bias=bias(2 * i + b),
                                       scale=scale(2 * i + b)).then_inc(c["down_used"], 1)

            splits(0)
            with act.Fori(0, pairs) as i:
                copies(0, i)
            splits(1)
            act.wait_ge(c["down_used"], f0 + KD + 2)
            ws.finished(act, units // 2 - 1)
            if post:
                rms[0].act_squares(act)
            copies(1, 0)
            if post:
                rms[0].act_root(act)
            for i in range(1, pairs):
                copies(1, i)
            if post:
                act.wait_ge(c["down_used"], f0 + 2 * KD + 2)
                ws.finished(act, units - 1)
                rms[1].act_squares(act)
                rms[1].act_root(act)

        @block.vector
        def _(dve):
            for half in range(2):
                for k in range(chunks):
                    dve.wait_ge(c["down_hi"], h0 + half * chunks + k + 1)
                    dve.tensor_tensor(lo(half, k), full(half, k), slot(half, k).bitcast(F32),
                                      ALU.subtract).then_inc(c["down_lo"], 1)
            for half in range(2):
                if post:
                    rms[half].dve_inverse(dve)
                    rms[half].dve_row(dve)
                    bank = rms[half].ready(dve, 0)
                    for k in range(KD):
                        dve.tensor_tensor(y(half, k), y(half, k), bank, ALU.mult
                                          ).then_inc(c["x_scaled"], 1)
                else:
                    dve.wait_ge(c["down_used"], f0 + (half + 1) * KD + 2)
                if x_load:
                    dve.wait_ge(c["x_loaded"], xl0 + 16 * (half + 1))
                for k in range(KD):
                    if post:
                        dve.wait_ge(c["x_scaled"], rx0 + half * KD + k + 1)
                        dve.scalar_tensor_tensor(
                            out=x(half, k), in0=y(half, k), scalar=post(k), in1=x(half, k),
                            op0=ALU.mult, op1=ALU.add).then_inc(c["x_new"], 1)
                    else:
                        dve.tensor_tensor(x(half, k), y(half, k), x(half, k), ALU.add
                                          ).then_inc(c["x_new"], 1)


def two(ap, n=2):
    return ap.rearrange("p (a t) -> p a t", a=n)


def attention_memory(m):
    m.kh = m.at("k_hi", XN, [P, KV, KEYS], F32R)
    m.kl = m.at("k_lo", XN + 10240, [P, KV, KEYS], F32R)
    m.vh = m.at("v_hi", XN + 20480, [P, KEYS // P, KV * P], F32R)
    m.vl = m.at("v_lo", XN + 30720, [P, KEYS // P, KV * P], F32R)
    m.qh = m.at("q_hi", XN + 40960, [P, 2, HALF], F32R)
    m.ql = m.at("q_lo", XN + 45056, [P, 2, HALF], F32R)
    m.probs = m.at("probs", XN + 49152, [P, 2, KEYS])
    m.pth = m.at("probs_t_hi", W_RAW, [P, KEYS // P, HALF], F32R)
    m.ptl = m.at("probs_t_lo", W_RAW + 20480, [P, KEYS // P, HALF], F32R)
    m.kv_raw = m.at("kv_raw", A0 + 16 * 4096, [P, 2 * KV, KEYS])


def rotate_stage(nc, c, m, ins):
    table = m.at("rope_tables", W_RAW, [P, 6, T])
    cos, sin = table[:, 0, :], table[:, 1, :]
    tmp = m.at("rope_tmp", YX, [P, 4, HALF])
    direct, swapped = tmp[:, 0:2, :], tmp[:, 2:4, :]
    sq = m.at("rope_squares", YX + 8192, [P, 3, HALF])
    perm = m.at("rope_perm", YX + 8192 + 6144, [P, P])
    items = []
    for h in range(HEADS):
        for half in range(2):
            s = slice(half * HALF, (half + 1) * HALF)
            items.append(("q", h, s, m.a[:, h, s]))
    for h in range(KV):
        for half in range(2):
            s = slice(half * HALF, (half + 1) * HALF)
            items.append(("k", h, s, m.kv_raw[:, h, CTX + half * HALF:CTX + (half + 1) * HALF]))
    items.append(("ctx", 0, None, m.kv_raw[:, 0:KV, 0:CTX]))
    n_rot = len(items) - 1
    n_k = 2 * KV + 1
    rms = RootMeanSquare(c, m, "qk", len(items), 1, 4, P, lambda i: items[i][3],
                         [sq[:, i, :] for i in range(3)], m.ps[:, 4, :], m.ps[:, 5, :],
                         [m.ps[:, 6, :], m.ps[:, 7, :]], 0)
    sw0 = c.take("rope_swapped", n_rot)
    dir0 = c.take("rope_direct", n_rot)
    sin0 = c.take("rope_sin", n_rot)
    sum0 = c.take("rope_sum", n_rot)
    out0 = c.take("rope_out", len(items))
    kh0, kl0 = c.take("rope_k_hi", n_k), c.take("rope_k_lo", n_k)
    vt0, vh0, vl0 = c.take("v_turned", 5), c.take("v_hi_done", 5), c.take("v_lo_done", 5)

    with nc.Block() as block:
        @block.sync
        def _(sp):
            sp.dma_start(perm[:], ins["k_perm1"]).then_inc(c["rope_perm_in"], 16)
            sp.dma_start(cos, ins["k_cos1"]).then_inc(c["rope_in"], 16)
            sp.dma_start(sin, ins["k_sin1"]).then_inc(c["rope_in"], 16)

        @block.tensor
        def _(pe):
            pe.wait_ge(c["rope_perm_in"], 16)
            for i, name in enumerate(("g_q", "g_k")):
                last = pe.matmul(m.ps[:, 3, i:i + 1], perm[:], vcol(m, name, 0),
                                 start=True, stop=True)
            last.then_inc(c["gains_swapped"], 1)
            rms.pe_sums(pe)
            rms.pe_turn(pe)
            pe.wait_ge(c["gains_copied"], 1)
            for g in range(5):
                if g >= 2:
                    pe.wait_ge(c["v_lo_done"], vl0 + g - 1)
                for q in range(4):
                    kt, v = 2 * g + q // 2, q % 2
                    last = pe.transpose(m.ps[:, 2 + g % 2, q * P:(q + 1) * P],
                                        m.kv_raw[:, KV + v, kt * P:(kt + 1) * P], m.ident[:])
                last.then_inc(c["v_turned"], 1)
            for g, (kind, h, s, src) in enumerate(items):
                if kind != "ctx":
                    if g >= 2:
                        pe.wait_ge(c["rope_sin"], sin0 + g - 1)
                    pe.matmul(m.ps[:, g % 2, :], perm[:], src, start=True, stop=True
                              ).then_inc(c["rope_swapped"], 1)
                rms.pe_broadcast(pe, g)

        @block.scalar
        def _(act):
            rms.act_squares(act)
            rms.act_root(act)
            for g in range(5):
                act.wait_ge(c["v_turned"], vt0 + g + 1)
                act.activation(m.vh[:, 2 * g:2 * g + 2, :], two(m.ps[:, 2 + g % 2, :]), ACT.Copy
                               ).then_inc(c["v_hi_done"], 1)
            for i in range(n_k):
                g = 2 * HEADS + i
                act.wait_ge(c["rope_out"], out0 + g + 1)
                kind, h, s, src = items[g]
                if kind == "k":
                    dst = m.kh[:, h, CTX + s.start:CTX + s.stop]
                    act.activation(dst, direct[:, g % 2, :], ACT.Copy
                                   ).then_inc(c["rope_k_hi"], 1)
                else:
                    act.activation(m.kh[:, :, 0:CTX], two(direct[:, g % 2, :]), ACT.Copy
                                   ).then_inc(c["rope_k_hi"], 1)

        @block.gpsimd
        def _(pool):
            pool.wait_ge(c["rope_tables"], 4)
            for g, (kind, h, s, src) in enumerate(items[:n_rot]):
                if g >= 2:
                    pool.wait_ge(c["rope_out"], out0 + g - 1)
                if g >= 2 * HEADS + 2:
                    pool.wait_ge(c["rope_k_lo"], kl0 + g - 2 * HEADS - 1)
                which = 2 if kind == "q" else 4
                pool.tensor_tensor(direct[:, g % 2, :], src, table[:, which, s], ALU.mult
                                   ).then_inc(c["rope_direct"], 1)

        @block.vector
        def _(dve):
            dve.wait_ge(c["gains_swapped"], 1)
            dve.tensor_copy(m.gains_sw[:], m.ps[:, 3, 0:2]).then_inc(c["gains_copied"], 1)
            dve.wait_ge(c["rope_in"], 32)
            dve.wait_ge(c["gains_copied"], 1)
            for i, name in enumerate(("g_q", "g_k")):
                dve.tensor_scalar(table[:, 2 + 2 * i, :], cos, vcol(m, name, 0), None, ALU.mult
                                  ).then_inc(c["rope_tables"], 1)
                dve.tensor_scalar(table[:, 3 + 2 * i, :], sin, m.gains_sw[:, i:i + 1], None,
                                  ALU.mult).then_inc(c["rope_tables"], 1)
            dve.wait_ge(c["rope_tables"], 4)
            rms.dve_inverse(dve)
            rms.dve_row(dve)
            for g in range(5):
                dve.wait_ge(c["v_hi_done"], vh0 + g + 1)
                dve.tensor_tensor(m.vl[:, 2 * g:2 * g + 2, :], two(m.ps[:, 2 + g % 2, :]),
                                  m.vh[:, 2 * g:2 * g + 2, :].bitcast(F32), ALU.subtract
                                  ).then_inc(c["v_lo_done"], 1)
            for g, (kind, h, s, src) in enumerate(items):
                if kind == "ctx":
                    bank = rms.ready(dve, g)
                    dve.wait_ge(c["rope_k_lo"], kl0 + g - 2 * HEADS - 1)
                    dve.scalar_tensor_tensor(out=two(direct[:, g % 2, :]), in0=src,
                                             scalar=vcol(m, "g_k", 0), in1=two(bank),
                                             op0=ALU.mult, op1=ALU.mult
                                             ).then_inc(c["rope_out"], 1)
                else:
                    which = 3 if kind == "q" else 5
                    dve.wait_ge(c["rope_swapped"], sw0 + g + 1)
                    dve.tensor_tensor(swapped[:, g % 2, :], m.ps[:, g % 2, :],
                                      table[:, which, s], ALU.mult).then_inc(c["rope_sin"], 1)
                    dve.wait_ge(c["rope_sin"], sin0 + g + 1)
                    dve.wait_ge(c["rope_direct"], dir0 + g + 1)
                    dve.tensor_tensor(swapped[:, g % 2, :], direct[:, g % 2, :],
                                      swapped[:, g % 2, :], ALU.add).then_inc(c["rope_sum"], 1)
                    bank = rms.ready(dve, g)
                    dve.wait_ge(c["rope_sum"], sum0 + g + 1)
                    dst = src if kind == "q" else direct[:, g % 2, :]
                    dve.tensor_tensor(dst, swapped[:, g % 2, :], bank, ALU.mult
                                      ).then_inc(c["rope_out"], 1)
                if kind != "q":
                    i = g - 2 * HEADS
                    dve.wait_ge(c["rope_k_hi"], kh0 + i + 1)
                    if kind == "k":
                        cols = slice(CTX + s.start, CTX + s.stop)
                        dve.tensor_tensor(m.kl[:, h, cols], direct[:, g % 2, :],
                                          m.kh[:, h, cols].bitcast(F32), ALU.subtract
                                          ).then_inc(c["rope_k_lo"], 1)
                    else:
                        dve.tensor_tensor(m.kl[:, :, 0:CTX], two(direct[:, g % 2, :]),
                                          m.kh[:, :, 0:CTX].bitcast(F32), ALU.subtract
                                          ).then_inc(c["rope_k_lo"], 1)
                dve.wait_ge(c["rope_out"], out0 + g + 1)
                dve.sem_inc(c["rms_broadcast_used"], 1)


def attention_stage(nc, c, m):
    flat = m.ps[:].rearrange("p b t -> p (b t)")
    pieces = [[(0, 512), (512, 1024), (1024, 1280)], [(256, 768), (768, 1280), (0, 256)]]
    groups = [(0, 4), (4, 8), (8, 10)]
    kt_n = KEYS // P
    out_ps = m.ps[:, 7, :]

    def tile(h, half, qi):
        return h * 8 + (4 * half + qi)

    for g in range(KV):
        first = 32 * g

        with nc.Block() as block:
            @block.tensor
            def _(pe):
                def scores(h, half, qi):
                    if qi == 0:
                        pe.wait_ge(c["at_q_lo"], h * 2 + (8 * g + half + 1))
                    pe.wait_ge(c["at_exp"], tile(h, half, qi) + (first + 1))
                    b = qi % 2
                    qs = slice(qi * P, (qi + 1) * P)
                    for i, (k0, k1) in enumerate(pieces[b]):
                        if i == 2:
                            pe.wait_ge(c["at_exp"], tile(h, half, qi) + (first + 2))
                        out = flat[:, b * KEYS + k0:b * KEYS + k1]
                        pe.matmul(out, m.qh[:, half, qs], m.kh[:, g, k0:k1], start=True, stop=False)
                        pe.matmul(out, m.qh[:, half, qs], m.kl[:, g, k0:k1], start=False,
                                  stop=False)
                        last = pe.matmul(out, m.ql[:, half, qs], m.kh[:, g, k0:k1], start=False,
                                         stop=True)
                    last.then_inc(c["at_scores"], 1)

                def turns(h, half, qi):
                    pe.wait_ge(c["at_probs"], tile(h, half, qi) + (first + 1))
                    for gi, (k0, k1) in enumerate(groups):
                        pe.wait_ge(c["at_lo"], h * 24 + (3 * first + 12 * half + 3 * qi + gi + 1))
                        for kt in range(k0, k1):
                            last = pe.transpose(
                                m.ps[:, 5 + (3 * qi + gi) % 2, (kt - k0) * P:(kt - k0 + 1) * P],
                                m.probs[:, qi % 2, kt * P:(kt + 1) * P], m.ident[:])
                        last.then_inc(c["at_turned"], 1)

                def values(h, half):
                    pe.wait_ge(c["at_lo"], h * 24 + (3 * first + 12 * half + 12 + 2))
                    pe.wait_ge(c["at_copied"], h * 2 + (8 * g + half + 1))
                    for kt in range(kt_n):
                        vs = slice(g * P, (g + 1) * P)
                        pe.matmul(out_ps, m.vh[:, kt, vs], m.pth[:, kt, :], start=(kt == 0),
                                  stop=False)
                        pe.matmul(out_ps, m.vh[:, kt, vs], m.ptl[:, kt, :], start=False, stop=False)
                        last = pe.matmul(out_ps, m.vl[:, kt, vs], m.pth[:, kt, :], start=False,
                                         stop=(kt == kt_n - 1))
                    last.then_inc(c["at_out"], 1)

                def item(h, half, more):
                    nh, nhalf = (h, 1) if half == 0 else (h + 1, 0)
                    turns(h, half, 0)
                    scores(h, half, 2)
                    turns(h, half, 1)
                    scores(h, half, 3)
                    turns(h, half, 2)
                    if more:
                        scores(nh, nhalf, 0)
                    turns(h, half, 3)
                    if more:
                        scores(nh, nhalf, 1)
                    values(h, half)

                scores(0, 0, 0)
                scores(0, 0, 1)
                with pe.Fori(0, GROUP - 1) as h:
                    item(h, 0, True)
                    item(h, 1, True)
                item(GROUP - 1, 0, True)
                item(GROUP - 1, 1, False)

            @block.scalar
            def _(act):
                def q(h, half):
                    src = m.a[:, bass.ds(h + GROUP * g, 1), half * HALF:(half + 1) * HALF]
                    act.activation(m.qh[:, half, :], src.rearrange("p o t -> p (o t)"), ACT.Copy
                                   ).then_inc(c["at_q_hi"], 1)

                def exps(h, half, qi):
                    act.wait_ge(c["at_neg"], tile(h, half, qi) + (first + 1))
                    b = qi % 2
                    act.activation(m.probs[:, b, :], flat[:, b * KEYS:(b + 1) * KEYS], ACT.Exp,
                                   bias=m.at_neg[:, qi:qi + 1], scale=ATT_SCALE,
                                   accum_out=m.at_sum[:, qi:qi + 1]).then_inc(c["at_exp"], 1)

                def highs(h, half, qi):
                    for gi, (k0, k1) in enumerate(groups):
                        act.wait_ge(c["at_turned"],
                                    h * 24 + (3 * first + 12 * half + 3 * qi + gi + 1))
                        src = m.ps[:, 5 + (3 * qi + gi) % 2, 0:(k1 - k0) * P]
                        act.activation(m.pth[:, k0:k1, qi * P:(qi + 1) * P], two(src, k1 - k0),
                                       ACT.Copy).then_inc(c["at_hi"], 1)

                def copy(h, half):
                    act.wait_ge(c["at_out"], h * 2 + (8 * g + half + 1))
                    stand_alone(act, c)
                    dst = m.a[:, bass.ds(h + GROUP * g, 1), half * HALF:(half + 1) * HALF]
                    act.activation(dst.rearrange("p o t -> p (o t)"), out_ps, ACT.Copy
                                   ).then_inc(c["at_copied"], 1)

                def item(h, half, more):
                    nh, nhalf = (h, 1) if half == 0 else (h + 1, 0)
                    if more:
                        q(nh, nhalf)
                    highs(h, half, 0)
                    exps(h, half, 2)
                    highs(h, half, 1)
                    exps(h, half, 3)
                    highs(h, half, 2)
                    if more:
                        exps(nh, nhalf, 0)
                    highs(h, half, 3)
                    if more:
                        exps(nh, nhalf, 1)
                    copy(h, half)

                q(0, 0)
                exps(0, 0, 0)
                exps(0, 0, 1)
                with act.Fori(0, GROUP - 1) as h:
                    item(h, 0, True)
                    item(h, 1, True)
                item(GROUP - 1, 0, True)
                item(GROUP - 1, 1, False)

            @block.vector
            def _(dve):
                def q(h, half):
                    dve.wait_ge(c["at_q_hi"], h * 2 + (8 * g + half + 1))
                    src = m.a[:, bass.ds(h + GROUP * g, 1), half * HALF:(half + 1) * HALF]
                    dve.tensor_tensor(m.ql[:, half, :], src.rearrange("p o t -> p (o t)"),
                                      m.qh[:, half, :].bitcast(F32), ALU.subtract
                                      ).then_inc(c["at_q_lo"], 1)

                def maxima(h, half, qi):
                    dve.wait_ge(c["at_scores"], tile(h, half, qi) + (first + 1))
                    b = qi % 2
                    dve.tensor_reduce(m.at_max[:, qi:qi + 1], flat[:, b * KEYS:(b + 1) * KEYS],
                                      AX_X, ALU.max).then_inc(c["at_max"], 1)
                    dve.wait_ge(c["at_max"], tile(h, half, qi) + (first + 1))
                    dve.tensor_scalar(m.at_neg[:, qi:qi + 1], m.at_max[:, qi:qi + 1], -ATT_SCALE,
                                      None, ALU.mult).then_inc(c["at_neg"], 1)

                def inverse(h, half, qi):
                    dve.wait_ge(c["at_exp"], tile(h, half, qi) + (first + 3))
                    dve.reciprocal(m.at_inv[:, qi:qi + 1], m.at_sum[:, qi:qi + 1]
                                   ).then_inc(c["at_inverse"], 1)

                def lows(h, half, qi):
                    for gi, (k0, k1) in enumerate(groups):
                        dve.wait_ge(c["at_hi"], h * 24 + (3 * first + 12 * half + 3 * qi + gi + 1))
                        src = m.ps[:, 5 + (3 * qi + gi) % 2, 0:(k1 - k0) * P]
                        qs = slice(qi * P, (qi + 1) * P)
                        dve.tensor_tensor(m.ptl[:, k0:k1, qs], two(src, k1 - k0),
                                          m.pth[:, k0:k1, qs].bitcast(F32), ALU.subtract
                                          ).then_inc(c["at_lo"], 1)

                def item(h, half, more):
                    nh, nhalf = (h, 1) if half == 0 else (h + 1, 0)
                    inverse(h, half, 1)
                    if more:
                        q(nh, nhalf)
                    lows(h, half, 0)
                    maxima(h, half, 2)
                    lows(h, half, 1)
                    inverse(h, half, 2)
                    maxima(h, half, 3)
                    lows(h, half, 2)
                    inverse(h, half, 3)
                    if more:
                        maxima(nh, nhalf, 0)
                    lows(h, half, 3)
                    if more:
                        inverse(nh, nhalf, 0)
                        maxima(nh, nhalf, 1)

                q(0, 0)
                maxima(0, 0, 0)
                maxima(0, 0, 1)
                inverse(0, 0, 0)
                with dve.Fori(0, GROUP - 1) as h:
                    item(h, 0, True)
                    item(h, 1, True)
                item(GROUP - 1, 0, True)
                item(GROUP - 1, 1, False)

            @block.gpsimd
            def _(pool):
                with pool.Fori(0, 2 * GROUP) as i:
                    for qi in range(4):
                        pool.wait_ge(c["at_inverse"], i * 4 + (first + qi + 1))
                        stand_alone(pool, c)
                        pool.tensor_scalar(m.probs[:, qi % 2, :], m.probs[:, qi % 2, :],
                                           m.at_inv[:, qi:qi + 1], 1.0, ALU.mult, ALU.mult
                                           ).then_inc(c["at_probs"], 1)


def pool_stage(nc, c, m, ins):
    pad = 8
    wide = T + 2 * pad
    h_pad = m.at("pool_h", XN, [P, KD, wide])
    sums = m.at("pool_sums", W_RAW, [P, 4, wide])
    inv = m.at("pool_inverse_counts", YX, [P, 4, T])
    parts = halves_parts(m, lambda k: m.coef[:, 1, 0, k:k + 1], lambda k: mod_col(m, 1, 0, k))
    for h, p in enumerate(parts):
        p["work"] = (lambda hh: lambda k: h_pad[:, k, pad + hh * HALF:pad + (hh + 1) * HALF])(h)
    pre = PreNorm(c, m, "pool", parts, split=False)
    aff0 = pre.aff0
    steps = [k // 2 + 1 for k in range(KD)]
    before = [sum(steps[:k]) for k in range(KD)]
    a0 = c.take("pool_added", sum(steps))
    m0, d0 = c.take("pool_mean", KD), c.take("pool_out", KD)

    with nc.Block() as block:
        @block.sync
        def _(sp):
            sp.dma_start(inv[:], ins["k_pool_inverse"].unsqueeze(0).to_broadcast([P, 4, T])
                         ).then_inc(c["pool_counts_in"], 16)

        @block.scalar
        def _(act):
            pre.act(act)

        @block.tensor
        def _(pe):
            for j in range(2):
                pre.pe_sums(pe, j)
                pre.pe_spread(pe, j)

        @block.vector
        def _(dve):
            dve.memset(h_pad[:, :, 0:pad], 0.0).then_inc(c["pool_zeros"], 1)
            dve.memset(h_pad[:, :, pad + T:wide], 0.0).then_inc(c["pool_zeros"], 1)
            pre.dve(dve)
            dve.wait_ge(c["pool_zeros"], 2)
            for k in range(KD):
                dve.wait_ge(c["pre_shifted"], aff0 + KD + k + 1)
                src, lo, hi = h_pad[:, k, :], 0, wide
                for i in range(steps[k]):
                    slot = 2 * (k % 2) + i % 2
                    if i == 0 and k >= 2:
                        dve.wait_ge(c["pool_mean"], m0 + k - 1)
                    if i:
                        dve.wait_ge(c["pool_added"], a0 + before[k] + i)
                    back, ahead = (1, 0) if i == 0 else (2 ** (i - 1), 2 ** (i - 1))
                    lo, hi = lo + back, hi - ahead
                    dve.tensor_tensor(sums[:, slot, lo:hi], src[:, lo - back:hi - back],
                                      src[:, lo + ahead:hi + ahead], ALU.add
                                      ).then_inc(c["pool_added"], 1)
                    src = sums[:, slot, :]

        @block.gpsimd
        def _(pool):
            pool.wait_ge(c["pool_counts_in"], 16)
            for k in range(KD):
                slot = 2 * (k % 2) + (steps[k] - 1) % 2
                pool.wait_ge(c["pool_added"], a0 + before[k] + steps[k])
                pool.tensor_tensor(m.a[:, k, :], sums[:, slot, pad:pad + T], inv[:, k // 2, :],
                                   ALU.mult).then_inc(c["pool_mean"], 1)
                pool.wait_ge(c["pool_mean"], m0 + k + 1)
                pool.tensor_tensor(m.a[:, k, :], m.a[:, k, :], h_pad[:, k, pad:pad + T],
                                   ALU.subtract).then_inc(c["pool_out"], 1)


def lru_stage(nc, c, m, ins):
    n = 4
    t = m.at("lru_work", XN, [P, 16, T])
    xc, ra, gi, mi = t[:, 0:4], t[:, 4:8], t[:, 8:12], t[:, 12:16]
    bd = m.at("lru_gates", YX, [P, 2, n, P])
    small = m.at("lru_small", YX + 4096, [P, 12, n])
    squares = m.at("lru_squares", YX + 8192, [P, 4, HALF])
    lam = m.vt[:, m.col["lambda"]:m.col["lambda"] + n]
    terms = 8
    rms = [RootMeanSquare(c, m, f"lru{h}", 1, n, 4, n * P,
                          (lambda hh: lambda k: m.a[:, k, hh * HALF:(hh + 1) * HALF])(h),
                          [squares[:, i, :] for i in range(4)], m.ps[:, 4, 8 * h:8 * h + 8],
                          m.ps[:, 5, h * P:(h + 1) * P], [m.ps[:, 6 + h, :]], 4 * h)
           for h in range(2)]

    def gate_ps(which):
        return m.ps[:, 2 * which:2 * which + 2, :].rearrange("p b t -> p (b t)")

    with nc.Block() as block:
        @block.sync
        def _(sp):
            sp.wait_ge(c["lru_zero"], 1)
            for w, name in enumerate(("lru_gate_a_w_2", "lru_gate_x_w_2")):
                for odd in range(2):
                    src = ins[name][0].rearrange("(b o) i j -> o i b j", o=2)[odd]
                    s = slice(odd * 64, odd * 64 + 64)
                    sp.dma_start(bd[s, w, :, s], src).then_inc(c["lru_gates_in"], 16)

        @block.scalar
        def _(act):
            for k in range(n):
                act.activation(xc[:, k, :], m.a[:, k, :], ACT.Identity,
                               bias=vcol(m, "lru_conv_b", k), scale=vcol(m, "lru_conv_w", 12 + k)
                               ).then_inc(c["lru_centre"], 1)
            act.wait_ge(c["lru_small"], 3)
            act.activation(small[:, 3, :], small[:, 2, :], ACT.Exp).then_inc(c["lru_u"], 1)
            for k in range(n):
                for w, (name, dst) in enumerate((("gate_a_b", ra), ("gate_x_b", gi))):
                    act.wait_ge(c["lru_gate"], 2 * k + w + 1)
                    act.activation(dst[:, k, :], gate_ps(w), ACT.Sigmoid, bias=vcol(m, name, k)
                                   ).then_inc(c["lru_sigmoid"], 1)
            act.wait_ge(c["lru_coefs"], 2)
            act.wait_ge(c["lru_sigmoid"], 2 * n)
            for k in range(n):
                act.activation(mi[:, k, :], ra[:, k, :], ACT.Tanh, scale=small[:, 10, k:k + 1]
                               ).then_inc(c["lru_tanh"], 1)
                act.wait_ge(c["lru_tanh"], k + 1)
                act.activation(ra[:, k, :], ra[:, k, :], ACT.Exp, scale=small[:, 11, k:k + 1]
                               ).then_inc(c["lru_a"], 1)
            for k in range(n):
                act.wait_ge(c["lru_a"], k + 1)
                act.wait_ge(c["lru_ix"], k + 1)
                act.activation(xc[:, k, :], ra[:, k, :], ACT.Square).then_inc(c["lru_a2"], 1)
            for k in range(n):
                act.wait_ge(c["lru_m2"], k + 1)
                act.activation(mi[:, k, :], mi[:, k, :], ACT.Sqrt).then_inc(c["lru_m"], 1)
            for k in range(n):
                act.activation(m.a[:, 4 + k, :], m.a[:, 4 + k, :], ACT.Gelu_apprx_tanh
                               ).then_inc(c["lru_gelu"], 1)
            for h in range(2):
                rms[h].act_squares(act, lambda i: act.wait_ge(c["lru_y"], i + 1))
                rms[h].act_root(act)

        @block.tensor
        def _(pe):
            pe.wait_ge(c["lru_gates_in"], 64)
            for k in range(n):
                pe.wait_ge(c["lru_side"], 3 * k + 3)
                for w in range(2):
                    if k:
                        pe.wait_ge(c["lru_sigmoid"], 2 * k + w - 1)
                    for h in range(2):
                        last = pe.matmul(m.ps[:, 2 * w + h, :], bd[:, w, k, :],
                                         xc[:, k, h * HALF:(h + 1) * HALF], start=True, stop=True)
                    last.then_inc(c["lru_gate"], 1)
            for h in range(2):
                rms[h].pe_sums(pe)
                rms[h].pe_turn(pe)
                rms[h].pe_broadcast(pe, 0)

        @block.gpsimd
        def _(pool):
            pool.memset(bd[:], 0.0).then_inc(c["lru_zero"], 1)

        @block.vector
        def _(dve):
            done = 0

            def step(ins):
                nonlocal done
                done += 1
                ins.then_inc(c["lru_small"], 1)
                dve.wait_ge(c["lru_small"], done)

            step(dve.tensor_scalar(small[:, 0, :], lam, -1.0, None, ALU.mult))
            step(dve.tensor_scalar(small[:, 1, :], small[:, 0, :], 0.0, None, ALU.max))
            step(dve.tensor_tensor(small[:, 2, :], small[:, 0, :], lam, ALU.min))
            dve.wait_ge(c["lru_u"], 1)
            step(dve.tensor_scalar(small[:, 4, :], small[:, 3, :], 2.0, None, ALU.add))
            step(dve.reciprocal(small[:, 5, :], small[:, 4, :]))
            step(dve.tensor_tensor(small[:, 6, :], small[:, 3, :], small[:, 5, :], ALU.mult))
            step(dve.tensor_tensor(small[:, 7, :], small[:, 6, :], small[:, 6, :], ALU.mult))
            step(dve.tensor_scalar(small[:, 8, :], small[:, 7, :], 1.0 / (2 * terms + 1), None,
                                   ALU.mult))
            for i in range(terms - 1, 0, -1):
                step(dve.scalar_tensor_tensor(out=small[:, 8, :], in0=small[:, 8, :],
                                              scalar=1.0 / (2 * i + 1), in1=small[:, 7, :],
                                              op0=ALU.add, op1=ALU.mult))
            step(dve.scalar_tensor_tensor(out=small[:, 8, :], in0=small[:, 8, :], scalar=1.0,
                                          in1=small[:, 6, :], op0=ALU.add, op1=ALU.mult))
            step(dve.scalar_tensor_tensor(out=small[:, 9, :], in0=small[:, 8, :], scalar=2.0,
                                          in1=small[:, 1, :], op0=ALU.mult, op1=ALU.add))
            dve.tensor_scalar(small[:, 10, :], small[:, 9, :], LRU_C, None, ALU.mult
                              ).then_inc(c["lru_coefs"], 1)
            dve.tensor_scalar(small[:, 11, :], small[:, 9, :], -LRU_C, None, ALU.mult
                              ).then_inc(c["lru_coefs"], 1)
            for k in range(n):
                dve.wait_ge(c["lru_centre"], k + 1)
                for tap in range(3):
                    back = 3 - tap
                    if tap:
                        dve.wait_ge(c["lru_side"], 3 * k + tap)
                    dve.scalar_tensor_tensor(
                        out=xc[:, k, back:T], in0=m.a[:, k, 0:T - back],
                        scalar=vcol(m, "lru_conv_w", 4 * tap + k), in1=xc[:, k, back:T],
                        op0=ALU.mult, op1=ALU.add).then_inc(c["lru_side"], 1)
            for k in range(n):
                dve.wait_ge(c["lru_sigmoid"], 2 * k + 2)
                dve.tensor_tensor(gi[:, k, :], gi[:, k, :], xc[:, k, :], ALU.mult
                                  ).then_inc(c["lru_ix"], 1)
            for k in range(n):
                dve.wait_ge(c["lru_a2"], k + 1)
                dve.scalar_tensor_tensor(out=mi[:, k, :], in0=xc[:, k, :], scalar=1.0,
                                         in1=mi[:, k, :], op0=ALU.add, op1=ALU.mult
                                         ).then_inc(c["lru_m2"], 1)
            for k in range(n):
                dve.wait_ge(c["lru_m"], k + 1)
                dve.tensor_tensor(mi[:, k, :], mi[:, k, :], gi[:, k, :], ALU.mult
                                  ).then_inc(c["lru_in"], 1)
                dve.wait_ge(c["lru_in"], k + 1)
                dve.tensor_tensor_scan(xc[:, k, :], ra[:, k, :], mi[:, k, :], 0.0, ALU.mult,
                                       ALU.add).then_inc(c["lru_scan"], 1)
            for k in range(n):
                dve.wait_ge(c["lru_gelu"], k + 1)
                dve.wait_ge(c["lru_scan"], k + 1)
                dve.tensor_tensor(m.a[:, k, :], xc[:, k, :], m.a[:, 4 + k, :], ALU.mult
                                  ).then_inc(c["lru_y"], 1)
            for h in range(2):
                rms[h].dve_inverse(dve)
                rms[h].dve_row(dve)
                bank = rms[h].ready(dve, 0)
                for k in range(n):
                    y = m.a[:, k, h * HALF:(h + 1) * HALF]
                    dve.scalar_tensor_tensor(out=y, in0=y, scalar=vcol(m, "lru_norm", k), in1=bank,
                                             op0=ALU.mult, op1=ALU.mult
                                             ).then_inc(c["lru_out"], 1)


def retention_stage(nc, c, m, ins):
    nh = RET_HEADS
    q, k, v, gate = (m.a[:, 8 + 4 * i:12 + 4 * i, :] for i in range(4))
    t = m.at("ret_work", XN, [P, 16, T])
    cos, sin = t[:, 0, :], t[:, 1, :]
    direct, swapped = t[:, 2, :], t[:, 3, :]
    v_rows = t[:, 4:8, :].rearrange("p a (b e) -> p (a b) e", b=2)
    k_rows = t[:, 8:12, :].rearrange("p a (b e) -> p (a b) e", b=2)
    decay = t[:, 12, 0:HALF]
    q_decay = t[:, 12, HALF:T]
    state = [t[:, 13, 0:HALF], t[:, 13, HALF:T]]
    masked = [t[:, 14, 0:HALF], t[:, 14, HALF:T]]
    q_scaled = [t[:, 15, 0:HALF], t[:, 15, HALF:T]]
    perm = m.at("ret_perm", YX, [P, P])
    zeta = m.at("ret_zeta", YX + 512, [P, nh])
    squares = m.at("ret_squares", YX + 8192, [P, 4, HALF])
    carry = [float(np.exp(np.float32(P) * np.float32(g))) for g in RET_DECAY]
    items = [(x, h, slice(half * HALF, (half + 1) * HALF)) for h in range(nh)
             for x in (q, k) for half in range(2)]
    outs = [(h, slice(half * HALF, (half + 1) * HALF)) for h in range(nh) for half in range(2)]
    rms = RootMeanSquare(c, m, "ret", len(outs), 1, 4, P, lambda i: v[:, outs[i][0], outs[i][1]],
                         [squares[:, i, :] for i in range(4)], m.ps[:, 4, :], m.ps[:, 5, :],
                         [m.ps[:, 6, :], m.ps[:, 7, :]], 0)

    with nc.Block() as block:
        @block.sync
        def _(sp):
            sp.dma_start(perm[:], ins["k_perm2"]).then_inc(c["ret_in"], 16)
            sp.dma_start(cos, ins["k_cos2"]).then_inc(c["ret_in"], 16)
            sp.dma_start(sin, ins["k_sin2"]).then_inc(c["ret_in"], 16)
            sp.dma_start(decay, ins["k_decay"]).then_inc(c["ret_in"], 16)
            sp.dma_start(q_decay, ins["k_q_decay"].unsqueeze(0).to_broadcast([P, HALF])
                         ).then_inc(c["ret_in"], 16)
            sp.dma_start(zeta[:], ins["k_zeta"]).then_inc(c["ret_in"], 16)

        @block.tensor
        def _(pe):
            pe.wait_ge(c["ret_in"], 96)
            for i, (x, h, s) in enumerate(items):
                if i >= 2:
                    pe.wait_ge(c["ret_sin"], i - 1)
                pe.matmul(m.ps[:, i % 2, :], perm[:], x[:, h, s], start=True, stop=True
                          ).then_inc(c["ret_swapped"], 1)
            for n in range(TT):
                tok = slice(n * P, (n + 1) * P)
                for w, x in enumerate((v, k)):
                    j = 2 * n + w
                    if w == 0 and n == 0:
                        pe.wait_ge(c["ret_rotated"], len(items))
                    if j >= 2:
                        pe.wait_ge(c["ret_rows_v" if w == 0 else "ret_rows_k"], n)
                    for h in range(nh):
                        last = pe.transpose(m.ps[:, 2 + w, h * P:(h + 1) * P], x[:, h, tok],
                                            m.ident[:])
                    last.then_inc(c["ret_turned"], 1)
            for n in range(TT):
                tok = slice(n * P, (n + 1) * P)
                if n:
                    pe.wait_ge(c["ret_masked"], n)
                for h in range(nh):
                    last = pe.matmul(m.ps[:, 0, h * P:(h + 1) * P], k[:, h, tok], q[:, h, tok],
                                     start=True, stop=True)
                last.then_inc(c["ret_scores"], 1)
                if n < TT - 1:
                    pe.wait_ge(c["ret_rows_v"], n + 1)
                    pe.wait_ge(c["ret_rows_k"], n + 1)
                    if n:
                        pe.wait_ge(c["ret_state"], nh * n)
                    for h in range(nh):
                        hs = slice(h * P, (h + 1) * P)
                        last = pe.matmul(m.ps[:, 1, hs], k_rows[:, n, hs], v_rows[:, n, hs],
                                         start=True, stop=True)
                    last.then_inc(c["ret_kv"], 1)
                pe.wait_ge(c["ret_rows_v"], n + 1)
                pe.wait_ge(c["ret_masked"], n + 1)
                if n >= 2:
                    pe.wait_ge(c["ret_copied"], n - 1)
                if n:
                    pe.wait_ge(c["ret_q_scaled"], n)
                    pe.wait_ge(c["ret_state"], nh * n)
                for h in range(nh):
                    hs = slice(h * P, (h + 1) * P)
                    out = m.ps[:, 6 + n % 2, hs]
                    last = pe.matmul(out, v_rows[:, n, hs], masked[n % 2][:, hs], start=True,
                                     stop=(n == 0))
                    if n:
                        last = pe.matmul(out, state[n % 2][:, hs], q_scaled[n % 2][:, hs],
                                         start=False, stop=True)
                last.then_inc(c["ret_out"], 1)
            for i, (h, s) in enumerate(outs):
                if i == 0:
                    pe.wait_ge(c["ret_copied"], TT)
                if i >= 2:
                    pe.wait_ge(c["ret_centred"], i - 1)
                pe.matmul(m.ps[:, i % 2, :], m.ones[:, 0:1].to_broadcast([P, P]), v[:, h, s],
                          start=True, stop=True).then_inc(c["ret_sums"], 1)
            rms.pe_sums(pe)
            rms.pe_turn(pe)
            for g in range(len(outs)):
                rms.pe_broadcast(pe, g)

        @block.scalar
        def _(act):
            for n in range(TT):
                act.wait_ge(c["ret_turned"], 2 * n + 1)
                act.activation(v_rows[:, n, :], m.ps[:, 2, :], ACT.Copy
                               ).then_inc(c["ret_rows_v"], 1)
            for n in range(TT):
                act.wait_ge(c["ret_out"], n + 1)
                act.activation(v[:, :, n * P:(n + 1) * P], two(m.ps[:, 6 + n % 2, :], nh), ACT.Copy
                               ).then_inc(c["ret_copied"], 1)
            for h in range(nh):
                act.activation(gate[:, h, :], gate[:, h, :], ACT.Silu).then_inc(c["ret_silu"], 1)
            rms.act_squares(act, lambda i: act.wait_ge(c["ret_centred"], i + 1))
            rms.act_root(act)

        @block.gpsimd
        def _(pool):
            pool.wait_ge(c["ret_in"], 96)
            for i, (x, h, s) in enumerate(items):
                if i >= 2:
                    pool.wait_ge(c["ret_rotated"], i - 1)
                pool.tensor_tensor(two(direct)[:, i % 2, :], x[:, h, s], cos[:, s], ALU.mult
                                   ).then_inc(c["ret_direct"], 1)
            pool.wait_ge(c["ret_rotated"], len(items))
            for n in range(1, TT):
                if n >= 3:
                    pool.wait_ge(c["ret_out"], n - 1)
                pool.tensor_tensor(two(q_scaled[n % 2], nh), q[:, :, n * P:(n + 1) * P],
                                   two(q_decay, nh), ALU.mult).then_inc(c["ret_q_scaled"], 1)

        @block.vector
        def _(dve):
            dve.wait_ge(c["ret_in"], 96)
            for i, (x, h, s) in enumerate(items):
                dve.wait_ge(c["ret_swapped"], i + 1)
                dve.tensor_tensor(two(swapped)[:, i % 2, :], m.ps[:, i % 2, :], sin[:, s],
                                  ALU.mult).then_inc(c["ret_sin"], 1)
                dve.wait_ge(c["ret_sin"], i + 1)
                dve.wait_ge(c["ret_direct"], i + 1)
                dve.tensor_tensor(x[:, h, s], two(direct)[:, i % 2, :], two(swapped)[:, i % 2, :],
                                  ALU.add).then_inc(c["ret_rotated"], 1)
            for n in range(TT):
                dve.wait_ge(c["ret_turned"], 2 * n + 2)
                dve.tensor_tensor(two(k_rows[:, n, :], nh), two(m.ps[:, 3, :], nh),
                                  zeta[:].unsqueeze(2).to_broadcast([P, nh, P]), ALU.mult
                                  ).then_inc(c["ret_rows_k"], 1)
            for n in range(TT):
                dve.wait_ge(c["ret_scores"], n + 1)
                if n >= 2:
                    dve.wait_ge(c["ret_out"], n - 1)
                dve.tensor_tensor(masked[n % 2], m.ps[:, 0, :], decay, ALU.mult
                                  ).then_inc(c["ret_masked"], 1)
                if n < TT - 1:
                    dve.wait_ge(c["ret_kv"], n + 1)
                    if n >= 1:
                        dve.wait_ge(c["ret_out"], n)
                        dve.wait_ge(c["ret_state"], nh * n)
                    for h in range(nh):
                        hs = slice(h * P, (h + 1) * P)
                        if n == 0:
                            dve.tensor_copy(state[1][:, hs], m.ps[:, 1, hs]
                                            ).then_inc(c["ret_state"], 1)
                        else:
                            dve.scalar_tensor_tensor(
                                out=state[(n + 1) % 2][:, hs], in0=state[n % 2][:, hs],
                                scalar=carry[h], in1=m.ps[:, 1, hs], op0=ALU.mult, op1=ALU.add
                                ).then_inc(c["ret_state"], 1)
            for i, (h, s) in enumerate(outs):
                dve.wait_ge(c["ret_sums"], i + 1)
                dve.scalar_tensor_tensor(out=v[:, h, s], in0=m.ps[:, i % 2, :], scalar=-1.0 / P,
                                         in1=v[:, h, s], op0=ALU.mult, op1=ALU.add
                                         ).then_inc(c["ret_centred"], 1)
            rms.dve_inverse(dve)
            rms.dve_row(dve)
            for i, (h, s) in enumerate(outs):
                bank = rms.ready(dve, i)
                rms.used(dve.scalar_tensor_tensor(
                    out=v[:, h, s], in0=v[:, h, s], scalar=vcol(m, "ret_norm", h), in1=bank,
                    op0=ALU.mult, op1=ALU.mult))
                dve.wait_ge(c["rms_broadcast_used"], rms.free0 + i + 1)
                dve.wait_ge(c["ret_silu"], h + 1)
                dve.tensor_tensor(m.a[:, 4 + h, s], v[:, h, s], gate[:, h, s], ALU.mult
                                  ).then_inc(c["ret_done"], 1)


def final_stage(nc, c, m, out):
    parts = halves_parts(m, lambda k: vcol(m, "final", k), lambda k: 0.0)
    pre = PreNorm(c, m, "final", parts, split=False)
    rows = m.at("out_rows", XN, [P, TT, D])
    out_tiles = out.rearrange("b (t p) d -> (b t) p d", p=P)
    groups = [(t, g) for t in range(TT) for g in range(2)]
    with nc.Block() as block:
        @block.scalar
        def _(act):
            pre.act(act)

        @block.tensor
        def _(pe):
            for j in range(2):
                pre.pe_sums(pe, j)
                pre.pe_spread(pe, j)
            for i, (t, g) in enumerate(groups):
                pe.wait_ge(c["pre_shifted"], pre.aff0 + KD * (t // 4 + 1))
                if i >= 4:
                    pe.wait_ge(c["out_copied"], i - 3)
                for q in range(4):
                    k = 4 * g + q
                    last = pe.transpose(m.ps[:, i % 4, q * P:(q + 1) * P],
                                        m.a[:, k, t * P:(t + 1) * P], m.ident[:])
                last.then_inc(c["out_turned"], 1)

        @block.vector
        def _(dve):
            pre.dve(dve)
            for i, (t, g) in enumerate(groups):
                dve.wait_ge(c["out_turned"], i + 1)
                dve.tensor_copy(rows[:, t, g * HALF:(g + 1) * HALF], m.ps[:, i % 4, :]
                                ).then_inc(c["out_copied"], 1)

        @block.sync
        def _(sp):
            for t in range(TT):
                sp.wait_ge(c["out_copied"], 2 * t + 2)
                sp.dma_start(out_tiles[t], rows[:, t, :]).then_inc(c["out_stored"], 16)
            sp.wait_ge(c["out_stored"], 16 * TT)


def build(nc, ins, out):
    c = Counters(nc)
    m = Memory(nc)
    x_dram = nc.dram_tensor("x_scratch", [P, KD, T], F32).ap()
    load_vectors(nc, c, m, ins)
    m.gains_sw = m.vec("gains_sw", [P, 2])
    m.at_max, m.at_neg = m.vec("at_max", [P, 4]), m.vec("at_neg", [P, 4])
    m.at_sum, m.at_inv = m.vec("at_sum", [P, 4]), m.vec("at_inv", [P, 4])
    attention_memory(m)

    parts = halves_parts(m, lambda k: m.coef[:, 0, 0, k:k + 1], lambda k: mod_col(m, 0, 0, k),
                         squares=5)
    parts.append(dict(
        source=lambda k: m.ctx_cm[:, k, :], work=lambda k: m.ctx_cm[:, k, :],
        hi=lambda k: m.xnc_hi[:, k, :], lo=lambda k: m.xnc_lo[:, k, :],
        scale=lambda k: m.coef_ctx[:, k:k + 1], shift=lambda k: mod_col(m, 0, 0, k, 1), tiles=2,
        stat=m.ps[:, 4, 16:24], turned=m.ps[:, 5, 2 * P:3 * P], bank=m.ps[:, 4, 256:512], small=8,
        squares=[m.a[:, 23, i * CTX:(i + 1) * CTX] for i in range(4)]))
    project_stage(nc, c, m, "qkv", PreNorm(c, m, "qkv", parts), ins["w_qkv"][0], 12, HEADS,
                  lambda u: (m.a[:, bass.ds(u, 1), :].rearrange("p o t -> p (o t)")
                             if not isinstance(u, int) or u < HEADS
                             else m.kv_raw[:, u - HEADS, CTX:KEYS]),
                  lambda u: m.kv_raw[:, u - HEADS, 0:CTX])
    rotate_stage(nc, c, m, ins)
    attention_stage(nc, c, m)
    w_o = ins["w_o"][0].rearrange("(k p) n -> p k n", p=P)
    down_stage(nc, c, m, "w_o", KD, [KD], lambda i, b, g: w_o[:, :, bass.ds(i * 256 + b * P, P)],
               lambda i, b: 0, None, lambda k: m.coef[:, 0, 1, k:k + 1], x_dram, False, True)

    def ffn(layer):
        parts = halves_parts(m, lambda k: m.coef[:, layer, 2, k:k + 1],
                             lambda k: mod_col(m, layer, 3, k))
        cw, cb = m.col[f"conv_w{layer}"], m.col["conv_b"] + layer * FF1
        ffn_up_stage(nc, c, m, f"up{layer}", PreNorm(c, m, f"up{layer}", parts),
                     ins["w_up"][layer], FF1,
                     lambda tap, j: m.vt[:, bass.ds(j + (cw + tap * FF1), 1)],
                     lambda j: m.vt[:, bass.ds(j + cb, 1)], False, None)
        w = ins["w_down"][layer].rearrange("(k p) n -> p k n", p=P)
        sizes = [8, 8, 6]
        down_stage(nc, c, m, f"down{layer}", FF1, sizes,
                   lambda i, b, g: w[:, 8 * g:8 * g + sizes[g], bass.ds(i * 256 + b * P, P)],
                   lambda i, b: 0, None, lambda k: m.coef[:, layer, 3, k:k + 1], x_dram, True,
                   True)

    ffn(0)
    pool_stage(nc, c, m, ins)
    w_pool = ins["w_pool"][0].rearrange("g (k p) n -> p g k n", p=P)
    bps = m.vec("pool_bias", [P, KD])
    with nc.Block() as block:
        @block.vector
        def _(dve):
            dve.tensor_tensor(bps[:], m.vt[:, m.col["b_pool"]:m.col["b_pool"] + KD],
                              m.vt[:, m.col["pool_scale"]:m.col["pool_scale"] + KD], ALU.mult
                              ).then_inc(c["pool_bias"], 1)
    down_stage(nc, c, m, "w_pool", KD, [2],
               lambda i, b, g: w_pool[:, bass.ds(i, 1), :, b * P:(b + 1) * P].rearrange(
                   "p g k n -> p (g k) n"),
               lambda i, b: 2 * i,
               (lambda n: m.vt[:, bass.ds(n + m.col["pool_scale"], 1)],
                lambda n: bps[:, bass.ds(n, 1)]),
               lambda k: m.coef[:, 1, 1, k:k + 1], x_dram, False, True)
    ffn(1)

    parts = halves_parts(m, lambda k: vcol(m, "norm1", k), lambda k: 0.0)
    project_stage(nc, c, m, "w_in", PreNorm(c, m, "w_in", parts), ins["w_in_2"][0], 24, 24,
                  lambda u: m.a[:, bass.ds(u, 1), :].rearrange("p o t -> p (o t)"), None)
    lru_stage(nc, c, m, ins)
    retention_stage(nc, c, m, ins)
    w_out = ins["w_out_2"][0].rearrange("(k p) n -> p k n", p=P)
    down_stage(nc, c, m, "w_out", KD, [KD],
               lambda i, b, g: w_out[:, :, bass.ds(i * 256 + b * P, P)],
               lambda i, b: 0, None, None, x_dram, True, True)
    parts = halves_parts(m, lambda k: vcol(m, "norm2", k), lambda k: 0.0)
    ffn_w = [m.col[f"ffn_w{tap}"] for tap in range(3)]
    ffn_up_stage(nc, c, m, "up2", PreNorm(c, m, "up2", parts), ins["ffn_up_w_2"][0], FF2,
                 lambda tap, j: m.vt[:, bass.ds(j + ffn_w[tap], 1)],
                 lambda j: m.vt[:, bass.ds(j + m.col["ffn_b"], 1)], True, None)
    w_d = ins["ffn_down_w_2"][0].rearrange("(k p) n -> p k n", p=P)
    down_stage(nc, c, m, "down2", FF2, [8, 8, 8],
               lambda i, b, g: w_d[:, 8 * g:8 * g + 8, bass.ds(i * 256 + b * P, P)],
               lambda i, b: 0, None, None, x_dram, True, False)
    final_stage(nc, c, m, out)


_INS = ["x", "c", "ctx", "c_ctx", "w_mod", "b_mod", "g_pre_mix", "g_post_mix", "g_pre_ffn",
        "g_post_ffn", "w_qkv", "g_q", "g_k", "w_o", "w_pool", "b_pool", "pool_scale", "w_up",
        "conv_w", "conv_b", "w_down", "norm1_gain_2", "w_in_2", "lru_conv_w_2", "lru_conv_b_2",
        "lru_gate_a_w_2", "lru_gate_a_b_2", "lru_gate_x_w_2", "lru_gate_x_b_2", "lru_lambda_2",
        "lru_norm_gain_2", "ret_norm_gain_2", "w_out_2", "norm2_gain_2", "ffn_up_w_2",
        "ffn_conv_w_2", "ffn_conv_b_2", "ffn_down_w_2", "final_norm_gain_2"]


def constants():
    f = np.float32
    t = np.arange(T)
    d = np.arange(P)
    inv = (f(10000.0) ** (-np.arange(32, dtype=f) / f(32))).astype(f)
    pos = np.where((d // 64)[:, None] == 0, (t // 64)[None], (t % 64)[None]).astype(f)
    ang = (pos * inv[d % 32][:, None]).astype(f)
    sign = np.where(d % 64 < 32, -1, 1).astype(f)[:, None]
    k = {"k_ident": np.eye(P, dtype=f), "k_cos1": np.cos(ang), "k_sin1": sign * np.sin(ang),
         "k_perm1": np.eye(P, dtype=f)[d ^ 32]}
    inv = (f(10000.0) ** (-np.arange(0, P, 2, dtype=f) / f(P))).astype(f)
    ang = (t.astype(f)[None] * inv[d % 64][:, None]).astype(f)
    sign = np.where(d < 64, -1, 1).astype(f)[:, None]
    k.update(k_cos2=np.cos(ang), k_sin2=sign * np.sin(ang), k_perm2=np.eye(P, dtype=f)[d ^ 64])
    k["k_pool_inverse"] = np.stack([
        1.0 / (np.minimum(t + w - w // 2, T) - np.maximum(t - w // 2, 0)) for w in (2, 4, 8, 16)])
    log_g = np.log1p(-np.exp2(f(-5.0) - np.arange(RET_HEADS, dtype=f))).astype(f)
    diff = (d[None, :] - d[:, None]).astype(f)
    decay = np.where(diff >= 0, np.exp(np.maximum(diff, 0)[:, None, :] * log_g[None, :, None])
                     .transpose(1, 0, 2), 0.0)
    k["k_decay"] = (decay.transpose(1, 0, 2) * RET_SCALE).reshape(P, RET_HEADS * P)
    k["k_zeta"] = np.exp((P - 1 - d).astype(f)[:, None] * log_g[None, :]) * RET_SCALE
    k["k_q_decay"] = np.exp((d + 1).astype(f)[None, :] * log_g[:, None]).reshape(-1)
    return {name: np.ascontiguousarray(v.astype(f)) for name, v in k.items()}


def kernel(**inputs):
    import concourse.bacc as bacc
    from concourse.bass_utils import run_bass_kernel_spmd as run

    nc = bacc.Bacc("TRN2", target_bir_lowering=False, num_devices=1)
    arrays, ins = {}, {}
    for name, a in [(n, np.ascontiguousarray(inputs[n])) for n in _INS] + list(constants().items()):
        arrays[f"in_{name}"] = a
        ins[name] = nc.dram_tensor(f"in_{name}", a.shape, mybir.dt.from_np(a.dtype),
                                   kind="ExternalInput").ap()
    out = nc.dram_tensor("out_x", [1, T, D], F32, kind="ExternalOutput").ap()
    build(nc, ins, out)
    r = run(nc, [arrays], core_ids=[0])
    return r.results[0]["out_x"]
```

```python
import math

import numpy as np

import concourse.bass as bass
from concourse import mybir

F32 = mybir.dt.float32
F32R = mybir.dt.float32r
ALU = mybir.AluOpType
ACT = mybir.ActivationFunctionType
AX_X = mybir.AxisListType.X

P = 128
D = 1024
KD = D // P
T = 1024
HALF = 512
TT = T // P
CTX = 256
KEYS = CTX + T
HEADS, KV, GROUP = 8, 2, 4
FF1, FF2 = 2816 // P, 3072 // P
RET_HEADS = 4
EPS = 1e-6
ATT_SCALE = 1.0 / math.sqrt(P)
RET_SCALE = float(P) ** -0.5
RET_DECAY = [float(np.log1p(-np.exp2(np.float32(-5.0 - h)))) for h in range(RET_HEADS)]
LRU_C = 8.0
PROBS = 5

BASE = 16512
CONST = 0
W_RAW = 7936
W_HI = W_RAW + 2 * 4096
W_LO = W_HI + 2 * 4096
YX = W_LO + 2 * 4096
XN = YX + 16384
A0 = XN + 65536
END = A0 + 24 * 4096


class Counters:

    def __init__(self, nc):
        self.nc, self.sems, self.reached = nc, {}, {}

    def __getitem__(self, name):
        if name not in self.sems:
            self.sems[name] = self.nc.alloc_semaphore(name)
            self.reached.setdefault(name, 0)
        return self.sems[name]

    def take(self, name, total):
        self[name]
        before = self.reached[name]
        self.reached[name] = before + total
        return before


class Memory:

    def __init__(self, nc):
        self.nc, self.small = nc, CONST

        def at(name, offset, shape, dtype=F32):
            return nc.alloc_sbuf_tensor_at(name, shape, dtype, offset=BASE + offset)

        self.at = at
        self.w_raw = at("w_raw", W_RAW, [P, 2, 8, P])
        self.w_hi = at("w_hi", W_HI, [P, 2, 8, P], F32R)
        self.w_lo = at("w_lo", W_LO, [P, 2, 8, P], F32R)
        self.xn_hi = at("xn_hi", XN, [P, KD, T], F32R)
        self.xn_lo = at("xn_lo", XN + 32768, [P, KD, T], F32R)
        self.ring = at("ring", XN, [P, 32, HALF], F32R)
        self.a = at("a", A0, [P, 24, T])
        self.a_lo = [at(f"a_lo{i}", A0 + 32768 * i, [P, 8, T], F32R) for i in range(3)]
        self.x = self.a[:, 8:16, :]
        self.yx = at("yx", YX, [P, KD, HALF])
        self.xnc_hi = at("xnc_hi", YX, [P, KD, CTX], F32R)
        self.xnc_lo = at("xnc_lo", YX + 8192, [P, KD, CTX], F32R)
        self.ps = nc.alloc_psum_tensor("ps", [P, 8, 512], F32)

    def vec(self, name, shape):
        n = 4 * int(np.prod(shape[1:]))
        t = self.at(name, self.small, shape)
        self.small += (n + 31) // 32 * 32
        assert self.small <= W_RAW, self.small
        return t


def stand_alone(eng, c):
    eng.sem_inc(c[f"waits_passed_{str(eng.engine).split('.')[-1].lower()}"], 1)


class WeightStream:

    def __init__(self, c, m, units):
        assert units % 2 == 0
        self.c, self.m = c, m
        self.raw0 = [c.take(f"w_raw{s}", 16 * units // 2) for s in (0, 1)]
        self.hi0 = c.take("w_hi", units)
        self.lo0 = c.take("w_lo", units)
        self.done0 = c.take("unit_done", units)

    def load(self, sp, u, slot, src):
        kc = src.shape[1]
        sp.wait_ge(self.c["w_lo"], self.lo0 + u + 1)
        sp.dma_start(self.m.w_raw[:, slot, 0:kc, :], src).then_inc(self.c[f"w_raw{slot}"], 16)

    def split(self, pool, u, pair, slot, kc):
        raw = self.m.w_raw[:, slot, 0:kc, :]
        hi = self.m.w_hi[:, slot, 0:kc, :]
        pool.wait_ge(self.c[f"w_raw{slot}"], 16 * pair + self.raw0[slot] + 16)
        pool.wait_ge(self.c["unit_done"], self.done0 + u + 1)
        stand_alone(pool, self.c)
        pool.tensor_scalar(hi, raw, 1.0, 1.0, ALU.mult, ALU.mult).then_inc(self.c["w_hi"], 1)
        pool.wait_ge(self.c["w_hi"], self.hi0 + u + 1)
        pool.tensor_tensor(self.m.w_lo[:, slot, 0:kc, :], raw, hi.bitcast(F32),
                           ALU.subtract).then_inc(self.c["w_lo"], 1)

    def ready(self, pe, u):
        pe.wait_ge(self.c["w_lo"], self.lo0 + u + 3)

    def products(self, pe, slot, out, k, hi, lo, start, stop):
        w_hi, w_lo = self.m.w_hi[:, slot, k, :], self.m.w_lo[:, slot, k, :]
        pe.matmul(out, w_hi, hi, start=start, stop=False)
        pe.matmul(out, w_hi, lo, start=False, stop=False)
        return pe.matmul(out, w_lo, hi, start=False, stop=stop)

    def finished(self, eng, u):
        eng.wait_ge(self.c["unit_done"], self.done0 + u + 3)


class RootMeanSquare:

    def __init__(self, c, m, name, groups, chunks, tiles, count, source, squares, stat, turned,
                 broadcast, small):
        self.c, self.m = c, m
        self.groups, self.chunks, self.tiles, self.count = groups, chunks, tiles, count
        self.source, self.squares = source, squares
        self.stat, self.turned, self.broadcast = stat, turned, broadcast
        self.cols = groups * tiles
        self.sd = m.rms_sd[:, small:small + self.cols]
        self.rs = m.rms_rs[:, small:small + self.cols]
        self.row = m.rms_row[small // 4] if self.cols <= 4 else m.rms_rows
        n = groups * chunks
        self.n = n
        self.sq0 = c.take("rms_squared", n)
        self.sum0 = c.take("rms_summed", n)
        self.sd0 = c.take("rms_root", 1)
        self.rc0 = c.take("rms_inverse", 1)
        self.tr0 = c.take("rms_turned", 1)
        self.row0 = c.take("rms_row", 1)
        self.rb0 = c.take("rms_broadcast", groups)
        self.free0 = c.take("rms_broadcast_used", groups if groups > len(broadcast) else 0)

    def act_squares(self, act, before=None):
        slots = len(self.squares)
        for i in range(self.n):
            if before:
                before(i)
            if i >= slots:
                act.wait_ge(self.c["rms_summed"], self.sum0 + i - slots + 1)
            src, out = self.source(i), self.squares[i % slots]
            if len(src.shape) == 3:
                out = out.rearrange("p (a t) -> p a t", a=src.shape[1])
            act.activation(out, src, ACT.Square).then_inc(self.c["rms_squared"], 1)

    def pe_sums(self, pe):
        for i in range(self.n):
            pe.wait_ge(self.c["rms_squared"], self.sq0 + i + 1)
            g, k = divmod(i, self.chunks)
            for t in range(self.tiles):
                col = g * self.tiles + t
                last = pe.matmul(self.stat[:, col:col + 1],
                                 self.squares[i % len(self.squares)][:, t * P:(t + 1) * P],
                                 self.m.ones[:, 0:1], start=(k == 0 and t == 0),
                                 stop=(k == self.chunks - 1), skip_group_check=True)
            last.then_inc(self.c["rms_summed"], 1)

    def act_root(self, act):
        act.wait_ge(self.c["rms_summed"], self.sum0 + self.n)
        act.activation(self.sd, self.stat[:, 0:self.cols], ACT.Sqrt, bias=self.m.eps[:, 0:1],
                       scale=1.0 / self.count).then_inc(self.c["rms_root"], 1)

    def dve_inverse(self, dve):
        dve.wait_ge(self.c["rms_root"], self.sd0 + 1)
        dve.reciprocal(self.rs, self.sd).then_inc(self.c["rms_inverse"], 1)

    def pe_turn(self, pe):
        pe.wait_ge(self.c["rms_inverse"], self.rc0 + 1)
        pe.transpose(self.turned[0:self.cols, 0:P], self.rs, self.m.ident[:]
                     ).then_inc(self.c["rms_turned"], 1)

    def dve_row(self, dve):
        dve.wait_ge(self.c["rms_turned"], self.tr0 + 1)
        dve.tensor_copy(self.row[0:self.cols, :], self.turned[0:self.cols, 0:P]
                        ).then_inc(self.c["rms_row"], 1)

    def pe_broadcast(self, pe, g):
        banks = len(self.broadcast)
        if g == 0:
            pe.wait_ge(self.c["rms_row"], self.row0 + 1)
        if g >= banks:
            pe.wait_ge(self.c["rms_broadcast_used"], self.free0 + g - banks + 1)
        out = self.broadcast[g % banks]
        for t in range(self.tiles):
            col = g * self.tiles + t
            last = pe.matmul(out[:, t * P:(t + 1) * P],
                             self.m.ident[0:self.cols, col:col + 1].to_broadcast([self.cols, P]),
                             self.row[0:self.cols, :], start=True, stop=True)
        last.then_inc(self.c["rms_broadcast"], 1)

    def ready(self, eng, g):
        eng.wait_ge(self.c["rms_broadcast"], self.rb0 + g + 1)
        return self.broadcast[g % len(self.broadcast)][:, 0:self.tiles * P]

    def used(self, last):
        return last.then_inc(self.c["rms_broadcast_used"], 1)


class PreNorm:

    def __init__(self, c, m, name, parts, split=True):
        self.c, self.m, self.parts, self.split = c, m, parts, split
        n = KD * len(parts)
        self.x0, self.aff0 = c.take("pre_scaled", n), c.take("pre_shifted", n)
        self.h0, self.l0 = c.take("pre_hi", n if split else 0), c.take("pre_lo", n if split else 0)
        self.rms = [
            RootMeanSquare(c, m, f"{name}{j}", 1, KD, p["tiles"], D, p["source"], p["squares"],
                           p["stat"], p["turned"], [p["bank"]], p["small"])
            for j, p in enumerate(parts)]

    def act(self, act):
        for j, (p, rms) in enumerate(zip(self.parts, self.rms)):
            rms.act_squares(act)
            rms.act_root(act)
            for k in range(KD):
                i = j * KD + k
                act.wait_ge(self.c["pre_scaled"], self.x0 + i + 1)
                act.activation(p["work"](k), p["work"](k), ACT.Identity, bias=p["shift"](k),
                               scale=p["scale"](k)).then_inc(self.c["pre_shifted"], 1)

    def pe_sums(self, pe, j):
        self.rms[j].pe_sums(pe)

    def pe_spread(self, pe, j):
        self.rms[j].pe_turn(pe)
        self.rms[j].pe_broadcast(pe, 0)

    def pool(self, pool):
        for j, p in enumerate(self.parts):
            for k in range(KD):
                i = j * KD + k
                pool.wait_ge(self.c["pre_shifted"], self.aff0 + i + 1)
                pool.tensor_scalar(p["hi"](k), p["work"](k), 1.0, 1.0, ALU.mult, ALU.mult
                                   ).then_inc(self.c["pre_hi"], 1)

    def dve(self, dve):
        for j, (p, rms) in enumerate(zip(self.parts, self.rms)):
            rms.dve_inverse(dve)
            rms.dve_row(dve)
            bank = rms.ready(dve, 0)
            for k in range(KD):
                last = dve.tensor_tensor(p["work"](k), p["source"](k), bank, ALU.mult)
                last.then_inc(self.c["pre_scaled"], 1)
            if self.split:
                for k in range(KD):
                    i = j * KD + k
                    dve.wait_ge(self.c["pre_hi"], self.h0 + i + 1)
                    dve.tensor_tensor(p["lo"](k), p["work"](k), p["hi"](k).bitcast(F32),
                                      ALU.subtract).then_inc(self.c["pre_lo"], 1)

    def ready(self, eng, part, k=KD - 1):
        eng.wait_ge(self.c["pre_lo"], self.l0 + part * KD + k + 1)


class Modulation:

    COLS = 2 * P

    def __init__(self, c, m, w_mod, layer, first, pieces, buf, acc, bank):
        self.c, self.m, self.layer, self.first, self.pieces = c, m, layer, first, pieces
        self.w = w_mod.rearrange("l (k p) n -> l p k n", p=P)[layer]
        self.buf, self.acc, self.sums = buf, acc, bank
        self.in0 = [c.take(f"mod_in{s}", 16 * pieces // 2) for s in range(2)]
        self.product0, self.reduced0 = c.take("mod_product", pieces), c.take("mod_reduced", pieces)
        self.summed0 = c.take("mod_summed", pieces)

    def load(self, sp, i, slot):
        sp.wait_ge(self.c["mod_reduced"], self.reduced0 + i + 1)
        sp.dma_start(self.buf[slot][:], self.w[:, :, bass.ds(i * self.COLS + self.first * P,
                                                             self.COLS)]
                     ).then_inc(self.c[f"mod_in{slot}"], 16)

    def product(self, pool, pair, slot):
        piece = self.buf[slot][:]
        pool.wait_ge(self.c[f"mod_in{slot}"], 16 * pair + self.in0[slot] + 16)
        pool.tensor_tensor(piece, piece, self.m.silu_c[:, :, 0:1].to_broadcast([P, KD, self.COLS]),
                           ALU.mult).then_inc(self.c["mod_product"], 1)

    def reduce(self, dve, i, slot):
        dve.wait_ge(self.c["mod_product"], self.product0 + i + 1)
        dve.wait_ge(self.c["mod_summed"], self.summed0 + i + 1)
        dve.tensor_reduce(self.acc[:], self.buf[slot][:].rearrange("p k n -> p n k"), AX_X,
                          ALU.add).then_inc(self.c["mod_reduced"], 1)

    def sum(self, pe, i):
        pe.wait_ge(self.c["mod_reduced"], self.reduced0 + i + 3)
        for q in range(2):
            last = pe.matmul(self.sums[:, bass.ds(2 * i + q, 1)],
                             self.acc[:, q * P:(q + 1) * P], self.m.ones[:, 0:1],
                             start=True, stop=True)
        last.then_inc(self.c["mod_summed"], 1)

    def finish(self, dve, coefs):
        n = 2 * self.pieces
        dve.wait_ge(self.c["mod_summed"], self.summed0 + self.pieces + 1)
        bias = self.m.col["b_mod"] + 48 * self.layer + self.first
        chunks = slice(self.first, self.first + n)
        done = self.c.take("mod_biased", 1)
        dve.tensor_tensor(self.m.mod[:, self.layer, chunks, 0], self.sums[:, 0:n],
                          self.m.vt[:, bias:bias + n], ALU.add).then_inc(self.c["mod_biased"], 1)
        dve.wait_ge(self.c["mod_biased"], done + 1)
        coefficients(self.c, self.m, dve, self.layer, coefs)


def coefficients(c, m, dve, layer, which):
    for j in which:
        what, gain = ((1, "g_pre_mix"), (2, "g_post_mix"), (4, "g_pre_ffn"), (5, "g_post_ffn"))[j]
        col = m.col[gain] + KD * layer
        dve.scalar_tensor_tensor(
            out=m.coef[:, layer, j, :], in0=m.mod[:, layer, 8 * what:8 * what + 8, 0],
            scalar=1.0 if j % 2 == 0 else 0.0, in1=m.vt[:, col:col + KD],
            op0=ALU.add, op1=ALU.mult).then_inc(c["coef"], 1)


def halves_parts(m, scale, shift, work=0, squares=8):
    def part(h):
        s = slice(h * HALF, (h + 1) * HALF)
        return dict(
            source=lambda k: m.x[:, k, s], work=lambda k: m.a[:, work + k, s],
            hi=lambda k: m.xn_hi[:, k, s], lo=lambda k: m.xn_lo[:, k, s],
            scale=scale, shift=shift, tiles=4, stat=m.ps[:, 4, 8 * h:8 * h + 8],
            turned=m.ps[:, 5, h * P:(h + 1) * P], bank=m.ps[:, 6 + h, :], small=4 * h,
            squares=[m.a[:, 16 + i, s] for i in range(squares)])
    return [part(0), part(1)]


def load_vectors(nc, c, m, ins):
    lists = [
        ("b_mod", ins["b_mod"].rearrange("l (k p) -> (l k) p", p=P)),
        ("c", ins["c"].rearrange("b (k p) -> (b k) p", p=P)),
        ("c_ctx", ins["c_ctx"].rearrange("(k p) -> k p", p=P)),
        ("g_pre_mix", ins["g_pre_mix"].rearrange("l (k p) -> (l k) p", p=P)),
        ("g_post_mix", ins["g_post_mix"].rearrange("l (k p) -> (l k) p", p=P)),
        ("g_pre_ffn", ins["g_pre_ffn"].rearrange("l (k p) -> (l k) p", p=P)),
        ("g_post_ffn", ins["g_post_ffn"].rearrange("l (k p) -> (l k) p", p=P)),
        ("b_pool", ins["b_pool"].rearrange("j g (k p) -> (j g k) p", p=P)),
        ("pool_scale", ins["pool_scale"].rearrange("j (k p) -> (j k) p", p=P)),
        ("g_q", ins["g_q"]), ("g_k", ins["g_k"]),
        ("norm1", ins["norm1_gain_2"].rearrange("j (k p) -> (j k) p", p=P)),
        ("norm2", ins["norm2_gain_2"].rearrange("j (k p) -> (j k) p", p=P)),
        ("final", ins["final_norm_gain_2"].rearrange("(k p) -> k p", p=P)),
        ("conv_w0", ins["conv_w"][0].rearrange("w (k p) -> (w k) p", p=P)),
        ("conv_w1", ins["conv_w"][1].rearrange("w (k p) -> (w k) p", p=P)),
        ("conv_b", ins["conv_b"].rearrange("l (k p) -> (l k) p", p=P)),
        ("lru_conv_w", ins["lru_conv_w_2"].rearrange("j w (k p) -> (j w k) p", p=P)),
        ("lru_conv_b", ins["lru_conv_b_2"].rearrange("j (k p) -> (j k) p", p=P)),
        ("gate_a_b", ins["lru_gate_a_b_2"].rearrange("j (k p) -> (j k) p", p=P)),
        ("gate_x_b", ins["lru_gate_x_b_2"].rearrange("j (k p) -> (j k) p", p=P)),
        ("lambda", ins["lru_lambda_2"].rearrange("j (k p) -> (j k) p", p=P)),
        ("lru_norm", ins["lru_norm_gain_2"].rearrange("j (k p) -> (j k) p", p=P)),
        ("ret_norm", ins["ret_norm_gain_2"].rearrange("j (k p) -> (j k) p", p=P)),
        ("ffn_w0", ins["ffn_conv_w_2"][0, 0].rearrange("(k p) -> k p", p=P)),
        ("ffn_w1", ins["ffn_conv_w_2"][0, 1].rearrange("(k p) -> k p", p=P)),
        ("ffn_w2", ins["ffn_conv_w_2"][0, 2].rearrange("(k p) -> k p", p=P)),
        ("ffn_b", ins["ffn_conv_b_2"].rearrange("j (k p) -> (j k) p", p=P)),
    ]
    fill, place = [], {}
    for name, ap in sorted(lists, key=lambda x: -x[1].shape[0]):
        n = ap.shape[0]
        tile = next((i for i, f in enumerate(fill) if f + n <= P), len(fill))
        if tile == len(fill):
            fill.append(0)
        place[name] = (tile, fill[tile], n)
        fill[tile] += n
    tiles = len(fill)
    m.vt = m.vec("vt", [P, tiles * P])
    m.col = {name: tile * P + at for name, (tile, at, n) in place.items()}
    m.ident = m.vec("ident", [P, P])
    m.mod = m.vec("mod", [P, 2, 48, 2])
    m.silu_c = m.vec("silu_c", [P, KD, 2])
    m.eps = m.vec("eps", [P, 1])
    m.ones = m.vec("ones", [P, 1])
    m.rms_sd = m.vec("rms_sd", [P, 96])
    m.rms_rs = m.vec("rms_rs", [P, 96])
    rms_row = m.vec("rms_row", [P, 3, P])
    m.rms_row = [rms_row[:, r, :] for r in range(3)]
    m.rms_rows = rms_row[:, 0, :]
    m.coef = m.vec("coef", [P, 2, 4, KD])
    m.coef_ctx = m.vec("coef_ctx", [P, KD])

    rows_in = m.at("vector_rows", YX, [P, tiles, P])
    x_rows = m.at("x_rows", A0, [P, TT, D])
    ctx_rows = m.at("ctx_rows", A0 + 16 * 4096, [P, 2, D])
    m.ctx_cm = m.at("ctx_cm", A0 + 21 * 4096, [P, KD, CTX])
    wm = m.at("w_mod_slots", XN, [P, 4, KD, HALF])
    x_tiles = ins["x"].rearrange("b (t p) d -> (b t) p d", p=P)
    ctx_tiles = ins["ctx"].rearrange("b (t p) d -> (b t) p d", p=P)
    w_mod = ins["w_mod"].rearrange("l (k p) n -> l p k n", p=P)
    mod_rows = m.at("mod_rows", YX + 8192, [2, 4 * HALF])
    groups = [(x_rows, t, g, m.x) for t in range(TT) for g in (0, 1)]
    groups += [(ctx_rows, t, g, m.ctx_cm) for t in range(2) for g in (0, 1)]

    with nc.Block() as block:
        @block.sync
        def _(sp):
            sp.dma_start(m.ident[:], ins["k_ident"]).then_inc(c["ident_in"], 16)
            for t in range(TT):
                sp.dma_start(x_rows[:, t, :], x_tiles[t]).then_inc(c["x_in"], 16)
            for t in range(2):
                sp.dma_start(ctx_rows[:, t, :], ctx_tiles[t]).then_inc(c["ctx_in"], 16)
            for s in range(4):
                sp.dma_start(wm[:, s], w_mod[0, :, :, s * HALF:(s + 1) * HALF]
                             ).then_inc(c[f"first_mod_in{s}"], 16)

        @block.gpsimd
        def _(pool):
            pool.memset(m.eps[:], EPS).then_inc(c["consts"], 1)
            pool.memset(m.ones[:], 1.0).then_inc(c["consts"], 1)
            for name in ("w_lo", "unit_done", "down_used", "at_exp", "at_summed", "mod_reduced"):
                pool.sem_inc(c[name], 2)
            for name in ("up_out", "at_max", "at_copied", "at_out_scaled", "mod_summed"):
                pool.sem_inc(c[name], 1)
            for name in ("at_lo", "at_used"):
                pool.sem_inc(c[name], PROBS)
            pool.sem_inc(c["at_added"], KEYS // P - 1)

        @block.tensor
        def _(pe):
            pe.wait_ge(c["ident_in"], 16)
            pe.wait_ge(c["rows_in"], 16 * len(lists))
            pe.wait_ge(c["consts"], 2)
            for s in range(tiles):
                last = pe.transpose(m.ps[:, s // 4, (s % 4) * P:(s % 4) * P + fill[s]],
                                    rows_in[0:fill[s], s, :], m.ident[0:fill[s], 0:fill[s]])
            last.then_inc(c["vt_turned"], 1)
            pe.wait_ge(c["x_in"], 16 * TT)
            for i, (src, t, g, dst) in enumerate(groups):
                if i == 2 * TT:
                    pe.wait_ge(c["ctx_in"], 32)
                if i >= 2:
                    pe.wait_ge(c["x_copied"], i - 1)
                for q in range(4):
                    k = 4 * g + q
                    last = pe.transpose(m.ps[:, 2 + i % 2, q * P:(q + 1) * P],
                                        src[:, t, k * P:(k + 1) * P], m.ident[:])
                last.then_inc(c["x_turned"], 1)
            pe.wait_ge(c["silu_c"], 2)
            for s in range(4):
                pe.wait_ge(c[f"first_mod_in{s}"], 16)
                for k in range(KD):
                    last = pe.matmul(m.ps[0:2, 4 + s, :], m.silu_c[:, k, :], wm[:, s, k, :],
                                     start=(k == 0), stop=(k == KD - 1))
                last.then_inc(c["first_mod_out"], 1)
            for s in range(4):
                pe.wait_ge(c["first_mod_rows"], s + 1)
                for q in range(4):
                    j = 4 * s + q
                    last = pe.transpose(m.ps[:, 0, 2 * j:2 * j + 2],
                                        mod_rows[0:2, j * P:(j + 1) * P], m.ident[0:2, 0:2])
            last.then_inc(c["first_mod_turned"], 1)

        @block.scalar
        def _(act):
            for name, ap in lists:
                tile, at, n = place[name]
                act.dma_start(rows_in[at:at + n, tile, :], ap).then_inc(c["rows_in"], 16)
            act.wait_ge(c["vt_copied"], tiles)
            for v, name in enumerate(("c", "c_ctx")):
                act.activation(m.silu_c[:, :, v], m.vt[:, m.col[name]:m.col[name] + KD],
                               ACT.Silu).then_inc(c["silu_c"], 1)
            for i, (src, t, g, dst) in enumerate(groups):
                act.wait_ge(c["x_turned"], i + 1)
                act.activation(dst[:, 4 * g:4 * g + 4, t * P:(t + 1) * P],
                               m.ps[:, 2 + i % 2, :].rearrange("p (q t) -> p q t", q=4),
                               ACT.Copy).then_inc(c["x_copied"], 1)
            for s in range(4):
                act.wait_ge(c["first_mod_out"], s + 1)
                act.activation(mod_rows[0:2, s * HALF:(s + 1) * HALF], m.ps[0:2, 4 + s, :],
                               ACT.Copy).then_inc(c["first_mod_rows"], 1)

        @block.vector
        def _(dve):
            dve.wait_ge(c["vt_turned"], 1)
            for s in range(tiles):
                dve.tensor_copy(m.vt[:, s * P:s * P + fill[s]],
                                m.ps[:, s // 4, (s % 4) * P:(s % 4) * P + fill[s]]
                                ).then_inc(c["vt_copied"], 1)
            dve.wait_ge(c["vt_copied"], tiles)
            dve.wait_ge(c["first_mod_turned"], 1)
            bias = m.vt[:, m.col["b_mod"]:m.col["b_mod"] + 16]
            dve.tensor_tensor(m.mod[:, 0, 0:16, :],
                              m.ps[:, 0, 0:32].rearrange("p (q v) -> p q v", v=2),
                              bias.unsqueeze(2).to_broadcast([P, 16, 2]),
                              ALU.add).then_inc(c["first_mod_done"], 1)
            dve.wait_ge(c["first_mod_done"], 1)
            coefficients(c, m, dve, 0, [0])
            dve.scalar_tensor_tensor(
                out=m.coef_ctx[:], in0=m.mod[:, 0, 8:16, 1], scalar=1.0,
                in1=m.vt[:, m.col["g_pre_mix"]:m.col["g_pre_mix"] + KD], op0=ALU.add,
                op1=ALU.mult).then_inc(c["coef"], 1)


def mod_col(m, layer, what, k, v=0):
    return m.mod[:, layer, 8 * what + k, v:v + 1]


def vcol(m, name, k):
    return m.vt[:, m.col[name] + k:m.col[name] + k + 1]


def weight_units(w, start, count):
    v = w.rearrange("(k p) n -> p k n", p=P)
    return lambda u: v[:, :, bass.ds(u * P + start, P)]


def unit_half(ws, m, pe, slot, half, pre=None):
    s = slice(half * HALF, (half + 1) * HALF)
    for k in range(KD):
        if pre:
            pre.ready(pe, half, k)
        last = ws.products(pe, slot, m.ps[:, 2 * slot + half, :], k, m.xn_hi[:, k, s],
                           m.xn_lo[:, k, s], k == 0, k == KD - 1)
    return last


def first_units(c, ws, m, pe, pre):
    pre.pe_sums(pe, 0)
    pre.pe_spread(pe, 0)
    ws.ready(pe, 0)
    unit_half(ws, m, pe, 0, 0, pre)
    pre.pe_sums(pe, 1)
    ws.ready(pe, 1)
    unit_half(ws, m, pe, 1, 0)
    pre.pe_spread(pe, 1)
    unit_half(ws, m, pe, 0, 1, pre).then_inc(c["unit_done"], 1)
    unit_half(ws, m, pe, 1, 1).then_inc(c["unit_done"], 1)
    for j in range(2, len(pre.parts)):
        pre.pe_sums(pe, j)
        pre.pe_spread(pe, j)


def project_stage(nc, c, m, name, pre, w, units, ctx_from, dest, ctx_dest):
    ws = WeightStream(c, m, units)
    f0 = c.take("project_copied", units)
    n_ctx = units - ctx_from
    cf0 = c.take("ctx_copied", n_ctx)
    src = weight_units(w, 0, units)
    loop = ctx_from // 2

    with nc.Block() as block:
        @block.sync
        def _(sp):
            with sp.Fori(0, units // 2) as i:
                for b in range(2):
                    ws.load(sp, 2 * i + b, b, src(2 * i + b))

        @block.gpsimd
        def _(pool):
            for b in range(2):
                ws.split(pool, b, 0, b, KD)
            pre.pool(pool)
            with pool.Fori(1, units // 2) as i:
                for b in range(2):
                    ws.split(pool, 2 * i + b, i, b, KD)

        @block.tensor
        def _(pe):
            first_units(c, ws, m, pe, pre)

            def unit(u, b, with_ctx):
                ws.ready(pe, u)
                pe.wait_ge(c["project_copied"], f0 + u - 1)
                for h in range(2):
                    last = unit_half(ws, m, pe, b, h)
                if with_ctx:
                    if u == ctx_from:
                        pre.ready(pe, 2)
                    else:
                        pe.wait_ge(c["ctx_copied"], cf0 + u - ctx_from)
                    for k in range(KD):
                        last = ws.products(pe, b, m.ps[:, 4, 0:CTX], k, m.xnc_hi[:, k, :],
                                           m.xnc_lo[:, k, :], k == 0, k == KD - 1)
                last.then_inc(c["unit_done"], 1)

            with pe.Fori(1, loop) as i:
                for b in range(2):
                    unit(2 * i + b, b, False)
            for u in range(ctx_from, units):
                unit(u, u % 2, True)

        @block.scalar
        def _(act):
            pre.act(act)

            def copy(u, b):
                ws.finished(act, u)
                stand_alone(act, c)
                act.activation(dest(u), m.ps[:, 2 * b:2 * b + 2, :].rearrange("p b t -> p (b t)"),
                               ACT.Copy).then_inc(c["project_copied"], 1)

            with act.Fori(0, loop) as i:
                for b in range(2):
                    copy(2 * i + b, b)
            for u in range(ctx_from, units):
                copy(u, u % 2)
                act.activation(ctx_dest(u), m.ps[:, 4, 0:CTX], ACT.Copy
                               ).then_inc(c["ctx_copied"], 1)

        @block.vector
        def _(dve):
            pre.dve(dve)


def ffn_up_stage(nc, c, m, name, pre, w, ff, conv_w, conv_b, causal, mod=None):
    ws = WeightStream(c, m, 2 * ff)
    out0 = c.take("up_out", ff)
    steps = 2 if causal else 1
    i0 = c.take("up_centre", steps * ff)
    s0 = c.take("up_side", 2 * steps * ff)
    act0 = c.take("up_act", ff)
    wv = w.rearrange("(k p) n -> p k n", p=P)
    work = m.at(f"{name}_work", YX, [P, 2, T])
    gate_work, value_work = work[:, 0, :], work[:, 1, :]
    banks = m.ps[:].rearrange("p b t -> p (b t)")
    gate_ps, value_ps = banks[:, 0:T], banks[:, T:2 * T]
    if causal:
        centre, sides = 2, [(slice(0, T - 2), slice(2, T), 0), (slice(0, T - 1), slice(1, T), 1)]
    else:
        centre, sides = 1, [(slice(0, T - 1), slice(1, T), 0), (slice(1, T), slice(0, T - 1), 2)]

    def chunks(eng, body):
        with eng.Fori(0, ff // 2 - 1) as i:
            body(2 * i + 1, i, 1)
            body(2 * i + 2, i + 1, 0)
        body(ff - 1, ff // 2 - 1, 1)

    with nc.Block() as block:
        @block.sync
        def _(sp):
            def chunk(j, pair, odd):
                for b in range(2):
                    ws.load(sp, 2 * j + b, b, wv[:, :, bass.ds(j * P + b * ff * P, P)])
                if mod:
                    mod.load(sp, j + 2, odd)

            for b in range(2):
                ws.load(sp, b, b, wv[:, :, b * ff * P:b * ff * P + P])
            if mod:
                for i in range(3):
                    mod.load(sp, i, i % 2)
            chunks(sp, chunk)

        @block.gpsimd
        def _(pool):
            for b in range(2):
                ws.split(pool, b, 0, b, KD)
            pre.pool(pool)

            def chunk(j, pair, odd):
                for b in range(2):
                    ws.split(pool, 2 * j + b, j, b, KD)
                if mod:
                    mod.product(pool, pair + 1, odd)

            if mod:
                for i in range(3):
                    mod.product(pool, i // 2, i % 2)
            chunks(pool, chunk)

        @block.tensor
        def _(pe):
            first_units(c, ws, m, pe, pre)
            if mod:
                for i in range(2):
                    mod.sum(pe, i)

            def chunk(j, pair, odd):
                for b in range(2):
                    ws.ready(pe, 2 * j + b)
                    if causal or b == 0:
                        pe.wait_ge(c["up_side"], 2 * steps * j + s0 - 2 * steps + 2 * b + 2)
                    else:
                        pe.wait_ge(c["up_out"], out0 + j + 1)
                    for h in range(2):
                        last = unit_half(ws, m, pe, b, h)
                    last.then_inc(c["unit_done"], 1)
                if mod:
                    mod.sum(pe, j + 1)

            chunks(pe, chunk)
            if mod:
                mod.sum(pe, ff + 1)

        @block.scalar
        def _(act):
            pre.act(act)

            def chunk(j, pair=None, odd=None):
                ws.finished(act, 2 * j)
                act.wait_ge(c["up_out"], out0 + j + 1)
                stand_alone(act, c)
                act.activation(gate_work, gate_ps, ACT.Identity, bias=conv_b(j),
                               scale=conv_w(centre, j)).then_inc(c["up_centre"], 1)
                if causal:
                    ws.finished(act, 2 * j + 1)
                    stand_alone(act, c)
                    act.activation(value_work, value_ps, ACT.Identity, bias=conv_b(j + ff),
                                   scale=conv_w(centre, j + ff)).then_inc(c["up_centre"], 1)
                act.wait_ge(c["up_side"], 2 * steps * j + s0 + 2)
                act.activation(gate_work, gate_work, ACT.Gelu_apprx_tanh if causal else ACT.Silu
                               ).then_inc(c["up_act"], 1)

            chunk(0)
            chunks(act, chunk)

        @block.vector
        def _(dve):
            pre.dve(dve)

            def neighbours(j, part, target, source, chunk):
                dve.wait_ge(c["up_centre"], steps * j + i0 + part + 1)
                for n, (src, dst, tap) in enumerate(sides):
                    if n:
                        dve.wait_ge(c["up_side"], 2 * steps * j + s0 + 2 * part + 1)
                    last = dve.scalar_tensor_tensor(
                        out=target[:, dst], in0=source[:, src], scalar=conv_w(tap, chunk),
                        in1=target[:, dst], op0=ALU.mult, op1=ALU.add)
                    last.then_inc(c["up_side"], 1)

            def chunk(j, pair=None, odd=None):
                neighbours(j, 0, gate_work, gate_ps, j)
                if causal:
                    neighbours(j, 1, value_work, value_ps, j + ff)
                    dve.wait_ge(c["up_side"], 2 * steps * j + s0 + 4)
                dve.wait_ge(c["up_act"], act0 + j + 1)
                if causal:
                    dve.tensor_tensor(m.a[:, bass.ds(j, 1), :].rearrange("p o t -> p (o t)"),
                                      gate_work, value_work, ALU.mult
                                      ).then_inc(c["up_out"], 1)
                else:
                    ws.finished(dve, 2 * j + 1)
                    dve.tensor_tensor(m.a[:, bass.ds(j, 1), :].rearrange("p o t -> p (o t)"),
                                      gate_work, value_ps, ALU.mult
                                      ).then_inc(c["up_out"], 1)
                if mod and pair is not None:
                    mod.reduce(dve, j + 2, odd)

            if mod:
                for i in range(3):
                    mod.reduce(dve, i, i % 2)
            chunk(0)
            chunks(dve, chunk)
            if mod:
                mod.finish(dve, range(4))


def down_stage(nc, c, m, name, chunks, groups, source, kmap, evac, post, x_dram, x_load, x_store):
    ng = len(groups)
    units = 2 * KD * ng
    ws = WeightStream(c, m, units)
    h0, l0 = c.take("down_hi", 2 * chunks), c.take("down_lo", 2 * chunks)
    f0 = c.take("down_used", 2 * KD)
    xl0 = c.take("x_loaded", 32 if x_load else 0)
    xs0 = c.take("x_stored", 32 if x_store else 0)
    rx0 = c.take("x_scaled", 2 * KD if post else 0)
    nx0 = c.take("x_new", 2 * KD)
    pairs = KD // 2
    per = 2 * ng

    def y(half, n):
        return m.yx[:, n, :] if half == 0 else m.a[:, n, 0:HALF]

    def x(half, k):
        return m.x[:, k, half * HALF:(half + 1) * HALF]

    def slot(half, k):
        return m.ring[:, (half * chunks + k) % 32, :]

    def lo(half, k):
        return m.a_lo[k // 8][:, k % 8, half * HALF:(half + 1) * HALF]

    def full(half, k):
        return m.a[:, k, half * HALF:(half + 1) * HALF]

    rms = []
    if post:
        for h in range(2):
            squares = [m.a[:, 16 + i, h * HALF:(h + 1) * HALF] for i in range(6)]
            rms.append(RootMeanSquare(c, m, f"{name}{h}", 1, KD, 4, D,
                                      (lambda hh: lambda k: y(hh, k))(h), squares,
                                      m.ps[:, 4, 8 * h:8 * h + 8], m.ps[:, 5, h * P:(h + 1) * P],
                                      [m.ps[:, 6 + h, :]], 4 * h))

    with nc.Block() as block:
        @block.sync
        def _(sp):
            def pair(half, i):
                for b in range(2):
                    for g in range(ng):
                        n = b * ng + g
                        ws.load(sp, per * i + half * KD * ng + n, n % 2, source(i, b, g))

            with sp.Fori(0, pairs) as i:
                pair(0, i)
            pair(1, 0)
            if x_load:
                ws.finished(sp, units // 2 - 1)
                sp.dma_start(m.x[:, :, 0:HALF], x_dram[:, :, 0:HALF]).then_inc(c["x_loaded"], 16)
            with sp.Fori(1, pairs) as i:
                pair(1, i)
            if x_load:
                ws.finished(sp, units - 1)
                sp.wait_ge(c["x_loaded"], xl0 + 16)
                sp.dma_start(m.x[:, :, HALF:T], x_dram[:, :, HALF:T]).then_inc(c["x_loaded"], 16)
            if x_store:
                for h in range(2):
                    if x_load:
                        sp.wait_ge(c["x_loaded"], xl0 + 32)
                    sp.wait_ge(c["x_new"], nx0 + (h + 1) * KD)
                    s = slice(h * HALF, (h + 1) * HALF)
                    sp.dma_start(x_dram[:, :, s], m.x[:, :, s]).then_inc(c["x_stored"], 16)
                sp.wait_ge(c["x_stored"], xs0 + 32)

        @block.gpsimd
        def _(pool):
            def pair(half, i):
                for b in range(2):
                    for g in range(ng):
                        n = b * ng + g
                        ws.split(pool, per * i + half * KD * ng + n,
                                 ng * i + half * KD * ng // 2 + n // 2, n % 2, groups[g])

            for half in range(2):
                with pool.Fori(0, pairs) as i:
                    pair(half, i)

        @block.tensor
        def _(pe):
            def pair(half, i, waits):
                for b in range(2):
                    pe.wait_ge(c["down_used"], 2 * i + f0 + half * KD + b + 1)
                    k = 0
                    first = kmap(i, b)
                    for g in range(ng):
                        n = b * ng + g
                        ws.ready(pe, per * i + half * KD * ng + n)
                        for q in range(groups[g]):
                            kk = first + k
                            if waits:
                                pe.wait_ge(c["down_lo"], l0 + half * chunks + kk + 1)
                            last = ws.products(pe, n % 2, m.ps[:, b, :], q, slot(half, kk),
                                               lo(half, kk), k == 0, k == sum(groups) - 1)
                            k += 1
                        last.then_inc(c["unit_done"], 1)

            looped = sum(groups) == chunks
            pair(0, 0, True)
            if looped:
                with pe.Fori(1, pairs) as i:
                    pair(0, i, False)
            else:
                for i in range(1, pairs):
                    pair(0, i, True)
            pair(1, 0, True)
            if post:
                rms[0].pe_sums(pe)
            pair(1, 1, not looped)
            if post:
                rms[0].pe_turn(pe)
            pair(1, 2, not looped)
            if post:
                rms[0].pe_broadcast(pe, 0)
            pair(1, 3, not looped)
            if post:
                rms[1].pe_sums(pe)
                rms[1].pe_turn(pe)
                rms[1].pe_broadcast(pe, 0)

        @block.scalar
        def _(act):
            def splits(half):
                for k in range(chunks):
                    if half and chunks + k >= 32:
                        ws.finished(act, units // 2 - 1)
                    act.activation(slot(half, k), full(half, k), ACT.Copy
                                   ).then_inc(c["down_hi"], 1)

            def copies(half, i):
                for b in range(2):
                    ws.finished(act, per * i + half * KD * ng + b * ng + ng - 1)
                    stand_alone(act, c)
                    if half == 0:
                        dst = m.yx[:, bass.ds(2 * i + b, 1), :].rearrange("p o t -> p (o t)")
                    else:
                        dst = y(1, 2 * i + b)
                    if evac is None:
                        act.activation(dst, m.ps[:, b, :], ACT.Copy).then_inc(c["down_used"], 1)
                    else:
                        scale, bias = evac
                        act.activation(dst, m.ps[:, b, :], ACT.Identity, bias=bias(2 * i + b),
                                       scale=scale(2 * i + b)).then_inc(c["down_used"], 1)

            splits(0)
            with act.Fori(0, pairs) as i:
                copies(0, i)
            splits(1)
            act.wait_ge(c["down_used"], f0 + KD + 2)
            ws.finished(act, units // 2 - 1)
            if post:
                rms[0].act_squares(act)
            copies(1, 0)
            if post:
                rms[0].act_root(act)
            for i in range(1, pairs):
                copies(1, i)
            if post:
                act.wait_ge(c["down_used"], f0 + 2 * KD + 2)
                ws.finished(act, units - 1)
                rms[1].act_squares(act)
                rms[1].act_root(act)

        @block.vector
        def _(dve):
            for half in range(2):
                for k in range(chunks):
                    dve.wait_ge(c["down_hi"], h0 + half * chunks + k + 1)
                    dve.tensor_tensor(lo(half, k), full(half, k), slot(half, k).bitcast(F32),
                                      ALU.subtract).then_inc(c["down_lo"], 1)
            for half in range(2):
                if post:
                    rms[half].dve_inverse(dve)
                    rms[half].dve_row(dve)
                    bank = rms[half].ready(dve, 0)
                    for k in range(KD):
                        dve.tensor_tensor(y(half, k), y(half, k), bank, ALU.mult
                                          ).then_inc(c["x_scaled"], 1)
                else:
                    dve.wait_ge(c["down_used"], f0 + (half + 1) * KD + 2)
                if x_load:
                    dve.wait_ge(c["x_loaded"], xl0 + 16 * (half + 1))
                for k in range(KD):
                    if post:
                        dve.wait_ge(c["x_scaled"], rx0 + half * KD + k + 1)
                        dve.scalar_tensor_tensor(
                            out=x(half, k), in0=y(half, k), scalar=post(k), in1=x(half, k),
                            op0=ALU.mult, op1=ALU.add).then_inc(c["x_new"], 1)
                    else:
                        dve.tensor_tensor(x(half, k), y(half, k), x(half, k), ALU.add
                                          ).then_inc(c["x_new"], 1)


def two(ap, n=2):
    return ap.rearrange("p (a t) -> p a t", a=n)


def attention_memory(m):
    m.kh = m.at("k_hi", XN, [P, KV, KEYS], F32R)
    m.kl = m.at("k_lo", XN + 10240, [P, KV, KEYS], F32R)
    m.vh = m.at("v_hi", XN + 20480, [P, KEYS // P, KV * P], F32R)
    m.vl = m.at("v_lo", XN + 30720, [P, KEYS // P, KV * P], F32R)
    m.qh = m.at("q_hi", XN + 40960, [P, 2, HALF], F32R)
    m.ql = m.at("q_lo", XN + 45056, [P, 2, HALF], F32R)
    m.ph = m.at("probs_hi", XN + 49152, [P, PROBS, HALF], F32R)
    m.neg_row = m.at("negative_maxima", XN + 59392, [1, 2, HALF], F32R)
    m.ones_row = m.at("ones_row", XN + 63488, [1, P], F32R)
    m.pl = m.at("probs_lo", W_RAW, [P, PROBS, HALF], F32R)
    m.probs = m.at("probs", W_RAW + 10240, [P, PROBS, HALF])
    m.added = m.at("probs_added", W_RAW + 20480, [P, 2, HALF])
    m.kv_raw = m.at("kv_raw", A0 + 16 * 4096, [P, 2 * KV, KEYS])
    m.mod_buf = [m.at(f"mod_buf{s}", A0 + (16 + 2 * s) * 4096, [P, KD, 2 * P]) for s in (0, 1)]


def rotate_stage(nc, c, m, ins):
    table = m.at("rope_tables", W_RAW, [P, 6, T])
    cos, sin = table[:, 0, :], table[:, 1, :]
    tmp = m.at("rope_tmp", YX, [P, 4, HALF])
    direct, swapped = tmp[:, 0:2, :], tmp[:, 2:4, :]
    sq = m.at("rope_squares", YX + 8192, [P, 3, HALF])
    perm = m.at("rope_perm", YX + 8192 + 6144, [P, P])
    items = []
    for h in range(HEADS):
        for half in range(2):
            s = slice(half * HALF, (half + 1) * HALF)
            items.append(("q", h, s, m.a[:, h, s]))
    for h in range(KV):
        for half in range(2):
            s = slice(half * HALF, (half + 1) * HALF)
            items.append(("k", h, s, m.kv_raw[:, h, CTX + half * HALF:CTX + (half + 1) * HALF]))
    items.append(("ctx", 0, None, m.kv_raw[:, 0:KV, 0:CTX]))
    n_rot = len(items) - 1
    n_k = 2 * KV + 1
    rms = RootMeanSquare(c, m, "qk", len(items), 1, 4, P, lambda i: items[i][3],
                         [sq[:, i, :] for i in range(3)], m.ps[:, 4, :], m.ps[:, 5, :],
                         [m.ps[:, 6, :], m.ps[:, 7, :]], 0)
    sw0 = c.take("rope_swapped", n_rot)
    dir0 = c.take("rope_direct", n_rot)
    sin0 = c.take("rope_sin", n_rot)
    sum0 = c.take("rope_sum", n_rot)
    out0 = c.take("rope_out", len(items))
    kh0, kl0 = c.take("rope_k_hi", n_k), c.take("rope_k_lo", n_k)
    vt0, vh0, vl0 = c.take("v_turned", 5), c.take("v_hi_done", 5), c.take("v_lo_done", 5)

    with nc.Block() as block:
        @block.sync
        def _(sp):
            sp.dma_start(perm[:], ins["k_perm1"]).then_inc(c["rope_perm_in"], 16)
            sp.dma_start(cos, ins["k_cos1"]).then_inc(c["rope_in"], 16)
            sp.dma_start(sin, ins["k_sin1"]).then_inc(c["rope_in"], 16)

        @block.tensor
        def _(pe):
            pe.wait_ge(c["rope_perm_in"], 16)
            for i, name in enumerate(("g_q", "g_k")):
                last = pe.matmul(m.ps[:, 3, i:i + 1], perm[:], vcol(m, name, 0),
                                 start=True, stop=True)
            last.then_inc(c["gains_swapped"], 1)
            rms.pe_sums(pe)
            rms.pe_turn(pe)
            pe.wait_ge(c["gains_copied"], 1)
            for g in range(5):
                if g >= 2:
                    pe.wait_ge(c["v_lo_done"], vl0 + g - 1)
                for q in range(4):
                    kt, v = 2 * g + q // 2, q % 2
                    last = pe.transpose(m.ps[:, 2 + g % 2, q * P:(q + 1) * P],
                                        m.kv_raw[:, KV + v, kt * P:(kt + 1) * P], m.ident[:])
                last.then_inc(c["v_turned"], 1)
            for g, (kind, h, s, src) in enumerate(items):
                if kind != "ctx":
                    if g >= 2:
                        pe.wait_ge(c["rope_sin"], sin0 + g - 1)
                    pe.matmul(m.ps[:, g % 2, :], perm[:], src, start=True, stop=True
                              ).then_inc(c["rope_swapped"], 1)
                rms.pe_broadcast(pe, g)

        @block.scalar
        def _(act):
            rms.act_squares(act)
            rms.act_root(act)
            for g in range(5):
                act.wait_ge(c["v_turned"], vt0 + g + 1)
                act.activation(m.vh[:, 2 * g:2 * g + 2, :], two(m.ps[:, 2 + g % 2, :]), ACT.Copy
                               ).then_inc(c["v_hi_done"], 1)
            for i in range(n_k):
                g = 2 * HEADS + i
                act.wait_ge(c["rope_out"], out0 + g + 1)
                kind, h, s, src = items[g]
                if kind == "k":
                    dst = m.kh[:, h, CTX + s.start:CTX + s.stop]
                    act.activation(dst, direct[:, g % 2, :], ACT.Copy
                                   ).then_inc(c["rope_k_hi"], 1)
                else:
                    act.activation(m.kh[:, :, 0:CTX], two(direct[:, g % 2, :]), ACT.Copy
                                   ).then_inc(c["rope_k_hi"], 1)

        @block.gpsimd
        def _(pool):
            pool.wait_ge(c["rope_tables"], 4)
            for g, (kind, h, s, src) in enumerate(items[:n_rot]):
                if g >= 2:
                    pool.wait_ge(c["rope_out"], out0 + g - 1)
                if g >= 2 * HEADS + 2:
                    pool.wait_ge(c["rope_k_lo"], kl0 + g - 2 * HEADS - 1)
                which = 2 if kind == "q" else 4
                pool.tensor_tensor(direct[:, g % 2, :], src, table[:, which, s], ALU.mult
                                   ).then_inc(c["rope_direct"], 1)

        @block.vector
        def _(dve):
            dve.wait_ge(c["gains_swapped"], 1)
            dve.tensor_copy(m.gains_sw[:], m.ps[:, 3, 0:2]).then_inc(c["gains_copied"], 1)
            dve.wait_ge(c["rope_in"], 32)
            dve.wait_ge(c["gains_copied"], 1)
            for i, name in enumerate(("g_q", "g_k")):
                dve.tensor_scalar(table[:, 2 + 2 * i, :], cos, vcol(m, name, 0), None, ALU.mult
                                  ).then_inc(c["rope_tables"], 1)
                dve.tensor_scalar(table[:, 3 + 2 * i, :], sin, m.gains_sw[:, i:i + 1], None,
                                  ALU.mult).then_inc(c["rope_tables"], 1)
            dve.wait_ge(c["rope_tables"], 4)
            rms.dve_inverse(dve)
            rms.dve_row(dve)
            for g in range(5):
                dve.wait_ge(c["v_hi_done"], vh0 + g + 1)
                dve.tensor_tensor(m.vl[:, 2 * g:2 * g + 2, :], two(m.ps[:, 2 + g % 2, :]),
                                  m.vh[:, 2 * g:2 * g + 2, :].bitcast(F32), ALU.subtract
                                  ).then_inc(c["v_lo_done"], 1)
            for g, (kind, h, s, src) in enumerate(items):
                if kind == "ctx":
                    bank = rms.ready(dve, g)
                    dve.wait_ge(c["rope_k_lo"], kl0 + g - 2 * HEADS - 1)
                    dve.scalar_tensor_tensor(out=two(direct[:, g % 2, :]), in0=src,
                                             scalar=vcol(m, "g_k", 0), in1=two(bank),
                                             op0=ALU.mult, op1=ALU.mult
                                             ).then_inc(c["rope_out"], 1)
                else:
                    which = 3 if kind == "q" else 5
                    dve.wait_ge(c["rope_swapped"], sw0 + g + 1)
                    dve.tensor_tensor(swapped[:, g % 2, :], m.ps[:, g % 2, :],
                                      table[:, which, s], ALU.mult).then_inc(c["rope_sin"], 1)
                    dve.wait_ge(c["rope_sin"], sin0 + g + 1)
                    dve.wait_ge(c["rope_direct"], dir0 + g + 1)
                    dve.tensor_tensor(swapped[:, g % 2, :], direct[:, g % 2, :],
                                      swapped[:, g % 2, :], ALU.add).then_inc(c["rope_sum"], 1)
                    bank = rms.ready(dve, g)
                    dve.wait_ge(c["rope_sum"], sum0 + g + 1)
                    dst = src if kind == "q" else direct[:, g % 2, :]
                    dve.tensor_tensor(dst, swapped[:, g % 2, :], bank, ALU.mult
                                      ).then_inc(c["rope_out"], 1)
                if kind != "q":
                    i = g - 2 * HEADS
                    dve.wait_ge(c["rope_k_hi"], kh0 + i + 1)
                    if kind == "k":
                        cols = slice(CTX + s.start, CTX + s.stop)
                        dve.tensor_tensor(m.kl[:, h, cols], direct[:, g % 2, :],
                                          m.kh[:, h, cols].bitcast(F32), ALU.subtract
                                          ).then_inc(c["rope_k_lo"], 1)
                    else:
                        dve.tensor_tensor(m.kl[:, :, 0:CTX], two(direct[:, g % 2, :]),
                                          m.kh[:, :, 0:CTX].bitcast(F32), ALU.subtract
                                          ).then_inc(c["rope_k_lo"], 1)
                dve.wait_ge(c["rope_out"], out0 + g + 1)
                dve.sem_inc(c["rms_broadcast_used"], 1)


def attention_stage(nc, c, m, mod):
    flat = m.ps[:].rearrange("p b t -> p (b t)")
    kt_n = KEYS // P
    adds = kt_n - 1
    lag = 3
    max_at = {0: 0, 2: 1, 4: 2, 6: 3}
    out_ps, scale_ps = m.ps[:, 5, :], m.ps[:, 6, :]
    sum_ps, turned_ps = m.ps[:, 7, 64:68], m.ps[0:4, 7, 128:256]

    def following(g, h, half):
        return (g, h, 1) if half == 0 else (g, h + 1, 0)

    def number(item):
        g, h, half = item
        return h * 2 + (8 * g + half)

    def head(item, ap):
        g, h, half = item
        return ap[:, bass.ds(h + GROUP * g, 1), half * HALF:(half + 1) * HALF].rearrange(
            "p o t -> p (o t)")

    def all_items(eng, body, last_of_all):
        for g in range(KV):
            prev_head = (g, -1, 1) if g == 0 else (0, GROUP - 1, 1)
            body((g, 0, 0), prev_head if g else None, (g, 0, 1))
            body((g, 0, 1), (g, 0, 0), (g, 1, 0))
            with eng.Fori(1, GROUP - 1) as h:
                body((g, h, 0), (g, h - 1, 1), (g, h, 1))
                body((g, h, 1), (g, h, 0), (g, h + 1, 0))
            h = GROUP - 1
            body((g, h, 0), (g, h - 1, 1), (g, h, 1))
            body((g, h, 1), (g, h, 0), (g + 1, 0, 0) if g + 1 < KV else None)
        last_of_all((KV - 1, GROUP - 1, 1))

    with nc.Block() as block:
        @block.sync
        def _(sp):
            def body(item, prev, following):
                mod.load(sp, number(item), item[2])

            all_items(sp, body, lambda item: None)

        @block.tensor
        def _(pe):
            def scores(item, kt):
                g, h, half = item
                n = number(item)
                out = m.ps[:, 3 + kt % 2, :]
                pe.wait_ge(c["at_exp"], n * kt_n + (kt + 1))
                if kt == 0:
                    pe.wait_ge(c["at_q_lo"], n + 1)
                ks = slice(kt * P, (kt + 1) * P)
                pe.matmul(out, m.kh[:, g, ks], m.qh[:, half, :], start=True, stop=False)
                pe.matmul(out, m.kh[:, g, ks], m.ql[:, half, :], start=False, stop=False)
                pe.matmul(out, m.kl[:, g, ks], m.qh[:, half, :], start=False, stop=False)
                if kt == 0:
                    pe.wait_ge(c["at_row"], n + 1)
                pe.matmul(out, m.ones_row[:], m.neg_row[:, half, :], start=False, stop=True
                          ).then_inc(c["at_scores"], 1)

            def maxima(item, qi):
                g, h, half = item
                n = number(item)
                if qi == 0:
                    pe.wait_ge(c["at_q_hi"], n + 1)
                pe.wait_ge(c["at_max"], n * 4 + (qi + 1))
                for k0, k1 in ((0, 512), (512, 1024), (1024, 1280)):
                    last = pe.matmul(flat[:, k0:k1], m.qh[:, half, qi * P:(qi + 1) * P],
                                     m.kh[:, g, k0:k1], start=True, stop=True)
                last.then_inc(c["at_max_scores"], 1)

            def turn_maxima(item):
                pe.wait_ge(c["at_max"], number(item) * 4 + 5)
                for qi in range(4):
                    last = pe.transpose(m.ps[0:1, 0, qi * P:(qi + 1) * P],
                                        m.at_max[:, qi:qi + 1], m.ident[:])
                last.then_inc(c["at_max_turned"], 1)

            def values(item, kt):
                g, h, half = item
                n = number(item)
                pe.wait_ge(c["at_lo"], n * kt_n + (kt + 1 + PROBS))
                if kt == 0:
                    pe.wait_ge(c["at_copied"], n + 1)
                vs, slot = slice(g * P, (g + 1) * P), kt % PROBS
                pe.matmul(out_ps, m.vh[:, kt, vs], m.ph[:, slot, :], start=(kt == 0), stop=False)
                pe.matmul(out_ps, m.vh[:, kt, vs], m.pl[:, slot, :], start=False, stop=False)
                pe.matmul(out_ps, m.vl[:, kt, vs], m.ph[:, slot, :], start=False,
                          stop=(kt == kt_n - 1)).then_inc(c["at_used"], 1)

            def sums(item):
                pe.wait_ge(c["at_added"], number(item) * adds + 2 * adds)
                for qi in range(4):
                    last = pe.matmul(sum_ps[:, qi:qi + 1],
                                     m.added[:, item[2], qi * P:(qi + 1) * P], m.ones[:, 0:1],
                                     start=True, stop=True)
                last.then_inc(c["at_summed"], 1)

            def turn_inverse(item):
                pe.wait_ge(c["at_inverse"], number(item) + 1)
                pe.transpose(turned_ps, m.at_inv[:], m.ident[:]).then_inc(c["at_inv_turned"], 1)

            def broadcast(item):
                n = number(item)
                pe.wait_ge(c["at_inv_rows"], n + 1)
                pe.wait_ge(c["at_out_scaled"], n + 1)
                for qi in range(4):
                    last = pe.matmul(scale_ps[:, qi * P:(qi + 1) * P],
                                     m.ident[0:4, qi:qi + 1].to_broadcast([4, P]),
                                     m.at_rows[0:4, :], start=True, stop=True)
                last.then_inc(c["at_scales"], 1)

            def body(item, prev, following):
                for kt in range(kt_n):
                    scores(item, kt)
                    if kt >= lag:
                        values(item, kt - lag)
                    elif prev:
                        values(prev, kt_n - lag + kt)
                    if following and kt in max_at:
                        maxima(following, max_at[kt])
                    if following and kt == 8:
                        turn_maxima(following)
                    if prev and kt == 1:
                        mod.sum(pe, number(prev))
                    if prev and kt == 3:
                        sums(prev)
                    if prev and kt == 5:
                        turn_inverse(prev)
                    if prev and kt == 8:
                        broadcast(prev)

            def end(item):
                for kt in range(kt_n - lag, kt_n):
                    values(item, kt)
                mod.sum(pe, number(item))
                sums(item)
                turn_inverse(item)
                broadcast(item)

            pe.wait_ge(c["at_ones"], 1)
            for qi in range(4):
                maxima((0, 0, 0), qi)
            turn_maxima((0, 0, 0))
            all_items(pe, body, end)

        @block.scalar
        def _(act):
            def q(item):
                act.activation(m.qh[:, item[2], :], head(item, m.a), ACT.Copy
                               ).then_inc(c["at_q_hi"], 1)

            def exps(item, kt):
                n, slot = number(item), kt % PROBS
                act.wait_ge(c["at_scores"], n * kt_n + (kt + 1))
                act.wait_ge(c["at_lo"], n * kt_n + (kt + 1))
                before = kt + 5 if kt < PROBS else adds + max(kt - PROBS, 1)
                act.wait_ge(c["at_added"], n * adds + before)
                act.activation(m.probs[:, slot, :], m.ps[:, 3 + kt % 2, :], ACT.Exp,
                               scale=ATT_SCALE).then_inc(c["at_exp"], 1)

            def highs(item, kt):
                n, slot = number(item), kt % PROBS
                act.wait_ge(c["at_used"], n * kt_n + (kt + 1))
                act.wait_ge(c["at_exp"], n * kt_n + (kt + 3))
                act.activation(m.ph[:, slot, :], m.probs[:, slot, :], ACT.Copy
                               ).then_inc(c["at_hi"], 1)

            def negated(item):
                act.wait_ge(c["at_max_turned"], number(item) + 1)
                act.activation(m.neg_row[:, item[2], :], m.ps[0:1, 0, :], ACT.Copy, scale=-1.0
                               ).then_inc(c["at_row"], 1)

            def copy(item):
                act.wait_ge(c["at_used"], number(item) * kt_n + (kt_n + PROBS))
                stand_alone(act, c)
                act.activation(head(item, m.a), out_ps, ACT.Copy).then_inc(c["at_copied"], 1)

            def body(item, prev, following):
                for kt in range(kt_n):
                    if following and kt == 0:
                        q(following)
                    exps(item, kt)
                    highs(item, kt)
                    if prev and kt == lag - 1:
                        copy(prev)
                    if following and kt == 8:
                        negated(following)

            act.activation(m.ones_row[:], m.ident[0:1, :], ACT.Identity, bias=m.ones[0:1, 0:1],
                           scale=0.0).then_inc(c["at_ones"], 1)
            q((0, 0, 0))
            negated((0, 0, 0))
            all_items(act, body, copy)

        @block.vector
        def _(dve):
            def q(item):
                dve.wait_ge(c["at_q_hi"], number(item) + 1)
                dve.tensor_tensor(m.ql[:, item[2], :], head(item, m.a),
                                  m.qh[:, item[2], :].bitcast(F32), ALU.subtract
                                  ).then_inc(c["at_q_lo"], 1)

            def maxima(item, qi):
                dve.wait_ge(c["at_max_scores"], number(item) * 4 + (qi + 1))
                dve.tensor_reduce(m.at_max[:, qi:qi + 1], flat[:, 0:KEYS], AX_X, ALU.max
                                  ).then_inc(c["at_max"], 1)

            def lows(item, kt):
                n, slot = number(item), kt % PROBS
                dve.wait_ge(c["at_hi"], n * kt_n + (kt + 1))
                dve.tensor_tensor(m.pl[:, slot, :], m.probs[:, slot, :],
                                  m.ph[:, slot, :].bitcast(F32), ALU.subtract
                                  ).then_inc(c["at_lo"], 1)

            def inverse(item):
                dve.wait_ge(c["at_summed"], number(item) + 3)
                dve.reciprocal(m.at_inv[:], sum_ps).then_inc(c["at_inverse"], 1)

            def rows(item):
                dve.wait_ge(c["at_inv_turned"], number(item) + 1)
                dve.tensor_copy(m.at_rows[0:4, :], turned_ps).then_inc(c["at_inv_rows"], 1)

            def scaled(item):
                dve.wait_ge(c["at_scales"], number(item) + 1)
                dve.wait_ge(c["at_copied"], number(item) + 2)
                dve.tensor_tensor(head(item, m.a), head(item, m.a), scale_ps, ALU.mult
                                  ).then_inc(c["at_out_scaled"], 1)

            def body(item, prev, following):
                for kt in range(kt_n):
                    if following and kt == 0:
                        q(following)
                    if prev and kt == 4:
                        inverse(prev)
                    if prev and kt == 6:
                        rows(prev)
                    lows(item, kt)
                    if following and kt in max_at:
                        maxima(following, max_at[kt])
                    if kt == 7:
                        mod.reduce(dve, number(item), item[2])
                    if prev and kt == 9:
                        scaled(prev)

            def end(item):
                inverse(item)
                rows(item)
                scaled(item)

            q((0, 0, 0))
            for qi in range(4):
                maxima((0, 0, 0), qi)
            all_items(dve, body, end)
            mod.finish(dve, [1, 2, 3])

        @block.gpsimd
        def _(pool):
            def body(item, prev, following):
                g, h, half = item
                n = number(item)
                for kt in range(1, kt_n):
                    pool.wait_ge(c["at_exp"], n * kt_n + (kt + 3))
                    if kt == 1:
                        pool.wait_ge(c["at_summed"], n + 1)
                        first = m.probs[:, 0, :]
                    else:
                        pool.wait_ge(c["at_added"], n * adds + (adds + kt - 1))
                        first = m.added[:, half, :]
                    pool.tensor_tensor(m.added[:, half, :], first, m.probs[:, kt % PROBS, :],
                                       ALU.add).then_inc(c["at_added"], 1)
                    if kt == 1:
                        mod.product(pool, h + GROUP * g, half)

            all_items(pool, body, lambda item: None)


def pool_stage(nc, c, m, ins):
    pad = 8
    wide = T + 2 * pad
    h_pad = m.at("pool_h", XN, [P, KD, wide])
    sums = m.at("pool_sums", W_RAW, [P, 4, wide])
    inv = m.at("pool_inverse_counts", YX, [P, 4, T])
    parts = halves_parts(m, lambda k: m.coef[:, 1, 0, k:k + 1], lambda k: mod_col(m, 1, 0, k))
    for h, p in enumerate(parts):
        p["work"] = (lambda hh: lambda k: h_pad[:, k, pad + hh * HALF:pad + (hh + 1) * HALF])(h)
    pre = PreNorm(c, m, "pool", parts, split=False)
    aff0 = pre.aff0
    steps = [k // 2 + 1 for k in range(KD)]
    before = [sum(steps[:k]) for k in range(KD)]
    a0 = c.take("pool_added", sum(steps))
    m0, d0 = c.take("pool_mean", KD), c.take("pool_out", KD)

    with nc.Block() as block:
        @block.sync
        def _(sp):
            sp.dma_start(inv[:], ins["k_pool_inverse"].unsqueeze(0).to_broadcast([P, 4, T])
                         ).then_inc(c["pool_counts_in"], 16)

        @block.scalar
        def _(act):
            pre.act(act)

        @block.tensor
        def _(pe):
            for j in range(2):
                pre.pe_sums(pe, j)
                pre.pe_spread(pe, j)

        @block.vector
        def _(dve):
            dve.memset(h_pad[:, :, 0:pad], 0.0).then_inc(c["pool_zeros"], 1)
            dve.memset(h_pad[:, :, pad + T:wide], 0.0).then_inc(c["pool_zeros"], 1)
            pre.dve(dve)
            dve.wait_ge(c["pool_zeros"], 2)
            for k in range(KD):
                dve.wait_ge(c["pre_shifted"], aff0 + KD + k + 1)
                src, lo, hi = h_pad[:, k, :], 0, wide
                for i in range(steps[k]):
                    slot = 2 * (k % 2) + i % 2
                    if i == 0 and k >= 2:
                        dve.wait_ge(c["pool_mean"], m0 + k - 1)
                    if i:
                        dve.wait_ge(c["pool_added"], a0 + before[k] + i)
                    back, ahead = (1, 0) if i == 0 else (2 ** (i - 1), 2 ** (i - 1))
                    lo, hi = lo + back, hi - ahead
                    dve.tensor_tensor(sums[:, slot, lo:hi], src[:, lo - back:hi - back],
                                      src[:, lo + ahead:hi + ahead], ALU.add
                                      ).then_inc(c["pool_added"], 1)
                    src = sums[:, slot, :]

        @block.gpsimd
        def _(pool):
            pool.wait_ge(c["pool_counts_in"], 16)
            for k in range(KD):
                slot = 2 * (k % 2) + (steps[k] - 1) % 2
                pool.wait_ge(c["pool_added"], a0 + before[k] + steps[k])
                pool.tensor_tensor(m.a[:, k, :], sums[:, slot, pad:pad + T], inv[:, k // 2, :],
                                   ALU.mult).then_inc(c["pool_mean"], 1)
                pool.wait_ge(c["pool_mean"], m0 + k + 1)
                pool.tensor_tensor(m.a[:, k, :], m.a[:, k, :], h_pad[:, k, pad:pad + T],
                                   ALU.subtract).then_inc(c["pool_out"], 1)


def lru_stage(nc, c, m, ins):
    n = 4
    t = m.at("lru_work", XN, [P, 16, T])
    xc, ra, gi, mi = t[:, 0:4], t[:, 4:8], t[:, 8:12], t[:, 12:16]
    bd = m.at("lru_gates", YX, [P, 2, n, P])
    small = m.at("lru_small", YX + 4096, [P, 12, n])
    squares = m.at("lru_squares", YX + 8192, [P, 4, HALF])
    lam = m.vt[:, m.col["lambda"]:m.col["lambda"] + n]
    terms = 8
    rms = [RootMeanSquare(c, m, f"lru{h}", 1, n, 4, n * P,
                          (lambda hh: lambda k: m.a[:, k, hh * HALF:(hh + 1) * HALF])(h),
                          [squares[:, i, :] for i in range(4)], m.ps[:, 4, 8 * h:8 * h + 8],
                          m.ps[:, 5, h * P:(h + 1) * P], [m.ps[:, 6 + h, :]], 4 * h)
           for h in range(2)]

    def gate_ps(which):
        return m.ps[:, 2 * which:2 * which + 2, :].rearrange("p b t -> p (b t)")

    with nc.Block() as block:
        @block.sync
        def _(sp):
            sp.wait_ge(c["lru_zero"], 1)
            for w, name in enumerate(("lru_gate_a_w_2", "lru_gate_x_w_2")):
                for odd in range(2):
                    src = ins[name][0].rearrange("(b o) i j -> o i b j", o=2)[odd]
                    s = slice(odd * 64, odd * 64 + 64)
                    sp.dma_start(bd[s, w, :, s], src).then_inc(c["lru_gates_in"], 16)

        @block.scalar
        def _(act):
            for k in range(n):
                act.activation(xc[:, k, :], m.a[:, k, :], ACT.Identity,
                               bias=vcol(m, "lru_conv_b", k), scale=vcol(m, "lru_conv_w", 12 + k)
                               ).then_inc(c["lru_centre"], 1)
            act.wait_ge(c["lru_small"], 3)
            act.activation(small[:, 3, :], small[:, 2, :], ACT.Exp).then_inc(c["lru_u"], 1)
            for k in range(n):
                for w, (name, dst) in enumerate((("gate_a_b", ra), ("gate_x_b", gi))):
                    act.wait_ge(c["lru_gate"], 2 * k + w + 1)
                    act.activation(dst[:, k, :], gate_ps(w), ACT.Sigmoid, bias=vcol(m, name, k)
                                   ).then_inc(c["lru_sigmoid"], 1)
            act.wait_ge(c["lru_coefs"], 2)
            act.wait_ge(c["lru_sigmoid"], 2 * n)
            for k in range(n):
                act.activation(mi[:, k, :], ra[:, k, :], ACT.Tanh, scale=small[:, 10, k:k + 1]
                               ).then_inc(c["lru_tanh"], 1)
                act.wait_ge(c["lru_tanh"], k + 1)
                act.activation(ra[:, k, :], ra[:, k, :], ACT.Exp, scale=small[:, 11, k:k + 1]
                               ).then_inc(c["lru_a"], 1)
            for k in range(n):
                act.wait_ge(c["lru_a"], k + 1)
                act.wait_ge(c["lru_ix"], k + 1)
                act.activation(xc[:, k, :], ra[:, k, :], ACT.Square).then_inc(c["lru_a2"], 1)
            for k in range(n):
                act.wait_ge(c["lru_m2"], k + 1)
                act.activation(mi[:, k, :], mi[:, k, :], ACT.Sqrt).then_inc(c["lru_m"], 1)
            for k in range(n):
                act.activation(m.a[:, 4 + k, :], m.a[:, 4 + k, :], ACT.Gelu_apprx_tanh
                               ).then_inc(c["lru_gelu"], 1)
            for h in range(2):
                rms[h].act_squares(act, lambda i: act.wait_ge(c["lru_y"], i + 1))
                rms[h].act_root(act)

        @block.tensor
        def _(pe):
            pe.wait_ge(c["lru_gates_in"], 64)
            for k in range(n):
                pe.wait_ge(c["lru_side"], 3 * k + 3)
                for w in range(2):
                    if k:
                        pe.wait_ge(c["lru_sigmoid"], 2 * k + w - 1)
                    for h in range(2):
                        last = pe.matmul(m.ps[:, 2 * w + h, :], bd[:, w, k, :],
                                         xc[:, k, h * HALF:(h + 1) * HALF], start=True, stop=True)
                    last.then_inc(c["lru_gate"], 1)
            for h in range(2):
                rms[h].pe_sums(pe)
                rms[h].pe_turn(pe)
                rms[h].pe_broadcast(pe, 0)

        @block.gpsimd
        def _(pool):
            pool.memset(bd[:], 0.0).then_inc(c["lru_zero"], 1)

        @block.vector
        def _(dve):
            done = 0

            def step(ins):
                nonlocal done
                done += 1
                ins.then_inc(c["lru_small"], 1)
                dve.wait_ge(c["lru_small"], done)

            step(dve.tensor_scalar(small[:, 0, :], lam, -1.0, None, ALU.mult))
            step(dve.tensor_scalar(small[:, 1, :], small[:, 0, :], 0.0, None, ALU.max))
            step(dve.tensor_tensor(small[:, 2, :], small[:, 0, :], lam, ALU.min))
            dve.wait_ge(c["lru_u"], 1)
            step(dve.tensor_scalar(small[:, 4, :], small[:, 3, :], 2.0, None, ALU.add))
            step(dve.reciprocal(small[:, 5, :], small[:, 4, :]))
            step(dve.tensor_tensor(small[:, 6, :], small[:, 3, :], small[:, 5, :], ALU.mult))
            step(dve.tensor_tensor(small[:, 7, :], small[:, 6, :], small[:, 6, :], ALU.mult))
            step(dve.tensor_scalar(small[:, 8, :], small[:, 7, :], 1.0 / (2 * terms + 1), None,
                                   ALU.mult))
            for i in range(terms - 1, 0, -1):
                step(dve.scalar_tensor_tensor(out=small[:, 8, :], in0=small[:, 8, :],
                                              scalar=1.0 / (2 * i + 1), in1=small[:, 7, :],
                                              op0=ALU.add, op1=ALU.mult))
            step(dve.scalar_tensor_tensor(out=small[:, 8, :], in0=small[:, 8, :], scalar=1.0,
                                          in1=small[:, 6, :], op0=ALU.add, op1=ALU.mult))
            step(dve.scalar_tensor_tensor(out=small[:, 9, :], in0=small[:, 8, :], scalar=2.0,
                                          in1=small[:, 1, :], op0=ALU.mult, op1=ALU.add))
            dve.tensor_scalar(small[:, 10, :], small[:, 9, :], LRU_C, None, ALU.mult
                              ).then_inc(c["lru_coefs"], 1)
            dve.tensor_scalar(small[:, 11, :], small[:, 9, :], -LRU_C, None, ALU.mult
                              ).then_inc(c["lru_coefs"], 1)
            for k in range(n):
                dve.wait_ge(c["lru_centre"], k + 1)
                for tap in range(3):
                    back = 3 - tap
                    if tap:
                        dve.wait_ge(c["lru_side"], 3 * k + tap)
                    dve.scalar_tensor_tensor(
                        out=xc[:, k, back:T], in0=m.a[:, k, 0:T - back],
                        scalar=vcol(m, "lru_conv_w", 4 * tap + k), in1=xc[:, k, back:T],
                        op0=ALU.mult, op1=ALU.add).then_inc(c["lru_side"], 1)
            for k in range(n):
                dve.wait_ge(c["lru_sigmoid"], 2 * k + 2)
                dve.tensor_tensor(gi[:, k, :], gi[:, k, :], xc[:, k, :], ALU.mult
                                  ).then_inc(c["lru_ix"], 1)
            for k in range(n):
                dve.wait_ge(c["lru_a2"], k + 1)
                dve.scalar_tensor_tensor(out=mi[:, k, :], in0=xc[:, k, :], scalar=1.0,
                                         in1=mi[:, k, :], op0=ALU.add, op1=ALU.mult
                                         ).then_inc(c["lru_m2"], 1)
            for k in range(n):
                dve.wait_ge(c["lru_m"], k + 1)
                dve.tensor_tensor(mi[:, k, :], mi[:, k, :], gi[:, k, :], ALU.mult
                                  ).then_inc(c["lru_in"], 1)
                dve.wait_ge(c["lru_in"], k + 1)
                dve.tensor_tensor_scan(xc[:, k, :], ra[:, k, :], mi[:, k, :], 0.0, ALU.mult,
                                       ALU.add).then_inc(c["lru_scan"], 1)
            for k in range(n):
                dve.wait_ge(c["lru_gelu"], k + 1)
                dve.wait_ge(c["lru_scan"], k + 1)
                dve.tensor_tensor(m.a[:, k, :], xc[:, k, :], m.a[:, 4 + k, :], ALU.mult
                                  ).then_inc(c["lru_y"], 1)
            for h in range(2):
                rms[h].dve_inverse(dve)
                rms[h].dve_row(dve)
                bank = rms[h].ready(dve, 0)
                for k in range(n):
                    y = m.a[:, k, h * HALF:(h + 1) * HALF]
                    dve.scalar_tensor_tensor(out=y, in0=y, scalar=vcol(m, "lru_norm", k), in1=bank,
                                             op0=ALU.mult, op1=ALU.mult
                                             ).then_inc(c["lru_out"], 1)


def retention_stage(nc, c, m, ins):
    nh = RET_HEADS
    q, k, v, gate = (m.a[:, 8 + 4 * i:12 + 4 * i, :] for i in range(4))
    t = m.at("ret_work", XN, [P, 16, T])
    cos, sin = t[:, 0, :], t[:, 1, :]
    direct, swapped = t[:, 2, :], t[:, 3, :]
    v_rows = t[:, 4:8, :].rearrange("p a (b e) -> p (a b) e", b=2)
    k_rows = t[:, 8:12, :].rearrange("p a (b e) -> p (a b) e", b=2)
    decay = t[:, 12, 0:HALF]
    q_decay = t[:, 12, HALF:T]
    state = [t[:, 13, 0:HALF], t[:, 13, HALF:T]]
    masked = [t[:, 14, 0:HALF], t[:, 14, HALF:T]]
    q_scaled = [t[:, 15, 0:HALF], t[:, 15, HALF:T]]
    perm = m.at("ret_perm", YX, [P, P])
    zeta = m.at("ret_zeta", YX + 512, [P, nh])
    squares = m.at("ret_squares", YX + 8192, [P, 4, HALF])
    carry = [float(np.exp(np.float32(P) * np.float32(g))) for g in RET_DECAY]
    items = [(x, h, slice(half * HALF, (half + 1) * HALF)) for h in range(nh)
             for x in (q, k) for half in range(2)]
    outs = [(h, slice(half * HALF, (half + 1) * HALF)) for h in range(nh) for half in range(2)]
    rms = RootMeanSquare(c, m, "ret", len(outs), 1, 4, P, lambda i: v[:, outs[i][0], outs[i][1]],
                         [squares[:, i, :] for i in range(4)], m.ps[:, 4, :], m.ps[:, 5, :],
                         [m.ps[:, 6, :], m.ps[:, 7, :]], 0)

    with nc.Block() as block:
        @block.sync
        def _(sp):
            sp.dma_start(perm[:], ins["k_perm2"]).then_inc(c["ret_in"], 16)
            sp.dma_start(cos, ins["k_cos2"]).then_inc(c["ret_in"], 16)
            sp.dma_start(sin, ins["k_sin2"]).then_inc(c["ret_in"], 16)
            sp.dma_start(decay, ins["k_decay"]).then_inc(c["ret_in"], 16)
            sp.dma_start(q_decay, ins["k_q_decay"].unsqueeze(0).to_broadcast([P, HALF])
                         ).then_inc(c["ret_in"], 16)
            sp.dma_start(zeta[:], ins["k_zeta"]).then_inc(c["ret_in"], 16)

        @block.tensor
        def _(pe):
            pe.wait_ge(c["ret_in"], 96)
            for i, (x, h, s) in enumerate(items):
                if i >= 2:
                    pe.wait_ge(c["ret_sin"], i - 1)
                pe.matmul(m.ps[:, i % 2, :], perm[:], x[:, h, s], start=True, stop=True
                          ).then_inc(c["ret_swapped"], 1)
            for n in range(TT):
                tok = slice(n * P, (n + 1) * P)
                for w, x in enumerate((v, k)):
                    j = 2 * n + w
                    if w == 0 and n == 0:
                        pe.wait_ge(c["ret_rotated"], len(items))
                    if j >= 2:
                        pe.wait_ge(c["ret_rows_v" if w == 0 else "ret_rows_k"], n)
                    for h in range(nh):
                        last = pe.transpose(m.ps[:, 2 + w, h * P:(h + 1) * P], x[:, h, tok],
                                            m.ident[:])
                    last.then_inc(c["ret_turned"], 1)
            for n in range(TT):
                tok = slice(n * P, (n + 1) * P)
                if n:
                    pe.wait_ge(c["ret_masked"], n)
                for h in range(nh):
                    last = pe.matmul(m.ps[:, 0, h * P:(h + 1) * P], k[:, h, tok], q[:, h, tok],
                                     start=True, stop=True)
                last.then_inc(c["ret_scores"], 1)
                if n < TT - 1:
                    pe.wait_ge(c["ret_rows_v"], n + 1)
                    pe.wait_ge(c["ret_rows_k"], n + 1)
                    if n:
                        pe.wait_ge(c["ret_state"], nh * n)
                    for h in range(nh):
                        hs = slice(h * P, (h + 1) * P)
                        last = pe.matmul(m.ps[:, 1, hs], k_rows[:, n, hs], v_rows[:, n, hs],
                                         start=True, stop=True)
                    last.then_inc(c["ret_kv"], 1)
                pe.wait_ge(c["ret_rows_v"], n + 1)
                pe.wait_ge(c["ret_masked"], n + 1)
                if n >= 2:
                    pe.wait_ge(c["ret_copied"], n - 1)
                if n:
                    pe.wait_ge(c["ret_q_scaled"], n)
                    pe.wait_ge(c["ret_state"], nh * n)
                for h in range(nh):
                    hs = slice(h * P, (h + 1) * P)
                    out = m.ps[:, 6 + n % 2, hs]
                    last = pe.matmul(out, v_rows[:, n, hs], masked[n % 2][:, hs], start=True,
                                     stop=(n == 0))
                    if n:
                        last = pe.matmul(out, state[n % 2][:, hs], q_scaled[n % 2][:, hs],
                                         start=False, stop=True)
                last.then_inc(c["ret_out"], 1)
            for i, (h, s) in enumerate(outs):
                if i == 0:
                    pe.wait_ge(c["ret_copied"], TT)
                if i >= 2:
                    pe.wait_ge(c["ret_centred"], i - 1)
                pe.matmul(m.ps[:, i % 2, :], m.ones[:, 0:1].to_broadcast([P, P]), v[:, h, s],
                          start=True, stop=True).then_inc(c["ret_sums"], 1)
            rms.pe_sums(pe)
            rms.pe_turn(pe)
            for g in range(len(outs)):
                rms.pe_broadcast(pe, g)

        @block.scalar
        def _(act):
            for n in range(TT):
                act.wait_ge(c["ret_turned"], 2 * n + 1)
                act.activation(v_rows[:, n, :], m.ps[:, 2, :], ACT.Copy
                               ).then_inc(c["ret_rows_v"], 1)
            for n in range(TT):
                act.wait_ge(c["ret_out"], n + 1)
                act.activation(v[:, :, n * P:(n + 1) * P], two(m.ps[:, 6 + n % 2, :], nh), ACT.Copy
                               ).then_inc(c["ret_copied"], 1)
            for h in range(nh):
                act.activation(gate[:, h, :], gate[:, h, :], ACT.Silu).then_inc(c["ret_silu"], 1)
            rms.act_squares(act, lambda i: act.wait_ge(c["ret_centred"], i + 1))
            rms.act_root(act)

        @block.gpsimd
        def _(pool):
            pool.wait_ge(c["ret_in"], 96)
            for i, (x, h, s) in enumerate(items):
                if i >= 2:
                    pool.wait_ge(c["ret_rotated"], i - 1)
                pool.tensor_tensor(two(direct)[:, i % 2, :], x[:, h, s], cos[:, s], ALU.mult
                                   ).then_inc(c["ret_direct"], 1)
            pool.wait_ge(c["ret_rotated"], len(items))
            for n in range(1, TT):
                if n >= 3:
                    pool.wait_ge(c["ret_out"], n - 1)
                pool.tensor_tensor(two(q_scaled[n % 2], nh), q[:, :, n * P:(n + 1) * P],
                                   two(q_decay, nh), ALU.mult).then_inc(c["ret_q_scaled"], 1)

        @block.vector
        def _(dve):
            dve.wait_ge(c["ret_in"], 96)
            for i, (x, h, s) in enumerate(items):
                dve.wait_ge(c["ret_swapped"], i + 1)
                dve.tensor_tensor(two(swapped)[:, i % 2, :], m.ps[:, i % 2, :], sin[:, s],
                                  ALU.mult).then_inc(c["ret_sin"], 1)
                dve.wait_ge(c["ret_sin"], i + 1)
                dve.wait_ge(c["ret_direct"], i + 1)
                dve.tensor_tensor(x[:, h, s], two(direct)[:, i % 2, :], two(swapped)[:, i % 2, :],
                                  ALU.add).then_inc(c["ret_rotated"], 1)
            for n in range(TT):
                dve.wait_ge(c["ret_turned"], 2 * n + 2)
                dve.tensor_tensor(two(k_rows[:, n, :], nh), two(m.ps[:, 3, :], nh),
                                  zeta[:].unsqueeze(2).to_broadcast([P, nh, P]), ALU.mult
                                  ).then_inc(c["ret_rows_k"], 1)
            for n in range(TT):
                dve.wait_ge(c["ret_scores"], n + 1)
                if n >= 2:
                    dve.wait_ge(c["ret_out"], n - 1)
                dve.tensor_tensor(masked[n % 2], m.ps[:, 0, :], decay, ALU.mult
                                  ).then_inc(c["ret_masked"], 1)
                if n < TT - 1:
                    dve.wait_ge(c["ret_kv"], n + 1)
                    if n >= 1:
                        dve.wait_ge(c["ret_out"], n)
                        dve.wait_ge(c["ret_state"], nh * n)
                    for h in range(nh):
                        hs = slice(h * P, (h + 1) * P)
                        if n == 0:
                            dve.tensor_copy(state[1][:, hs], m.ps[:, 1, hs]
                                            ).then_inc(c["ret_state"], 1)
                        else:
                            dve.scalar_tensor_tensor(
                                out=state[(n + 1) % 2][:, hs], in0=state[n % 2][:, hs],
                                scalar=carry[h], in1=m.ps[:, 1, hs], op0=ALU.mult, op1=ALU.add
                                ).then_inc(c["ret_state"], 1)
            for i, (h, s) in enumerate(outs):
                dve.wait_ge(c["ret_sums"], i + 1)
                dve.scalar_tensor_tensor(out=v[:, h, s], in0=m.ps[:, i % 2, :], scalar=-1.0 / P,
                                         in1=v[:, h, s], op0=ALU.mult, op1=ALU.add
                                         ).then_inc(c["ret_centred"], 1)
            rms.dve_inverse(dve)
            rms.dve_row(dve)
            for i, (h, s) in enumerate(outs):
                bank = rms.ready(dve, i)
                rms.used(dve.scalar_tensor_tensor(
                    out=v[:, h, s], in0=v[:, h, s], scalar=vcol(m, "ret_norm", h), in1=bank,
                    op0=ALU.mult, op1=ALU.mult))
                dve.wait_ge(c["rms_broadcast_used"], rms.free0 + i + 1)
                dve.wait_ge(c["ret_silu"], h + 1)
                dve.tensor_tensor(m.a[:, 4 + h, s], v[:, h, s], gate[:, h, s], ALU.mult
                                  ).then_inc(c["ret_done"], 1)


def final_stage(nc, c, m, out):
    parts = halves_parts(m, lambda k: vcol(m, "final", k), lambda k: 0.0)
    pre = PreNorm(c, m, "final", parts, split=False)
    rows = m.at("out_rows", XN, [P, TT, D])
    out_tiles = out.rearrange("b (t p) d -> (b t) p d", p=P)
    groups = [(t, g) for t in range(TT) for g in range(2)]
    with nc.Block() as block:
        @block.scalar
        def _(act):
            pre.act(act)

        @block.tensor
        def _(pe):
            for j in range(2):
                pre.pe_sums(pe, j)
                pre.pe_spread(pe, j)
            for i, (t, g) in enumerate(groups):
                pe.wait_ge(c["pre_shifted"], pre.aff0 + KD * (t // 4 + 1))
                if i >= 4:
                    pe.wait_ge(c["out_copied"], i - 3)
                for q in range(4):
                    k = 4 * g + q
                    last = pe.transpose(m.ps[:, i % 4, q * P:(q + 1) * P],
                                        m.a[:, k, t * P:(t + 1) * P], m.ident[:])
                last.then_inc(c["out_turned"], 1)

        @block.vector
        def _(dve):
            pre.dve(dve)
            for i, (t, g) in enumerate(groups):
                dve.wait_ge(c["out_turned"], i + 1)
                dve.tensor_copy(rows[:, t, g * HALF:(g + 1) * HALF], m.ps[:, i % 4, :]
                                ).then_inc(c["out_copied"], 1)

        @block.sync
        def _(sp):
            for t in range(TT):
                sp.wait_ge(c["out_copied"], 2 * t + 2)
                sp.dma_start(out_tiles[t], rows[:, t, :]).then_inc(c["out_stored"], 16)
            sp.wait_ge(c["out_stored"], 16 * TT)


def build(nc, ins, out):
    c = Counters(nc)
    m = Memory(nc)
    x_dram = nc.dram_tensor("x_scratch", [P, KD, T], F32).ap()
    load_vectors(nc, c, m, ins)
    m.gains_sw = m.vec("gains_sw", [P, 2])
    m.at_max, m.at_inv = m.vec("at_max", [P, 4]), m.vec("at_inv", [P, 4])
    m.at_rows = m.rms_row[0]
    m.mod_acc = m.vec("mod_acc", [P, 2 * P])
    attention_memory(m)

    parts = halves_parts(m, lambda k: m.coef[:, 0, 0, k:k + 1], lambda k: mod_col(m, 0, 0, k),
                         squares=5)
    parts.append(dict(
        source=lambda k: m.ctx_cm[:, k, :], work=lambda k: m.ctx_cm[:, k, :],
        hi=lambda k: m.xnc_hi[:, k, :], lo=lambda k: m.xnc_lo[:, k, :],
        scale=lambda k: m.coef_ctx[:, k:k + 1], shift=lambda k: mod_col(m, 0, 0, k, 1), tiles=2,
        stat=m.ps[:, 4, 16:24], turned=m.ps[:, 5, 2 * P:3 * P], bank=m.ps[:, 4, 256:512], small=8,
        squares=[m.a[:, 23, i * CTX:(i + 1) * CTX] for i in range(4)]))
    project_stage(nc, c, m, "qkv", PreNorm(c, m, "qkv", parts), ins["w_qkv"][0], 12, HEADS,
                  lambda u: (m.a[:, bass.ds(u, 1), :].rearrange("p o t -> p (o t)")
                             if not isinstance(u, int) or u < HEADS
                             else m.kv_raw[:, u - HEADS, CTX:KEYS]),
                  lambda u: m.kv_raw[:, u - HEADS, 0:CTX])
    rotate_stage(nc, c, m, ins)
    attention_stage(nc, c, m, Modulation(c, m, ins["w_mod"], 0, 16, 16, m.mod_buf, m.mod_acc,
                                         m.ps[:, 7, 0:32]))
    w_o = ins["w_o"][0].rearrange("(k p) n -> p k n", p=P)
    down_stage(nc, c, m, "w_o", KD, [KD], lambda i, b, g: w_o[:, :, bass.ds(i * 256 + b * P, P)],
               lambda i, b: 0, None, lambda k: m.coef[:, 0, 1, k:k + 1], x_dram, False, True)

    def ffn(layer):
        parts = halves_parts(m, lambda k: m.coef[:, layer, 2, k:k + 1],
                             lambda k: mod_col(m, layer, 3, k), squares=6)
        cw, cb = m.col[f"conv_w{layer}"], m.col["conv_b"] + layer * FF1
        ffn_up_stage(nc, c, m, f"up{layer}", PreNorm(c, m, f"up{layer}", parts),
                     ins["w_up"][layer], FF1,
                     lambda tap, j: m.vt[:, bass.ds(j + (cw + tap * FF1), 1)],
                     lambda j: m.vt[:, bass.ds(j + cb, 1)], False,
                     None if layer else Modulation(
                         c, m, ins["w_mod"], 1, 0, 24,
                         [m.at("mod_buf_up0", A0 + 22 * 4096, [P, KD, 2 * P]),
                          m.at("mod_buf_up1", YX + 8192, [P, KD, 2 * P])], m.mod_acc,
                         m.ps[:, 4, 64:112]))
        w = ins["w_down"][layer].rearrange("(k p) n -> p k n", p=P)
        sizes = [8, 8, 6]
        down_stage(nc, c, m, f"down{layer}", FF1, sizes,
                   lambda i, b, g: w[:, 8 * g:8 * g + sizes[g], bass.ds(i * 256 + b * P, P)],
                   lambda i, b: 0, None, lambda k: m.coef[:, layer, 3, k:k + 1], x_dram, True,
                   True)

    ffn(0)
    pool_stage(nc, c, m, ins)
    w_pool = ins["w_pool"][0].rearrange("g (k p) n -> p g k n", p=P)
    bps = m.vec("pool_bias", [P, KD])
    with nc.Block() as block:
        @block.vector
        def _(dve):
            dve.tensor_tensor(bps[:], m.vt[:, m.col["b_pool"]:m.col["b_pool"] + KD],
                              m.vt[:, m.col["pool_scale"]:m.col["pool_scale"] + KD], ALU.mult
                              ).then_inc(c["pool_bias"], 1)
    down_stage(nc, c, m, "w_pool", KD, [2],
               lambda i, b, g: w_pool[:, bass.ds(i, 1), :, b * P:(b + 1) * P].rearrange(
                   "p g k n -> p (g k) n"),
               lambda i, b: 2 * i,
               (lambda n: m.vt[:, bass.ds(n + m.col["pool_scale"], 1)],
                lambda n: bps[:, bass.ds(n, 1)]),
               lambda k: m.coef[:, 1, 1, k:k + 1], x_dram, False, True)
    ffn(1)

    parts = halves_parts(m, lambda k: vcol(m, "norm1", k), lambda k: 0.0)
    project_stage(nc, c, m, "w_in", PreNorm(c, m, "w_in", parts), ins["w_in_2"][0], 24, 24,
                  lambda u: m.a[:, bass.ds(u, 1), :].rearrange("p o t -> p (o t)"), None)
    lru_stage(nc, c, m, ins)
    retention_stage(nc, c, m, ins)
    w_out = ins["w_out_2"][0].rearrange("(k p) n -> p k n", p=P)
    down_stage(nc, c, m, "w_out", KD, [KD],
               lambda i, b, g: w_out[:, :, bass.ds(i * 256 + b * P, P)],
               lambda i, b: 0, None, None, x_dram, True, True)
    parts = halves_parts(m, lambda k: vcol(m, "norm2", k), lambda k: 0.0)
    ffn_w = [m.col[f"ffn_w{tap}"] for tap in range(3)]
    ffn_up_stage(nc, c, m, "up2", PreNorm(c, m, "up2", parts), ins["ffn_up_w_2"][0], FF2,
                 lambda tap, j: m.vt[:, bass.ds(j + ffn_w[tap], 1)],
                 lambda j: m.vt[:, bass.ds(j + m.col["ffn_b"], 1)], True)
    w_d = ins["ffn_down_w_2"][0].rearrange("(k p) n -> p k n", p=P)
    down_stage(nc, c, m, "down2", FF2, [8, 8, 8],
               lambda i, b, g: w_d[:, 8 * g:8 * g + 8, bass.ds(i * 256 + b * P, P)],
               lambda i, b: 0, None, None, x_dram, True, False)
    final_stage(nc, c, m, out)


_INS = ["x", "c", "ctx", "c_ctx", "w_mod", "b_mod", "g_pre_mix", "g_post_mix", "g_pre_ffn",
        "g_post_ffn", "w_qkv", "g_q", "g_k", "w_o", "w_pool", "b_pool", "pool_scale", "w_up",
        "conv_w", "conv_b", "w_down", "norm1_gain_2", "w_in_2", "lru_conv_w_2", "lru_conv_b_2",
        "lru_gate_a_w_2", "lru_gate_a_b_2", "lru_gate_x_w_2", "lru_gate_x_b_2", "lru_lambda_2",
        "lru_norm_gain_2", "ret_norm_gain_2", "w_out_2", "norm2_gain_2", "ffn_up_w_2",
        "ffn_conv_w_2", "ffn_conv_b_2", "ffn_down_w_2", "final_norm_gain_2"]


def constants():
    f = np.float32
    t = np.arange(T)
    d = np.arange(P)
    inv = (f(10000.0) ** (-np.arange(32, dtype=f) / f(32))).astype(f)
    pos = np.where((d // 64)[:, None] == 0, (t // 64)[None], (t % 64)[None]).astype(f)
    ang = (pos * inv[d % 32][:, None]).astype(f)
    sign = np.where(d % 64 < 32, -1, 1).astype(f)[:, None]
    k = {"k_ident": np.eye(P, dtype=f), "k_cos1": np.cos(ang), "k_sin1": sign * np.sin(ang),
         "k_perm1": np.eye(P, dtype=f)[d ^ 32]}
    inv = (f(10000.0) ** (-np.arange(0, P, 2, dtype=f) / f(P))).astype(f)
    ang = (t.astype(f)[None] * inv[d % 64][:, None]).astype(f)
    sign = np.where(d < 64, -1, 1).astype(f)[:, None]
    k.update(k_cos2=np.cos(ang), k_sin2=sign * np.sin(ang), k_perm2=np.eye(P, dtype=f)[d ^ 64])
    k["k_pool_inverse"] = np.stack([
        1.0 / (np.minimum(t + w - w // 2, T) - np.maximum(t - w // 2, 0)) for w in (2, 4, 8, 16)])
    log_g = np.log1p(-np.exp2(f(-5.0) - np.arange(RET_HEADS, dtype=f))).astype(f)
    diff = (d[None, :] - d[:, None]).astype(f)
    decay = np.where(diff >= 0, np.exp(np.maximum(diff, 0)[:, None, :] * log_g[None, :, None])
                     .transpose(1, 0, 2), 0.0)
    k["k_decay"] = (decay.transpose(1, 0, 2) * RET_SCALE).reshape(P, RET_HEADS * P)
    k["k_zeta"] = np.exp((P - 1 - d).astype(f)[:, None] * log_g[None, :]) * RET_SCALE
    k["k_q_decay"] = np.exp((d + 1).astype(f)[None, :] * log_g[:, None]).reshape(-1)
    return {name: np.ascontiguousarray(v.astype(f)) for name, v in k.items()}


def kernel(**inputs):
    import concourse.bacc as bacc
    from concourse.bass_utils import run_bass_kernel_spmd as run

    nc = bacc.Bacc("TRN2", target_bir_lowering=False, num_devices=1)
    arrays, ins = {}, {}
    for name, a in [(n, np.ascontiguousarray(inputs[n])) for n in _INS] + list(constants().items()):
        arrays[f"in_{name}"] = a
        ins[name] = nc.dram_tensor(f"in_{name}", a.shape, mybir.dt.from_np(a.dtype),
                                   kind="ExternalInput").ap()
    out = nc.dram_tensor("out_x", [1, T, D], F32, kind="ExternalOutput").ap()
    build(nc, ins, out)
    r = run(nc, [arrays], core_ids=[0])
    return r.results[0]["out_x"]
```

```python
import math

import numpy as np

import concourse.bass as bass
from concourse import mybir

F32 = mybir.dt.float32
F32R = mybir.dt.float32r
ALU = mybir.AluOpType
ACT = mybir.ActivationFunctionType
AX_X = mybir.AxisListType.X

P = 128
D = 1024
KD = D // P
T = 1024
HALF = 512
TT = T // P
CTX = 256
KEYS = CTX + T
HEADS, KV, GROUP = 8, 2, 4
FF1, FF2 = 2816 // P, 3072 // P
RET_HEADS = 4
EPS = 1e-6
ATT_SCALE = 1.0 / math.sqrt(P)
RET_SCALE = float(P) ** -0.5
RET_DECAY = [float(np.log1p(-np.exp2(np.float32(-5.0 - h)))) for h in range(RET_HEADS)]
LRU_C = 8.0
PROBS = 5

BASE = 16512
CONST = 0
W_RAW = 7936
W_HI = W_RAW + 2 * 4096
W_LO = W_HI + 2 * 4096
YX = W_LO + 2 * 4096
XN = YX + 16384
A0 = XN + 65536
END = A0 + 24 * 4096


class Counters:

    def __init__(self, nc):
        self.nc, self.sems, self.reached = nc, {}, {}

    def __getitem__(self, name):
        if name not in self.sems:
            self.sems[name] = self.nc.alloc_semaphore(name)
            self.reached.setdefault(name, 0)
        return self.sems[name]

    def take(self, name, total):
        self[name]
        before = self.reached[name]
        self.reached[name] = before + total
        return before


class Memory:

    def __init__(self, nc):
        self.nc, self.small = nc, CONST

        def at(name, offset, shape, dtype=F32):
            return nc.alloc_sbuf_tensor_at(name, shape, dtype, offset=BASE + offset)

        self.at = at
        self.w_raw = at("w_raw", W_RAW, [P, 2, 8, P])
        self.w_hi = at("w_hi", W_HI, [P, 2, 8, P], F32R)
        self.w_lo = at("w_lo", W_LO, [P, 2, 8, P], F32R)
        self.xn_hi = at("xn_hi", XN, [P, KD, T], F32R)
        self.xn_lo = at("xn_lo", XN + 32768, [P, KD, T], F32R)
        self.ring = at("ring", XN, [P, 32, HALF], F32R)
        self.a = at("a", A0, [P, 24, T])
        self.a_lo = [at(f"a_lo{i}", A0 + 32768 * i, [P, 8, T], F32R) for i in range(3)]
        self.x = self.a[:, 8:16, :]
        self.yx = at("yx", YX, [P, KD, HALF])
        self.xnc_hi = at("xnc_hi", YX, [P, KD, CTX], F32R)
        self.xnc_lo = at("xnc_lo", YX + 8192, [P, KD, CTX], F32R)
        self.ps = nc.alloc_psum_tensor("ps", [P, 8, 512], F32)

    def vec(self, name, shape):
        n = 4 * int(np.prod(shape[1:]))
        t = self.at(name, self.small, shape)
        self.small += (n + 31) // 32 * 32
        assert self.small <= W_RAW, self.small
        return t


def stand_alone(eng, c):
    eng.sem_inc(c[f"waits_passed_{str(eng.engine).split('.')[-1].lower()}"], 1)


class WeightStream:

    def __init__(self, c, m, units, first):
        assert units % 2 == 0
        self.first = first
        self.loaded = self.divided = False
        self.c, self.m = c, m
        self.raw0 = [c.take(f"w_raw{s}", 16 * units // 2) for s in (0, 1)]
        self.hi0 = c.take("w_hi", units)
        self.lo0 = c.take("w_lo", units)
        self.done0 = c.take("unit_done", units)

    def load(self, sp, u, slot, src):
        kc = src.shape[1]
        sp.wait_ge(self.c["w_lo"], self.lo0 + u + 1)
        sp.dma_start(self.m.w_raw[:, slot, 0:kc, :], src).then_inc(self.c[f"w_raw{slot}"], 16)

    def split(self, pool, u, pair, slot, kc):
        raw = self.m.w_raw[:, slot, 0:kc, :]
        hi = self.m.w_hi[:, slot, 0:kc, :]
        pool.wait_ge(self.c[f"w_raw{slot}"], 16 * pair + self.raw0[slot] + 16)
        pool.wait_ge(self.c["unit_done"], self.done0 + u + 1)
        stand_alone(pool, self.c)
        pool.tensor_scalar(hi, raw, 1.0, 1.0, ALU.mult, ALU.mult).then_inc(self.c["w_hi"], 1)
        pool.wait_ge(self.c["w_hi"], self.hi0 + u + 1)
        pool.tensor_tensor(self.m.w_lo[:, slot, 0:kc, :], raw, hi.bitcast(F32),
                           ALU.subtract).then_inc(self.c["w_lo"], 1)

    def load_first(self, sp):
        self.loaded = True
        for u in range(2):
            self.load(sp, u, u, self.first[u])

    def split_first(self, pool, u):
        if u == 0:
            self.divided = True
        self.split(pool, u, 0, u, self.first[u].shape[1])

    def ready(self, pe, u):
        pe.wait_ge(self.c["w_lo"], self.lo0 + u + 3)

    def products(self, pe, slot, out, k, hi, lo, start, stop):
        w_hi, w_lo = self.m.w_hi[:, slot, k, :], self.m.w_lo[:, slot, k, :]
        pe.matmul(out, w_hi, hi, start=start, stop=False)
        pe.matmul(out, w_hi, lo, start=False, stop=False)
        return pe.matmul(out, w_lo, hi, start=False, stop=stop)

    def finished(self, eng, u):
        eng.wait_ge(self.c["unit_done"], self.done0 + u + 3)


class RootMeanSquare:

    def __init__(self, c, m, name, groups, chunks, tiles, count, source, squares, stat, turned,
                 broadcast, small, family="rms"):
        self.c, self.m, self.family = c, m, family

        def take(what, total):
            return c.take(f"{family}_{what}", total)

        self.groups, self.chunks, self.tiles, self.count = groups, chunks, tiles, count
        self.source, self.squares = source, squares
        self.stat, self.turned, self.broadcast = stat, turned, broadcast
        self.cols = groups * tiles
        self.sd = m.rms_sd[:, small:small + self.cols]
        self.rs = m.rms_rs[:, small:small + self.cols]
        self.row = m.rms_row[small // 4] if self.cols <= 4 else m.rms_rows
        n = groups * chunks
        self.n = n
        self.sq0 = take("squared", n)
        assert groups == 1 or chunks == 1
        self.add0 = take("added", n - 1 if chunks > 1 else 0)
        self.sum0 = take("summed", 1 if chunks > 1 else n)
        self.sd0 = take("root", 1)
        self.rc0 = take("inverse", 1)
        self.tr0 = take("turned", 1)
        self.row0 = take("row", 1)
        self.rb0 = take("broadcast", groups)
        self.free0 = take("broadcast_used", groups if groups > len(broadcast) else 0)

    def sem(self, what):
        return self.c[f"{self.family}_{what}"]

    def square(self, i):
        if self.chunks == 1:
            return self.squares[i % len(self.squares)]
        return self.squares[0 if i == 0 else 1 + (i - 1) % (len(self.squares) - 1)]

    def act_squares(self, act, before=None, which=None):
        slots = len(self.squares)
        for i in which or range(self.n):
            if before:
                before(i)
            if i >= slots and self.chunks == 1:
                act.wait_ge(self.sem("summed"), self.sum0 + i - slots + 1)
            elif i >= slots:
                act.wait_ge(self.sem("added"), self.add0 + i - slots + 1)
            src, out = self.source(i), self.square(i)
            if len(src.shape) == 3:
                out = out.rearrange("p (a t) -> p a t", a=src.shape[1])
            act.activation(out, src, ACT.Square).then_inc(self.sem("squared"), 1)

    def dve_sums(self, dve, which=None):
        for i in which or range(1, self.n):
            dve.wait_ge(self.sem("squared"), self.sq0 + i + 1)
            if i > 1:
                dve.wait_ge(self.sem("added"), self.add0 + i - 1)
            dve.tensor_tensor(self.square(0), self.square(0), self.square(i), ALU.add
                              ).then_inc(self.sem("added"), 1)

    def pe_sums(self, pe):
        for i in range(self.n if self.chunks == 1 else 1):
            if self.chunks == 1:
                pe.wait_ge(self.sem("squared"), self.sq0 + i + 1)
            else:
                pe.wait_ge(self.sem("added"), self.add0 + self.n - 1)
            for t in range(self.tiles):
                col = i * self.tiles + t
                last = pe.matmul(self.stat[:, col:col + 1],
                                 self.square(i)[:, t * P:(t + 1) * P],
                                 self.m.ones[:, 0:1], start=True, stop=True)
            last.then_inc(self.sem("summed"), 1)

    def summed(self, eng):
        eng.wait_ge(self.sem("summed"), self.sum0 + (self.n if self.chunks == 1 else 1))

    def act_root(self, act):
        act.wait_ge(self.sem("summed"), self.sum0 + (self.n if self.chunks == 1 else 1))
        act.activation(self.sd, self.stat[:, 0:self.cols], ACT.Sqrt, bias=self.m.eps[:, 0:1],
                       scale=1.0 / self.count).then_inc(self.sem("root"), 1)

    def dve_inverse(self, dve, sums=True):
        if self.chunks > 1 and sums:
            self.dve_sums(dve)
        dve.wait_ge(self.sem("root"), self.sd0 + 1)
        dve.reciprocal(self.rs, self.sd).then_inc(self.sem("inverse"), 1)

    def pe_turn(self, pe):
        pe.wait_ge(self.sem("inverse"), self.rc0 + 1)
        pe.transpose(self.turned[0:self.cols, 0:P], self.rs, self.m.ident[:]
                     ).then_inc(self.sem("turned"), 1)

    def dve_row(self, dve):
        dve.wait_ge(self.sem("turned"), self.tr0 + 1)
        dve.tensor_copy(self.row[0:self.cols, :], self.turned[0:self.cols, 0:P]
                        ).then_inc(self.sem("row"), 1)

    def pe_broadcast(self, pe, g):
        banks = len(self.broadcast)
        if g == 0:
            pe.wait_ge(self.sem("row"), self.row0 + 1)
        if g >= banks:
            pe.wait_ge(self.sem("broadcast_used"), self.free0 + g - banks + 1)
        out = self.broadcast[g % banks]
        for t in range(self.tiles):
            col = g * self.tiles + t
            last = pe.matmul(out[:, t * P:(t + 1) * P],
                             self.m.ident[0:self.cols, col:col + 1].to_broadcast([self.cols, P]),
                             self.row[0:self.cols, :], start=True, stop=True)
        last.then_inc(self.sem("broadcast"), 1)

    def ready(self, eng, g):
        eng.wait_ge(self.sem("broadcast"), self.rb0 + g + 1)
        return self.broadcast[g % len(self.broadcast)][:, 0:self.tiles * P]

    def used(self, last):
        return last.then_inc(self.sem("broadcast_used"), 1)


class PreNorm:

    def __init__(self, c, m, name, parts, split=True, early=0):
        self.c, self.m, self.parts, self.split, self.early = c, m, parts, split, early
        n = KD * len(parts)
        self.x0, self.aff0 = c.take("pre_scaled", n), c.take("pre_shifted", n)
        self.h0, self.l0 = c.take("pre_hi", n if split else 0), c.take("pre_lo", n if split else 0)
        self.name, self.rms = name, [None] * len(parts)
        self.late = range(early, len(parts))
        for j in range(early):
            self.rms[j] = self.norm(j, "early")

    def norm(self, j, family):
        p = self.parts[j]
        return RootMeanSquare(self.c, self.m, f"{self.name}{j}", 1, KD, p["tiles"], D, p["source"],
                              p["squares"], p["stat"], p["turned"], [p["bank"]], p["small"],
                              family)

    def begin(self, tail=None):
        self.tail = tail
        for j in self.late:
            self.rms[j] = self.norm(j, "rms")

    def act_shift(self, act, j):
        p = self.parts[j]
        for k in range(KD):
            act.wait_ge(self.c["pre_scaled"], self.x0 + j * KD + k + 1)
            act.activation(p["work"](k), p["work"](k), ACT.Identity, bias=p["shift"](k),
                           scale=p["scale"](k)).then_inc(self.c["pre_shifted"], 1)

    def dve_scale(self, dve, j):
        p = self.parts[j]
        bank = self.rms[j].ready(dve, 0)
        for k in range(KD):
            dve.tensor_tensor(p["work"](k), p["source"](k), bank, ALU.mult
                              ).then_inc(self.c["pre_scaled"], 1)

    def dve_lows(self, dve, j, steps=()):
        p, steps = self.parts[j], list(steps)
        for k in range(KD):
            if k in (3, 6) and steps:
                steps.pop(0)()
            dve.wait_ge(self.c["pre_hi"], self.h0 + j * KD + k + 1)
            dve.tensor_tensor(p["lo"](k), p["work"](k), p["hi"](k).bitcast(F32),
                              ALU.subtract).then_inc(self.c["pre_lo"], 1)

    def act(self, act, between=None):
        if self.tail:
            self.tail.act(act)
        if between:
            between()
        for j in range(0 if self.tail else self.early):
            self.act_shift(act, j)
        for j in self.late:
            self.rms[j].act_squares(act, lambda k: self.tail and self.tail.wait(act, k))
            if self.tail:
                self.tail.act_store(act)
            self.rms[j].act_root(act)
            self.act_shift(act, j)

    def pe_steps(self, pe):
        return self.tail.pe_steps(pe) if self.tail else []

    def pe_sums(self, pe, j):
        if j in self.late:
            self.rms[j].pe_sums(pe)

    def pe_spread(self, pe, j):
        if j in self.late:
            self.rms[j].pe_turn(pe)
            self.rms[j].pe_broadcast(pe, 0)

    def pool(self, pool, ws):
        for j, p in enumerate(self.parts):
            if j == 1:
                ws.split_first(pool, 1)
            for k in range(KD):
                pool.wait_ge(self.c["pre_shifted"], self.aff0 + j * KD + k + 1)
                pool.tensor_scalar(p["hi"](k), p["work"](k), 1.0, 1.0, ALU.mult, ALU.mult
                                   ).then_inc(self.c["pre_hi"], 1)

    def dve(self, dve):
        for j in range(0 if self.tail else self.early):
            self.dve_lows(dve, j)
        if self.tail:
            steps = self.tail.dve_steps(dve)
            if self.split:
                self.dve_lows(dve, 0, steps)
            else:
                for step in steps:
                    step()
            self.tail.dve(dve)
        for j in self.late:
            self.rms[j].dve_inverse(dve)
            self.rms[j].dve_row(dve)
            if self.tail:
                self.tail.wait(dve, KD - 1)
            self.dve_scale(dve, j)
            if self.split:
                self.dve_lows(dve, j)

    def ready(self, eng, part, k=KD - 1):
        eng.wait_ge(self.c["pre_lo"], self.l0 + part * KD + k + 1)


class Residual:

    def __init__(self, c, m, rms, y, x, post, used, loaded, scaled, new, store):
        self.c, self.m, self.rms, self.y, self.x, self.post = c, m, rms, y, x, post
        self.used, self.loaded, self.scaled, self.new, self.store = used, loaded, scaled, new, store

    def pe_steps(self, pe):
        if not self.rms:
            return []
        return [lambda: self.rms.pe_sums(pe), lambda: self.rms.pe_turn(pe),
                lambda: self.rms.pe_broadcast(pe, 0)]

    def act(self, act):
        if self.rms:
            self.rms.act_root(act)

    def act_store(self, act):
        if self.store is not None:
            act.wait_ge(self.c["x_new"], self.new + KD)
            act.dma_start(self.store, self.m.x[:, :, HALF:T]).then_inc(self.c["x_stored"], 16)

    def dve_steps(self, dve):
        if not self.rms:
            return []
        return [lambda: self.rms.dve_inverse(dve, sums=False), lambda: self.rms.dve_row(dve)]

    def dve(self, dve):
        if self.rms:
            bank = self.rms.ready(dve, 0)
        else:
            dve.wait_ge(self.c["down_used"], self.used)
        if self.loaded is not None:
            dve.wait_ge(self.c["x_loaded"], self.loaded)
        for k in range(KD + 1 if self.post else 0):
            if k < KD:
                dve.tensor_tensor(self.y(k), self.y(k), bank, ALU.mult
                                  ).then_inc(self.c["x_scaled"], 1)
            if k:
                dve.wait_ge(self.c["x_scaled"], self.scaled + k)
                dve.scalar_tensor_tensor(out=self.x(k - 1), in0=self.y(k - 1),
                                         scalar=self.post(k - 1), in1=self.x(k - 1),
                                         op0=ALU.mult, op1=ALU.add
                                         ).then_inc(self.c["x_new"], 1)
        for k in range(0 if self.post else KD):
            dve.tensor_tensor(self.x(k), self.y(k), self.x(k), ALU.add
                              ).then_inc(self.c["x_new"], 1)

    def wait(self, eng, k):
        eng.wait_ge(self.c["x_new"], self.new + k + 1)


class Modulation:

    COLS = 2 * P

    def __init__(self, c, m, w_mod, layer, first, pieces, buf, acc, bank):
        self.c, self.m, self.layer, self.first, self.pieces = c, m, layer, first, pieces
        self.w = w_mod.rearrange("l (k p) n -> l p k n", p=P)[layer]
        self.buf, self.acc, self.sums = buf, acc, bank
        self.in0 = [c.take(f"mod_in{s}", 16 * pieces // 2) for s in range(2)]
        self.product0, self.reduced0 = c.take("mod_product", pieces), c.take("mod_reduced", pieces)
        self.summed0 = c.take("mod_summed", pieces)

    def load(self, sp, i, slot):
        sp.wait_ge(self.c["mod_reduced"], self.reduced0 + i + 1)
        sp.dma_start(self.buf[slot][:], self.w[:, :, bass.ds(i * self.COLS + self.first * P,
                                                             self.COLS)]
                     ).then_inc(self.c[f"mod_in{slot}"], 16)

    def product(self, pool, pair, slot):
        piece = self.buf[slot][:]
        pool.wait_ge(self.c[f"mod_in{slot}"], 16 * pair + self.in0[slot] + 16)
        pool.tensor_tensor(piece, piece, self.m.silu_c[:, :, 0:1].to_broadcast([P, KD, self.COLS]),
                           ALU.mult).then_inc(self.c["mod_product"], 1)

    def reduce(self, dve, i, slot):
        dve.wait_ge(self.c["mod_product"], self.product0 + i + 1)
        dve.wait_ge(self.c["mod_summed"], self.summed0 + i + 1)
        dve.tensor_reduce(self.acc[:], self.buf[slot][:].rearrange("p k n -> p n k"), AX_X,
                          ALU.add).then_inc(self.c["mod_reduced"], 1)

    def sum(self, pe, i):
        pe.wait_ge(self.c["mod_reduced"], self.reduced0 + i + 3)
        for q in range(2):
            last = pe.matmul(self.sums[:, bass.ds(2 * i + q, 1)],
                             self.acc[:, q * P:(q + 1) * P], self.m.ones[:, 0:1],
                             start=True, stop=True)
        last.then_inc(self.c["mod_summed"], 1)

    def finish(self, dve, coefs):
        n = 2 * self.pieces
        dve.wait_ge(self.c["mod_summed"], self.summed0 + self.pieces + 1)
        bias = self.m.col["b_mod"] + 48 * self.layer + self.first
        chunks = slice(self.first, self.first + n)
        done = self.c.take("mod_biased", 1)
        dve.tensor_tensor(self.m.mod[:, self.layer, chunks, 0], self.sums[:, 0:n],
                          self.m.vt[:, bias:bias + n], ALU.add).then_inc(self.c["mod_biased"], 1)
        dve.wait_ge(self.c["mod_biased"], done + 1)
        coefficients(self.c, self.m, dve, self.layer, coefs)


def coefficients(c, m, dve, layer, which):
    for j in which:
        what, gain = ((1, "g_pre_mix"), (2, "g_post_mix"), (4, "g_pre_ffn"), (5, "g_post_ffn"))[j]
        col = m.col[gain] + KD * layer
        dve.scalar_tensor_tensor(
            out=m.coef[:, layer, j, :], in0=m.mod[:, layer, 8 * what:8 * what + 8, 0],
            scalar=1.0 if j % 2 == 0 else 0.0, in1=m.vt[:, col:col + KD],
            op0=ALU.add, op1=ALU.mult).then_inc(c["coef"], 1)


def halves_parts(m, scale, shift, work=0, squares=8, early=False):
    def part(h):
        s = slice(h * HALF, (h + 1) * HALF)
        return dict(
            source=lambda k: m.x[:, k, s], work=lambda k: m.a[:, work + k, s],
            hi=lambda k: m.xn_hi[:, k, s], lo=lambda k: m.xn_lo[:, k, s],
            scale=scale, shift=shift, tiles=4, stat=m.ps[:, 4, 8 * h:8 * h + 8],
            turned=m.ps[:, 5, h * P:(h + 1) * P], bank=m.ps[:, 6 + h, :], small=4 * h,
            squares=[m.a[:, 16 + i, s] for i in range(squares)])
    parts = [part(0), part(1)]
    if early:
        parts[0].update(work=lambda k: m.yx[:, k, :],
                        squares=[m.a[:, 3 + i, 0:HALF] for i in range(3)],
                        stat=m.ps[:, 4, 16:24], bank=m.ps[:, 5, :], turned=m.ps[:, 4, P:2 * P],
                        small=8)
    return parts


def load_vectors(nc, c, m, ins, after, norm):
    lists = [
        ("b_mod", ins["b_mod"].rearrange("l (k p) -> (l k) p", p=P)),
        ("c", ins["c"].rearrange("b (k p) -> (b k) p", p=P)),
        ("c_ctx", ins["c_ctx"].rearrange("(k p) -> k p", p=P)),
        ("g_pre_mix", ins["g_pre_mix"].rearrange("l (k p) -> (l k) p", p=P)),
        ("g_post_mix", ins["g_post_mix"].rearrange("l (k p) -> (l k) p", p=P)),
        ("g_pre_ffn", ins["g_pre_ffn"].rearrange("l (k p) -> (l k) p", p=P)),
        ("g_post_ffn", ins["g_post_ffn"].rearrange("l (k p) -> (l k) p", p=P)),
        ("b_pool", ins["b_pool"].rearrange("j g (k p) -> (j g k) p", p=P)),
        ("pool_scale", ins["pool_scale"].rearrange("j (k p) -> (j k) p", p=P)),
        ("g_q", ins["g_q"]), ("g_k", ins["g_k"]),
        ("norm1", ins["norm1_gain_2"].rearrange("j (k p) -> (j k) p", p=P)),
        ("norm2", ins["norm2_gain_2"].rearrange("j (k p) -> (j k) p", p=P)),
        ("final", ins["final_norm_gain_2"].rearrange("(k p) -> k p", p=P)),
        ("conv_w0", ins["conv_w"][0].rearrange("w (k p) -> (w k) p", p=P)),
        ("conv_w1", ins["conv_w"][1].rearrange("w (k p) -> (w k) p", p=P)),
        ("conv_b", ins["conv_b"].rearrange("l (k p) -> (l k) p", p=P)),
        ("lru_conv_w", ins["lru_conv_w_2"].rearrange("j w (k p) -> (j w k) p", p=P)),
        ("lru_conv_b", ins["lru_conv_b_2"].rearrange("j (k p) -> (j k) p", p=P)),
        ("gate_a_b", ins["lru_gate_a_b_2"].rearrange("j (k p) -> (j k) p", p=P)),
        ("gate_x_b", ins["lru_gate_x_b_2"].rearrange("j (k p) -> (j k) p", p=P)),
        ("lambda", ins["lru_lambda_2"].rearrange("j (k p) -> (j k) p", p=P)),
        ("lru_norm", ins["lru_norm_gain_2"].rearrange("j (k p) -> (j k) p", p=P)),
        ("ret_norm", ins["ret_norm_gain_2"].rearrange("j (k p) -> (j k) p", p=P)),
        ("ffn_w0", ins["ffn_conv_w_2"][0, 0].rearrange("(k p) -> k p", p=P)),
        ("ffn_w1", ins["ffn_conv_w_2"][0, 1].rearrange("(k p) -> k p", p=P)),
        ("ffn_w2", ins["ffn_conv_w_2"][0, 2].rearrange("(k p) -> k p", p=P)),
        ("ffn_b", ins["ffn_conv_b_2"].rearrange("j (k p) -> (j k) p", p=P)),
    ]
    fill, place = [], {}
    for name, ap in sorted(lists, key=lambda x: -x[1].shape[0]):
        n = ap.shape[0]
        tile = next((i for i, f in enumerate(fill) if f + n <= P), len(fill))
        if tile == len(fill):
            fill.append(0)
        place[name] = (tile, fill[tile], n)
        fill[tile] += n
    tiles = len(fill)
    m.vt = m.vec("vt", [P, tiles * P])
    m.col = {name: tile * P + at for name, (tile, at, n) in place.items()}
    m.ident = m.vec("ident", [P, P])
    m.mod = m.vec("mod", [P, 2, 48, 2])
    m.silu_c = m.vec("silu_c", [P, KD, 2])
    m.eps = m.vec("eps", [P, 1])
    m.ones = m.vec("ones", [P, 1])
    m.rms_sd = m.vec("rms_sd", [P, 96])
    m.rms_rs = m.vec("rms_rs", [P, 96])
    rms_row = m.vec("rms_row", [P, 3, P])
    m.rms_row = [rms_row[:, r, :] for r in range(3)]
    m.rms_rows = rms_row[:, 0, :]
    m.coef = m.vec("coef", [P, 2, 4, KD])
    m.coef_ctx = m.vec("coef_ctx", [P, KD])

    rows_in = m.at("vector_rows", YX, [P, tiles, P])
    x_rows = m.at("x_rows", A0, [P, TT, D])
    ctx_rows = m.at("ctx_rows", A0 + 16 * 4096, [P, 2, D])
    m.ctx_cm = m.at("ctx_cm", A0 + 21 * 4096, [P, KD, CTX])
    wm = m.at("w_mod_slots", XN, [P, 4, KD, HALF])
    x_tiles = ins["x"].rearrange("b (t p) d -> (b t) p d", p=P)
    ctx_tiles = ins["ctx"].rearrange("b (t p) d -> (b t) p d", p=P)
    w_mod = ins["w_mod"].rearrange("l (k p) n -> l p k n", p=P)
    mod_rows = m.at("mod_rows", YX + 8192, [2, 4 * HALF])
    groups = [(x_rows, t, g, m.x) for t in range(TT) for g in (0, 1)]
    groups += [(ctx_rows, t, g, m.ctx_cm) for t in range(2) for g in (0, 1)]

    m.qkv_norm = pre = norm(c, m)

    with nc.Block() as block:
        @block.sync
        def _(sp):
            sp.dma_start(m.ident[:], ins["k_ident"]).then_inc(c["ident_in"], 16)
            def mod_piece(s):
                sp.dma_start(wm[:, s], w_mod[0, :, :, s * HALF:(s + 1) * HALF]
                             ).then_inc(c[f"first_mod_in{s}"], 16)

            for t in range(TT):
                if t == TT // 2:
                    sp.wait_ge(c["rows_in"], 16 * len(lists))
                    mod_piece(0)
                sp.dma_start(x_rows[:, t, :], x_tiles[t]
                             ).then_inc(c["x_in" if t < TT // 2 else "x_in2"], 16)
            mod_piece(1)
            for t in range(2):
                sp.dma_start(ctx_rows[:, t, :], ctx_tiles[t]).then_inc(c["ctx_in"], 16)
            for s in (2, 3):
                mod_piece(s)
            after.load_first(sp)

        @block.gpsimd
        def _(pool):
            pool.memset(m.eps[:], EPS).then_inc(c["consts"], 1)
            pool.memset(m.ones[:], 1.0).then_inc(c["consts"], 1)
            for name in ("w_lo", "unit_done", "down_used", "at_exp", "at_summed", "mod_reduced"):
                pool.sem_inc(c[name], 2)
            for name in ("up_out", "at_max", "at_copied", "at_out_scaled", "mod_summed"):
                pool.sem_inc(c[name], 1)
            for name in ("at_lo", "at_used"):
                pool.sem_inc(c[name], PROBS)
            pool.sem_inc(c["at_added"], KEYS // P - 1)
            after.split_first(pool, 0)

        @block.tensor
        def _(pe):
            pe.wait_ge(c["ident_in"], 16)
            pe.wait_ge(c["rows_in"], 16 * len(lists))
            pe.wait_ge(c["consts"], 2)
            for s in range(tiles):
                last = pe.transpose(m.ps[:, s // 4, (s % 4) * P:(s % 4) * P + fill[s]],
                                    rows_in[0:fill[s], s, :], m.ident[0:fill[s], 0:fill[s]])
            last.then_inc(c["vt_turned"], 1)

            def turns(part):
                pe.wait_ge(c[("x_in", "x_in2", "ctx_in")[part]], 64 if part < 2 else 32)
                for i, (src, t, g, dst) in list(enumerate(groups))[part * TT:(part + 1) * TT]:
                    if i >= 2:
                        pe.wait_ge(c["x_copied"], i - 1)
                    for q in range(4):
                        k = 4 * g + q
                        last = pe.transpose(m.ps[:, 2 + i % 2, q * P:(q + 1) * P],
                                            src[:, t, k * P:(k + 1) * P], m.ident[:])
                    last.then_inc(c["x_turned"], 1)

            def piece(s):
                pe.wait_ge(c[f"first_mod_in{s}"], 16)
                for k in range(KD):
                    last = pe.matmul(m.ps[0:2, 4 + s, :], m.silu_c[:, k, :], wm[:, s, k, :],
                                     start=(k == 0), stop=(k == KD - 1))
                last.then_inc(c["first_mod_out"], 1)

            turns(0)
            pe.wait_ge(c["silu_c"], 2)
            piece(0)
            turns(1)
            piece(1)
            turns(2)
            piece(2)
            pre.rms[0].pe_sums(pe)
            piece(3)
            pre.rms[0].pe_turn(pe)
            pre.rms[1].pe_sums(pe)
            pre.rms[0].pe_broadcast(pe, 0)
            pre.rms[2].pe_sums(pe)
            pre.rms[1].pe_turn(pe)
            pre.rms[1].pe_broadcast(pe, 0)
            pre.rms[2].pe_turn(pe)
            pre.rms[2].pe_broadcast(pe, 0)
            for s in range(4):
                pe.wait_ge(c["first_mod_rows"], s + 1)
                for q in range(4):
                    j = 4 * s + q
                    last = pe.transpose(m.ps[:, 0, 2 * j:2 * j + 2],
                                        mod_rows[0:2, j * P:(j + 1) * P], m.ident[0:2, 0:2])
            last.then_inc(c["first_mod_turned"], 1)

        @block.scalar
        def _(act):
            for name, ap in lists:
                tile, at, n = place[name]
                act.dma_start(rows_in[at:at + n, tile, :], ap).then_inc(c["rows_in"], 16)
            act.wait_ge(c["vt_copied"], tiles)
            for v, name in enumerate(("c", "c_ctx")):
                act.activation(m.silu_c[:, :, v], m.vt[:, m.col[name]:m.col[name] + KD],
                               ACT.Silu).then_inc(c["silu_c"], 1)
            for i, (src, t, g, dst) in enumerate(groups):
                act.wait_ge(c["x_turned"], i + 1)
                act.activation(dst[:, 4 * g:4 * g + 4, t * P:(t + 1) * P],
                               m.ps[:, 2 + i % 2, :].rearrange("p (q t) -> p q t", q=4),
                               ACT.Copy).then_inc(c["x_copied"], 1)
            act.wait_ge(c["x_copied"], len(groups))
            for h in range(3):
                pre.rms[h].act_squares(act)
            for s in range(4):
                if s < 3:
                    pre.rms[s].act_root(act)
                act.wait_ge(c["first_mod_out"], s + 1)
                act.activation(mod_rows[0:2, s * HALF:(s + 1) * HALF], m.ps[0:2, 4 + s, :],
                               ACT.Copy).then_inc(c["first_mod_rows"], 1)

        @block.vector
        def _(dve):
            dve.wait_ge(c["vt_turned"], 1)
            for s in range(tiles):
                dve.tensor_copy(m.vt[:, s * P:s * P + fill[s]],
                                m.ps[:, s // 4, (s % 4) * P:(s % 4) * P + fill[s]]
                                ).then_inc(c["vt_copied"], 1)
            dve.wait_ge(c["x_copied"], len(groups))
            for h in range(3):
                pre.rms[h].dve_sums(dve)
            for h in range(3):
                pre.rms[h].dve_inverse(dve, sums=False)
                pre.rms[h].dve_row(dve)
            for h in range(3):
                pre.dve_scale(dve, h)
            dve.wait_ge(c["vt_copied"], tiles)
            dve.wait_ge(c["first_mod_turned"], 1)
            bias = m.vt[:, m.col["b_mod"]:m.col["b_mod"] + 16]
            dve.tensor_tensor(m.mod[:, 0, 0:16, :],
                              m.ps[:, 0, 0:32].rearrange("p (q v) -> p q v", v=2),
                              bias.unsqueeze(2).to_broadcast([P, 16, 2]),
                              ALU.add).then_inc(c["first_mod_done"], 1)
            dve.wait_ge(c["first_mod_done"], 1)
            coefficients(c, m, dve, 0, [0])
            dve.scalar_tensor_tensor(
                out=m.coef_ctx[:], in0=m.mod[:, 0, 8:16, 1], scalar=1.0,
                in1=m.vt[:, m.col["g_pre_mix"]:m.col["g_pre_mix"] + KD], op0=ALU.add,
                op1=ALU.mult).then_inc(c["coef"], 1)


def mod_col(m, layer, what, k, v=0):
    return m.mod[:, layer, 8 * what + k, v:v + 1]


def vcol(m, name, k):
    return m.vt[:, m.col[name] + k:m.col[name] + k + 1]


def weight_units(w, start, count):
    v = w.rearrange("(k p) n -> p k n", p=P)
    return lambda u: v[:, :, bass.ds(u * P + start, P)]


def unit_half(ws, m, pe, slot, half, pre=None, steps=()):
    s, steps = slice(half * HALF, (half + 1) * HALF), list(steps)
    for k in range(KD):
        if k in (3, 6) and steps:
            steps.pop(0)()
        if pre:
            pre.ready(pe, half, k)
        last = ws.products(pe, slot, m.ps[:, 2 * slot + half, :], k, m.xn_hi[:, k, s],
                           m.xn_lo[:, k, s], k == 0, k == KD - 1)
    for step in steps:
        step()
    return last


def first_units(c, ws, m, pe, pre):
    pre.pe_sums(pe, 0)
    pre.pe_spread(pe, 0)
    ws.ready(pe, 0)
    unit_half(ws, m, pe, 0, 0, pre, pre.pe_steps(pe))
    ws.ready(pe, 1)
    if pre.tail:
        unit_half(ws, m, pe, 1, 0)
        pre.pe_sums(pe, 1)
    else:
        pre.pe_sums(pe, 1)
        unit_half(ws, m, pe, 1, 0)
    pre.pe_spread(pe, 1)
    unit_half(ws, m, pe, 0, 1, pre).then_inc(c["unit_done"], 1)
    for j in range(2, len(pre.parts)):
        pre.pe_sums(pe, j)
    unit_half(ws, m, pe, 1, 1).then_inc(c["unit_done"], 1)
    for j in range(2, len(pre.parts)):
        pre.pe_spread(pe, j)


def project_stage(nc, c, m, name, pre, tail, ws, after, w, units, ctx_from, dest,
                  ctx_dest, beside=None):
    pre.begin(tail)
    beside = beside and beside()
    f0 = c.take("project_copied", units)
    n_ctx = units - ctx_from
    cf0 = c.take("ctx_copied", n_ctx)
    src = weight_units(w, 0, units)
    loop = 4 if beside else ctx_from // 2

    with nc.Block() as block:
        @block.sync
        def _(sp):
            with sp.Fori(1, units // 2) as i:
                for b in range(2):
                    ws.load(sp, 2 * i + b, b, src(2 * i + b))
            if after:
                after.load_first(sp)

        @block.gpsimd
        def _(pool):
            pre.pool(pool, ws)
            if beside:
                beside.pool(pool)
            with pool.Fori(1, units // 2) as i:
                for b in range(2):
                    ws.split(pool, 2 * i + b, i, b, KD)
            if after:
                after.split_first(pool, 0)

        @block.tensor
        def _(pe):
            first_units(c, ws, m, pe, pre)

            def unit(u, b, with_ctx):
                ws.ready(pe, u)
                pe.wait_ge(c["project_copied"], f0 + u - 1)
                for h in range(2):
                    last = unit_half(ws, m, pe, b, h)
                if with_ctx and n_ctx:
                    if u == ctx_from:
                        pre.ready(pe, 2)
                    else:
                        pe.wait_ge(c["ctx_copied"], cf0 + u - ctx_from)
                    for k in range(KD):
                        last = ws.products(pe, b, m.ps[:, 4, 0:CTX], k, m.xnc_hi[:, k, :],
                                           m.xnc_lo[:, k, :], k == 0, k == KD - 1)
                last.then_inc(c["unit_done"], 1)

            with pe.Fori(1, loop) as i:
                for b in range(2):
                    unit(2 * i + b, b, False)
            for u in range(2 * loop, units):
                unit(u, u % 2, True)
                if beside:
                    beside.pe(pe, u)

        @block.scalar
        def _(act):
            pre.act(act)
            if tail:
                act.wait_ge(c["x_stored"], c.reached["x_stored"])

            def copy(u, b):
                ws.finished(act, u)
                stand_alone(act, c)
                act.activation(dest(u), m.ps[:, 2 * b:2 * b + 2, :].rearrange("p b t -> p (b t)"),
                               ACT.Copy).then_inc(c["project_copied"], 1)

            with act.Fori(0, loop) as i:
                for b in range(2):
                    copy(2 * i + b, b)
            if beside:
                act.wait_ge(c["project_copied"], f0 + 8)
                beside.begin(act)
            for u in range(2 * loop, units):
                copy(u, u % 2)
                if n_ctx:
                    act.activation(ctx_dest(u), m.ps[:, 4, 0:CTX], ACT.Copy
                                   ).then_inc(c["ctx_copied"], 1)
                if beside:
                    beside.act(act, u)

        @block.vector
        def _(dve):
            pre.dve(dve)
            if beside:
                beside.dve(dve)


def ffn_up_stage(nc, c, m, name, pre, tail, ws, after, w, ff, conv_w, conv_b, causal, mod=None):
    pre.begin(tail)
    out0 = c.take("up_out", ff)
    steps = 2 if causal else 1
    i0 = c.take("up_centre", steps * ff)
    s0 = c.take("up_side", 2 * steps * ff)
    act0 = c.take("up_act", ff)
    wv = w.rearrange("(k p) n -> p k n", p=P)
    work = m.at(f"{name}_work", YX, [P, 2, T])
    gate_work, value_work = work[:, 0, :], work[:, 1, :]
    banks = m.ps[:].rearrange("p b t -> p (b t)")
    gate_ps, value_ps = banks[:, 0:T], banks[:, T:2 * T]
    if causal:
        centre, sides = 2, [(slice(0, T - 2), slice(2, T), 0), (slice(0, T - 1), slice(1, T), 1)]
    else:
        centre, sides = 1, [(slice(0, T - 1), slice(1, T), 0), (slice(1, T), slice(0, T - 1), 2)]

    def chunks(eng, body):
        with eng.Fori(0, ff // 2 - 1) as i:
            body(2 * i + 1, i, 1)
            body(2 * i + 2, i + 1, 0)
        body(ff - 1, ff // 2 - 1, 1)

    with nc.Block() as block:
        @block.sync
        def _(sp):
            def chunk(j, pair, odd):
                for b in range(2):
                    ws.load(sp, 2 * j + b, b, wv[:, :, bass.ds(j * P + b * ff * P, P)])
                if mod:
                    mod.load(sp, j + 2, odd)

            if mod:
                pre.ready(sp, 1)
                for i in range(3):
                    mod.load(sp, i, i % 2)
            chunks(sp, chunk)
            after.load_first(sp)

        @block.gpsimd
        def _(pool):
            pre.pool(pool, ws)

            def chunk(j, pair, odd):
                for b in range(2):
                    ws.split(pool, 2 * j + b, j, b, KD)
                if mod:
                    mod.product(pool, pair + 1, odd)

            if mod:
                for i in range(3):
                    mod.product(pool, i // 2, i % 2)
            chunks(pool, chunk)
            after.split_first(pool, 0)

        @block.tensor
        def _(pe):
            first_units(c, ws, m, pe, pre)
            if mod:
                for i in range(2):
                    mod.sum(pe, i)

            def chunk(j, pair, odd):
                for b in range(2):
                    ws.ready(pe, 2 * j + b)
                    if causal or b == 0:
                        pe.wait_ge(c["up_side"], 2 * steps * j + s0 - 2 * steps + 2 * b + 2)
                    else:
                        pe.wait_ge(c["up_out"], out0 + j + 1)
                    for h in range(2):
                        last = unit_half(ws, m, pe, b, h)
                    last.then_inc(c["unit_done"], 1)
                if mod:
                    mod.sum(pe, j + 1)

            chunks(pe, chunk)
            if mod:
                mod.sum(pe, ff + 1)

        @block.scalar
        def _(act):
            pre.act(act)

            def chunk(j, pair=None, odd=None):
                ws.finished(act, 2 * j)
                act.wait_ge(c["up_out"], out0 + j + 1)
                stand_alone(act, c)
                act.activation(gate_work, gate_ps, ACT.Identity, bias=conv_b(j),
                               scale=conv_w(centre, j)).then_inc(c["up_centre"], 1)
                if causal:
                    ws.finished(act, 2 * j + 1)
                    stand_alone(act, c)
                    act.activation(value_work, value_ps, ACT.Identity, bias=conv_b(j + ff),
                                   scale=conv_w(centre, j + ff)).then_inc(c["up_centre"], 1)
                act.wait_ge(c["up_side"], 2 * steps * j + s0 + 2)
                act.activation(gate_work, gate_work, ACT.Gelu_apprx_tanh if causal else ACT.Silu
                               ).then_inc(c["up_act"], 1)

            chunk(0)
            chunks(act, chunk)

        @block.vector
        def _(dve):
            pre.dve(dve)
            dve.wait_ge(c["x_stored"], c.reached["x_stored"])

            def neighbours(j, part, target, source, chunk):
                dve.wait_ge(c["up_centre"], steps * j + i0 + part + 1)
                for n, (src, dst, tap) in enumerate(sides):
                    if n:
                        dve.wait_ge(c["up_side"], 2 * steps * j + s0 + 2 * part + 1)
                    last = dve.scalar_tensor_tensor(
                        out=target[:, dst], in0=source[:, src], scalar=conv_w(tap, chunk),
                        in1=target[:, dst], op0=ALU.mult, op1=ALU.add)
                    last.then_inc(c["up_side"], 1)

            def chunk(j, pair=None, odd=None):
                neighbours(j, 0, gate_work, gate_ps, j)
                if causal:
                    neighbours(j, 1, value_work, value_ps, j + ff)
                    dve.wait_ge(c["up_side"], 2 * steps * j + s0 + 4)
                dve.wait_ge(c["up_act"], act0 + j + 1)
                if causal:
                    dve.tensor_tensor(m.a[:, bass.ds(j, 1), :].rearrange("p o t -> p (o t)"),
                                      gate_work, value_work, ALU.mult
                                      ).then_inc(c["up_out"], 1)
                else:
                    ws.finished(dve, 2 * j + 1)
                    dve.tensor_tensor(m.a[:, bass.ds(j, 1), :].rearrange("p o t -> p (o t)"),
                                      gate_work, value_ps, ALU.mult
                                      ).then_inc(c["up_out"], 1)
                if mod and pair is not None:
                    mod.reduce(dve, j + 2, odd)

            if mod:
                for i in range(3):
                    mod.reduce(dve, i, i % 2)
            chunk(0)
            chunks(dve, chunk)
            if mod:
                mod.finish(dve, range(4))


def down_stage(nc, c, m, name, chunks, groups, ws, after, early, source, kmap, evac, post, x_dram,
               x_load, x_store):
    ng = len(groups)
    units = 2 * KD * ng
    h0, l0 = c.take("down_hi", 2 * chunks), c.take("down_lo", 2 * chunks)
    f0 = c.take("down_used", 2 * KD)
    xl0 = c.take("x_loaded", 32 if x_load else 0)
    c.take("x_stored", 32 if x_store else 0)
    rx0 = c.take("x_scaled", 2 * KD if post else 0)
    nx0 = c.take("x_new", 2 * KD)
    pairs = KD // 2
    per = 2 * ng

    def y(half, n):
        return m.yx[:, n, :] if half == 0 else m.a[:, 16 + n, 0:HALF]

    def x(half, k):
        return m.x[:, k, half * HALF:(half + 1) * HALF]

    def slot(half, k):
        return m.ring[:, (half * chunks + k) % 32, :]

    def lo(half, k):
        return m.a_lo[k // 8][:, k % 8, half * HALF:(half + 1) * HALF]

    def full(half, k):
        return m.a[:, k, half * HALF:(half + 1) * HALF]

    rms = []
    if post:
        for h, places in enumerate(((0, 1, 2), (6, 7, 0, 1, 2))):
            squares = [m.a[:, i, 0:HALF] for i in places]
            rms.append(RootMeanSquare(c, m, f"{name}{h}", 1, KD, 4, D,
                                      (lambda hh: lambda k: y(hh, k))(h), squares,
                                      m.ps[:, 4, 8 * h:8 * h + 8], m.ps[:, 5, h * P:(h + 1) * P],
                                      [m.ps[:, 6 + h, :]], 4 * h))
    first, second = [
        Residual(c, m, rms[h] if post else None, (lambda hh: lambda k: y(hh, k))(h),
                 (lambda hh: lambda k: x(hh, k))(h), post, f0 + (h + 1) * KD + 2,
                 xl0 + 16 * (h + 1) if x_load else None, rx0 + h * KD, nx0 + h * KD,
                 x_dram[:, :, HALF:T] if x_store else None) for h in range(2)]
    early_rms = early.rms[0]
    post_at = (0, 1, 2)
    if post:
        early_at = (4, 5, 6) if chunks <= KD else (3, 4, 5)
    else:
        early_at = (3, 4, 5) if chunks <= KD else (1, 2, 3)

    with nc.Block() as block:
        @block.sync
        def _(sp):
            def pair(half, i, first=0):
                for b in range(2):
                    for g in range(ng):
                        n = b * ng + g
                        if n < first:
                            continue
                        ws.load(sp, per * i + half * KD * ng + n, n % 2, source(i, b, g))

            if not ws.loaded:
                ws.load_first(sp)
            pair(0, 0, 2)
            with sp.Fori(1, pairs) as i:
                pair(0, i)
            pair(1, 0)
            if x_load:
                ws.finished(sp, units // 2 - 1)
                sp.dma_start(m.x[:, :, 0:HALF], x_dram[:, :, 0:HALF]).then_inc(c["x_loaded"], 16)
            with sp.Fori(1, pairs) as i:
                pair(1, i)
            if after:
                after.load_first(sp)
            if x_load:
                ws.finished(sp, units - 1)
                sp.wait_ge(c["x_loaded"], xl0 + 16)
                sp.dma_start(m.x[:, :, HALF:T], x_dram[:, :, HALF:T]).then_inc(c["x_loaded"], 16)
            if x_store:
                sp.wait_ge(c["x_new"], nx0 + KD)
                sp.dma_start(x_dram[:, :, 0:HALF], m.x[:, :, 0:HALF]).then_inc(c["x_stored"], 16)

        @block.gpsimd
        def _(pool):
            def pair(half, i, first=0):
                for b in range(2):
                    for g in range(ng):
                        n = b * ng + g
                        if n < first:
                            continue
                        ws.split(pool, per * i + half * KD * ng + n,
                                 ng * i + half * KD * ng // 2 + n // 2, n % 2, groups[g])

            if not ws.divided:
                ws.split_first(pool, 0)
            ws.split_first(pool, 1)
            pair(0, 0, 2)
            with pool.Fori(1, pairs) as i:
                pair(0, i)
            with pool.Fori(0, pairs) as i:
                pair(1, i)
            if after:
                after.split_first(pool, 0)

        @block.tensor
        def _(pe):
            def chunk(half, i, b, bank, waits):
                k = 0
                first = kmap(i, b)
                for g in range(ng):
                    n = b * ng + g
                    ws.ready(pe, per * i + half * KD * ng + n)
                    for q in range(groups[g]):
                        kk = first + k
                        if waits:
                            pe.wait_ge(c["down_lo"], l0 + half * chunks + kk + 1)
                        last = ws.products(pe, n % 2, m.ps[:, bank, :], q, slot(half, kk),
                                           lo(half, kk), k == 0, k == sum(groups) - 1)
                        k += 1
                    last.then_inc(c["unit_done"], 1)

            def first_half(i, waits):
                for b in range(2):
                    pe.wait_ge(c["down_used"], 2 * i + f0 + b + 1)
                    chunk(0, i, b, b, waits)

            looped = sum(groups) == chunks
            first_half(0, True)
            if looped:
                with pe.Fori(1, pairs) as i:
                    first_half(i, False)
            else:
                for i in range(1, pairs):
                    first_half(i, True)
            for n in range(KD):
                if n < 2:
                    pe.wait_ge(c["down_used"], f0 + KD + n + 1)
                elif n >= 4:
                    pe.wait_ge(c["down_used"], f0 + KD + n - 1)
                chunk(1, n // 2, n % 2, n % 4, n == 0 or not looped)
                if post and n == post_at[0]:
                    rms[0].pe_sums(pe)
                if post and n == post_at[1]:
                    rms[0].pe_turn(pe)
                if post and n == post_at[2]:
                    rms[0].pe_broadcast(pe, 0)
                if n == early_at[0]:
                    early_rms.pe_sums(pe)
                if n == early_at[1]:
                    early_rms.pe_turn(pe)
                if n == early_at[2]:
                    early_rms.pe_broadcast(pe, 0)

        @block.scalar
        def _(act):
            def splits(half):
                for k in range(chunks):
                    if half and chunks + k >= 32:
                        ws.finished(act, units // 2 - 1)
                    act.activation(slot(half, k), full(half, k), ACT.Copy
                                   ).then_inc(c["down_hi"], 1)

            def copy(half, i, b, bank):
                ws.finished(act, per * i + half * KD * ng + b * ng + ng - 1)
                stand_alone(act, c)
                if half == 0:
                    dst = m.yx[:, bass.ds(2 * i + b, 1), :].rearrange("p o t -> p (o t)")
                else:
                    dst = y(1, 2 * i + b)
                if evac is None:
                    act.activation(dst, m.ps[:, bank, :], ACT.Copy).then_inc(c["down_used"], 1)
                else:
                    scale, bias = evac
                    act.activation(dst, m.ps[:, bank, :], ACT.Identity, bias=bias(2 * i + b),
                                   scale=scale(2 * i + b)).then_inc(c["down_used"], 1)

            def early_squares():
                early_rms.act_squares(act, lambda k: act.wait_ge(c["x_new"], nx0 + k + 1))

            splits(0)
            with act.Fori(0, pairs) as i:
                for b in range(2):
                    copy(0, i, b, b)
            splits(1)
            act.wait_ge(c["down_used"], f0 + KD + 2)
            ws.finished(act, units // 2 - 1)
            if post:
                rms[0].act_squares(act)
            else:
                early_squares()
            for n in range(KD):
                copy(1, n // 2, n % 2, n % 4)
                if post and n == post_at[0]:
                    rms[0].act_root(act)
                if post:
                    rms[1].act_squares(act, lambda k: act.wait_ge(c["down_used"],
                                                                  f0 + KD + k + 3), [n])
                if post and n == post_at[2]:
                    early_squares()
                if n == early_at[0]:
                    early_rms.act_root(act)
                if n == early_at[2]:
                    early.act_shift(act, 0)

        @block.vector
        def _(dve):
            for half in range(2):
                for k in range(chunks):
                    dve.wait_ge(c["down_hi"], h0 + half * chunks + k + 1)
                    dve.tensor_tensor(lo(half, k), full(half, k), slot(half, k).bitcast(F32),
                                      ALU.subtract).then_inc(c["down_lo"], 1)
            if post:
                rms[0].dve_inverse(dve)
                rms[0].dve_row(dve)
            first.dve(dve)
            early_rms.dve_inverse(dve)
            early_rms.dve_row(dve)
            if post:
                rms[1].dve_sums(dve, range(1, 6))
            first.wait(dve, KD - 1)
            early.dve_scale(dve, 0)
            if post:
                rms[1].dve_sums(dve, range(6, KD))

    return second


def two(ap, n=2):
    return ap.rearrange("p (a t) -> p a t", a=n)


def attention_memory(m):
    m.kh = m.at("k_hi", XN, [P, KV, KEYS], F32R)
    m.kl = m.at("k_lo", XN + 10240, [P, KV, KEYS], F32R)
    m.vh = m.at("v_hi", XN + 20480, [P, KEYS // P, KV * P], F32R)
    m.vl = m.at("v_lo", XN + 30720, [P, KEYS // P, KV * P], F32R)
    m.qh = m.at("q_hi", XN + 40960, [P, 2, HALF], F32R)
    m.ql = m.at("q_lo", XN + 45056, [P, 2, HALF], F32R)
    m.ph = m.at("probs_hi", XN + 49152, [P, PROBS, HALF], F32R)
    m.neg_row = m.at("negative_maxima", XN + 59392, [1, 2, HALF], F32R)
    m.ones_row = m.at("ones_row", XN + 63488, [1, P], F32R)
    m.pl = m.at("probs_lo", A0 + 20 * 4096, [P, PROBS, HALF], F32R)
    m.probs = m.at("probs", YX, [P, PROBS, HALF])
    m.added = m.at("probs_added", YX + 10240, [P, 2, HALF])
    m.kv_raw = m.at("kv_raw", A0 + 16 * 4096, [P, 2 * KV, KEYS])
    m.mod_buf = [m.at(f"mod_buf{s}", A0 + (16 + 2 * s) * 4096, [P, KD, 2 * P]) for s in (0, 1)]


def rotate_stage(nc, c, m, ins):
    table = m.at("rope_tables", W_RAW, [P, 6, T])
    cos, sin = table[:, 0, :], table[:, 1, :]
    depth = 4
    tmp = m.at("rope_tmp", XN + 40960, [P, 2 * depth, HALF])
    direct, swapped = tmp[:, 0:depth, :], tmp[:, depth:2 * depth, :]
    sq = m.at("rope_squares", YX + 8192, [P, 3, HALF])
    perm = m.at("rope_perm", YX + 8192 + 6144, [P, P])
    items = []
    for h in range(HEADS):
        for half in range(2):
            s = slice(half * HALF, (half + 1) * HALF)
            items.append(("q", h, s, m.a[:, h, s]))
    for h in range(KV):
        for half in range(2):
            s = slice(half * HALF, (half + 1) * HALF)
            items.append(("k", h, s, m.kv_raw[:, h, CTX + half * HALF:CTX + (half + 1) * HALF]))
    items.append(("ctx", 0, None, m.kv_raw[:, 0:KV, 0:CTX]))
    n_rot = len(items) - 1
    n_k = 2 * KV + 1
    rms = RootMeanSquare(c, m, "qk", len(items), 1, 4, P, lambda i: items[i][3],
                         [sq[:, i, :] for i in range(3)], m.ps[:, 4, :], m.ps[:, 5, :],
                         [m.ps[:, b, :] for b in (6, 7, 2, 3)], 0)
    sw0 = c.take("rope_swapped", n_rot)
    dir0 = c.take("rope_direct", n_rot)
    sin0 = c.take("rope_sin", n_rot)
    sum0 = c.take("rope_sum", n_rot)
    out0 = c.take("rope_out", len(items))
    kh0, kl0 = c.take("rope_k_hi", n_k), c.take("rope_k_lo", n_k)
    vt0, vh0, vl0 = c.take("v_turned", 5), c.take("v_hi_done", 5), c.take("v_lo_done", 5)

    with nc.Block() as block:
        @block.sync
        def _(sp):
            sp.dma_start(perm[:], ins["k_perm1"]).then_inc(c["rope_perm_in"], 16)
            sp.dma_start(cos, ins["k_cos1"]).then_inc(c["rope_in"], 16)
            sp.dma_start(sin, ins["k_sin1"]).then_inc(c["rope_in"], 16)

        @block.tensor
        def _(pe):
            pe.wait_ge(c["rope_perm_in"], 16)
            for i, name in enumerate(("g_q", "g_k")):
                last = pe.matmul(m.ps[:, 3, i:i + 1], perm[:], vcol(m, name, 0),
                                 start=True, stop=True)
            last.then_inc(c["gains_swapped"], 1)
            rms.pe_sums(pe)
            rms.pe_turn(pe)
            pe.wait_ge(c["gains_copied"], 1)
            for g in range(5):
                if g >= 2:
                    pe.wait_ge(c["v_lo_done"], vl0 + g - 1)
                for q in range(4):
                    kt, v = 2 * g + q // 2, q % 2
                    last = pe.transpose(m.ps[:, 2 + g % 2, q * P:(q + 1) * P],
                                        m.kv_raw[:, KV + v, kt * P:(kt + 1) * P], m.ident[:])
                last.then_inc(c["v_turned"], 1)
            for g, (kind, h, s, src) in enumerate(items):
                if kind != "ctx":
                    if g >= 2:
                        pe.wait_ge(c["rope_sin"], sin0 + g - 1)
                    pe.matmul(m.ps[:, g % 2, :], perm[:], src, start=True, stop=True
                              ).then_inc(c["rope_swapped"], 1)
                if g == 2:
                    pe.wait_ge(c["v_lo_done"], vl0 + 5)
                rms.pe_broadcast(pe, g)

        @block.scalar
        def _(act):
            rms.act_squares(act)
            rms.act_root(act)
            for g in range(5):
                act.wait_ge(c["v_turned"], vt0 + g + 1)
                act.activation(m.vh[:, 2 * g:2 * g + 2, :], two(m.ps[:, 2 + g % 2, :]), ACT.Copy
                               ).then_inc(c["v_hi_done"], 1)
            for i in range(n_k):
                g = 2 * HEADS + i
                act.wait_ge(c["rope_out"], out0 + g + 1)
                kind, h, s, src = items[g]
                if kind == "k":
                    dst = m.kh[:, h, CTX + s.start:CTX + s.stop]
                    act.activation(dst, direct[:, g % depth, :], ACT.Copy
                                   ).then_inc(c["rope_k_hi"], 1)
                else:
                    act.activation(m.kh[:, :, 0:CTX], two(direct[:, g % depth, :]), ACT.Copy
                                   ).then_inc(c["rope_k_hi"], 1)

        @block.gpsimd
        def _(pool):
            def add(g):
                pool.wait_ge(c["rope_direct"], dir0 + g + 1)
                pool.wait_ge(c["rope_sin"], sin0 + g + 1)
                pool.tensor_tensor(swapped[:, g % depth, :], direct[:, g % depth, :],
                                   swapped[:, g % depth, :], ALU.add).then_inc(c["rope_sum"], 1)

            pool.wait_ge(c["rope_tables"], 4)
            for g, (kind, h, s, src) in enumerate(items[:n_rot]):
                if g >= depth:
                    pool.wait_ge(c["rope_out"], out0 + g - depth + 1)
                if g >= 2 * HEADS + depth:
                    pool.wait_ge(c["rope_k_lo"], kl0 + g - 2 * HEADS - depth + 1)
                which = 2 if kind == "q" else 4
                pool.tensor_tensor(direct[:, g % depth, :], src, table[:, which, s], ALU.mult
                                   ).then_inc(c["rope_direct"], 1)
                if g:
                    add(g - 1)
            add(n_rot - 1)

        @block.vector
        def _(dve):
            dve.wait_ge(c["gains_swapped"], 1)
            dve.tensor_copy(m.gains_sw[:], m.ps[:, 3, 0:2]).then_inc(c["gains_copied"], 1)
            dve.wait_ge(c["rope_in"], 32)
            dve.wait_ge(c["gains_copied"], 1)
            for i, name in enumerate(("g_q", "g_k")):
                dve.tensor_scalar(table[:, 2 + 2 * i, :], cos, vcol(m, name, 0), None, ALU.mult
                                  ).then_inc(c["rope_tables"], 1)
                dve.tensor_scalar(table[:, 3 + 2 * i, :], sin, m.gains_sw[:, i:i + 1], None,
                                  ALU.mult).then_inc(c["rope_tables"], 1)
            dve.wait_ge(c["rope_tables"], 4)
            rms.dve_inverse(dve)
            rms.dve_row(dve)
            for g in range(5):
                dve.wait_ge(c["v_hi_done"], vh0 + g + 1)
                dve.tensor_tensor(m.vl[:, 2 * g:2 * g + 2, :], two(m.ps[:, 2 + g % 2, :]),
                                  m.vh[:, 2 * g:2 * g + 2, :].bitcast(F32), ALU.subtract
                                  ).then_inc(c["v_lo_done"], 1)

            def sine(g):
                kind, h, s, src = items[g]
                which = 3 if kind == "q" else 5
                dve.wait_ge(c["rope_swapped"], sw0 + g + 1)
                dve.tensor_tensor(swapped[:, g % depth, :], m.ps[:, g % 2, :],
                                  table[:, which, s], ALU.mult).then_inc(c["rope_sin"], 1)

            def finish(g):
                kind, h, s, src = items[g]
                bank = rms.ready(dve, g)
                if kind == "ctx":
                    dve.wait_ge(c["rope_k_lo"], kl0 + g - 2 * HEADS - depth + 1)
                    dve.scalar_tensor_tensor(out=two(direct[:, g % depth, :]), in0=src,
                                             scalar=vcol(m, "g_k", 0), in1=two(bank),
                                             op0=ALU.mult, op1=ALU.mult
                                             ).then_inc(c["rope_out"], 1)
                else:
                    dve.wait_ge(c["rope_sum"], sum0 + g + 1)
                    dst = src if kind == "q" else direct[:, g % depth, :]
                    dve.tensor_tensor(dst, swapped[:, g % depth, :], bank, ALU.mult
                                      ).then_inc(c["rope_out"], 1)
                if kind != "q":
                    i = g - 2 * HEADS
                    dve.wait_ge(c["rope_k_hi"], kh0 + i + 1)
                    if kind == "k":
                        cols = slice(CTX + s.start, CTX + s.stop)
                        dve.tensor_tensor(m.kl[:, h, cols], direct[:, g % depth, :],
                                          m.kh[:, h, cols].bitcast(F32), ALU.subtract
                                          ).then_inc(c["rope_k_lo"], 1)
                    else:
                        dve.tensor_tensor(m.kl[:, :, 0:CTX], two(direct[:, g % depth, :]),
                                          m.kh[:, :, 0:CTX].bitcast(F32), ALU.subtract
                                          ).then_inc(c["rope_k_lo"], 1)
                dve.wait_ge(c["rope_out"], out0 + g + 1)
                dve.sem_inc(c["rms_broadcast_used"], 1)

            for g in range(n_rot + 2):
                if g < n_rot:
                    sine(g)
                if g >= 2:
                    finish(g - 2)
            finish(n_rot)


def attention_stage(nc, c, m, mod, after):
    flat = m.ps[:].rearrange("p b t -> p (b t)")
    kt_n = KEYS // P
    adds = kt_n - 1
    lag = 3
    max_at = {0: 0, 2: 1, 4: 2, 6: 3}
    out_ps, scale_ps = m.ps[:, 5, :], m.ps[:, 6, :]
    sum_ps, turned_ps = m.ps[:, 7, 64:68], m.ps[0:4, 7, 128:256]

    def following(g, h, half):
        return (g, h, 1) if half == 0 else (g, h + 1, 0)

    def number(item):
        g, h, half = item
        return h * 2 + (8 * g + half)

    def head(item, ap):
        g, h, half = item
        return ap[:, bass.ds(h + GROUP * g, 1), half * HALF:(half + 1) * HALF].rearrange(
            "p o t -> p (o t)")

    def all_items(eng, body, last_of_all):
        for g in range(KV):
            prev_head = (g, -1, 1) if g == 0 else (0, GROUP - 1, 1)
            body((g, 0, 0), prev_head if g else None, (g, 0, 1))
            body((g, 0, 1), (g, 0, 0), (g, 1, 0))
            with eng.Fori(1, GROUP - 1) as h:
                body((g, h, 0), (g, h - 1, 1), (g, h, 1))
                body((g, h, 1), (g, h, 0), (g, h + 1, 0))
            h = GROUP - 1
            body((g, h, 0), (g, h - 1, 1), (g, h, 1))
            body((g, h, 1), (g, h, 0), (g + 1, 0, 0) if g + 1 < KV else None)
        last_of_all((KV - 1, GROUP - 1, 1))

    with nc.Block() as block:
        @block.sync
        def _(sp):
            def body(item, prev, following):
                mod.load(sp, number(item), item[2])

            after.load_first(sp)
            all_items(sp, body, lambda item: None)

        @block.tensor
        def _(pe):
            def scores(item, kt):
                g, h, half = item
                n = number(item)
                out = m.ps[:, 3 + kt % 2, :]
                pe.wait_ge(c["at_exp"], n * kt_n + (kt + 1))
                if kt == 0:
                    pe.wait_ge(c["at_q_lo"], n + 1)
                ks = slice(kt * P, (kt + 1) * P)
                pe.matmul(out, m.kh[:, g, ks], m.qh[:, half, :], start=True, stop=False)
                pe.matmul(out, m.kh[:, g, ks], m.ql[:, half, :], start=False, stop=False)
                pe.matmul(out, m.kl[:, g, ks], m.qh[:, half, :], start=False, stop=False)
                if kt == 0:
                    pe.wait_ge(c["at_row"], n + 1)
                pe.matmul(out, m.ones_row[:], m.neg_row[:, half, :], start=False, stop=True
                          ).then_inc(c["at_scores"], 1)

            def maxima(item, qi):
                g, h, half = item
                n = number(item)
                if qi == 0:
                    pe.wait_ge(c["at_q_hi"], n + 1)
                pe.wait_ge(c["at_max"], n * 4 + (qi + 1))
                for k0, k1 in ((0, 512), (512, 1024), (1024, 1280)):
                    last = pe.matmul(flat[:, k0:k1], m.qh[:, half, qi * P:(qi + 1) * P],
                                     m.kh[:, g, k0:k1], start=True, stop=True)
                last.then_inc(c["at_max_scores"], 1)

            def turn_maxima(item):
                pe.wait_ge(c["at_max"], number(item) * 4 + 5)
                for qi in range(4):
                    last = pe.transpose(m.ps[0:1, 0, qi * P:(qi + 1) * P],
                                        m.at_max[:, qi:qi + 1], m.ident[:])
                last.then_inc(c["at_max_turned"], 1)

            def values(item, kt):
                g, h, half = item
                n = number(item)
                pe.wait_ge(c["at_lo"], n * kt_n + (kt + 1 + PROBS))
                if kt == 0:
                    pe.wait_ge(c["at_copied"], n + 1)
                vs, slot = slice(g * P, (g + 1) * P), kt % PROBS
                pe.matmul(out_ps, m.vh[:, kt, vs], m.ph[:, slot, :], start=(kt == 0), stop=False)
                pe.matmul(out_ps, m.vh[:, kt, vs], m.pl[:, slot, :], start=False, stop=False)
                pe.matmul(out_ps, m.vl[:, kt, vs], m.ph[:, slot, :], start=False,
                          stop=(kt == kt_n - 1)).then_inc(c["at_used"], 1)

            def sums(item):
                pe.wait_ge(c["at_added"], number(item) * adds + 2 * adds)
                for qi in range(4):
                    last = pe.matmul(sum_ps[:, qi:qi + 1],
                                     m.added[:, item[2], qi * P:(qi + 1) * P], m.ones[:, 0:1],
                                     start=True, stop=True)
                last.then_inc(c["at_summed"], 1)

            def turn_inverse(item):
                pe.wait_ge(c["at_inverse"], number(item) + 1)
                pe.transpose(turned_ps, m.at_inv[:], m.ident[:]).then_inc(c["at_inv_turned"], 1)

            def broadcast(item):
                n = number(item)
                pe.wait_ge(c["at_inv_rows"], n + 1)
                pe.wait_ge(c["at_out_scaled"], n + 1)
                for qi in range(4):
                    last = pe.matmul(scale_ps[:, qi * P:(qi + 1) * P],
                                     m.ident[0:4, qi:qi + 1].to_broadcast([4, P]),
                                     m.at_rows[0:4, :], start=True, stop=True)
                last.then_inc(c["at_scales"], 1)

            def body(item, prev, following):
                for kt in range(kt_n):
                    scores(item, kt)
                    if kt >= lag:
                        values(item, kt - lag)
                    elif prev:
                        values(prev, kt_n - lag + kt)
                    if following and kt in max_at:
                        maxima(following, max_at[kt])
                    if following and kt == 8:
                        turn_maxima(following)
                    if prev and kt == 1:
                        mod.sum(pe, number(prev))
                    if prev and kt == 3:
                        sums(prev)
                    if prev and kt == 5:
                        turn_inverse(prev)
                    if prev and kt == 8:
                        broadcast(prev)

            def end(item):
                for kt in range(kt_n - lag, kt_n):
                    values(item, kt)
                mod.sum(pe, number(item))
                sums(item)
                turn_inverse(item)
                broadcast(item)

            pe.wait_ge(c["at_ones"], 1)
            for qi in range(4):
                maxima((0, 0, 0), qi)
            turn_maxima((0, 0, 0))
            all_items(pe, body, end)

        @block.scalar
        def _(act):
            def q(item):
                act.activation(m.qh[:, item[2], :], head(item, m.a), ACT.Copy
                               ).then_inc(c["at_q_hi"], 1)

            def exps(item, kt):
                n, slot = number(item), kt % PROBS
                act.wait_ge(c["at_scores"], n * kt_n + (kt + 1))
                act.wait_ge(c["at_lo"], n * kt_n + (kt + 1))
                before = kt + 5 if kt < PROBS else adds + max(kt - PROBS, 1)
                act.wait_ge(c["at_added"], n * adds + before)
                act.activation(m.probs[:, slot, :], m.ps[:, 3 + kt % 2, :], ACT.Exp,
                               scale=ATT_SCALE).then_inc(c["at_exp"], 1)

            def highs(item, kt):
                n, slot = number(item), kt % PROBS
                act.wait_ge(c["at_used"], n * kt_n + (kt + 1))
                act.wait_ge(c["at_exp"], n * kt_n + (kt + 3))
                act.activation(m.ph[:, slot, :], m.probs[:, slot, :], ACT.Copy
                               ).then_inc(c["at_hi"], 1)

            def negated(item):
                act.wait_ge(c["at_max_turned"], number(item) + 1)
                act.activation(m.neg_row[:, item[2], :], m.ps[0:1, 0, :], ACT.Copy, scale=-1.0
                               ).then_inc(c["at_row"], 1)

            def copy(item):
                act.wait_ge(c["at_used"], number(item) * kt_n + (kt_n + PROBS))
                stand_alone(act, c)
                act.activation(head(item, m.a), out_ps, ACT.Copy).then_inc(c["at_copied"], 1)

            def body(item, prev, following):
                for kt in range(kt_n):
                    if following and kt == 0:
                        q(following)
                    exps(item, kt)
                    highs(item, kt)
                    if prev and kt == lag - 1:
                        copy(prev)
                    if following and kt == 8:
                        negated(following)

            act.activation(m.ones_row[:], m.ident[0:1, :], ACT.Identity, bias=m.ones[0:1, 0:1],
                           scale=0.0).then_inc(c["at_ones"], 1)
            q((0, 0, 0))
            negated((0, 0, 0))
            all_items(act, body, copy)

        @block.vector
        def _(dve):
            def q(item):
                dve.wait_ge(c["at_q_hi"], number(item) + 1)
                dve.tensor_tensor(m.ql[:, item[2], :], head(item, m.a),
                                  m.qh[:, item[2], :].bitcast(F32), ALU.subtract
                                  ).then_inc(c["at_q_lo"], 1)

            def maxima(item, qi):
                dve.wait_ge(c["at_max_scores"], number(item) * 4 + (qi + 1))
                dve.tensor_reduce(m.at_max[:, qi:qi + 1], flat[:, 0:KEYS], AX_X, ALU.max
                                  ).then_inc(c["at_max"], 1)

            def lows(item, kt):
                n, slot = number(item), kt % PROBS
                dve.wait_ge(c["at_hi"], n * kt_n + (kt + 1))
                dve.tensor_tensor(m.pl[:, slot, :], m.probs[:, slot, :],
                                  m.ph[:, slot, :].bitcast(F32), ALU.subtract
                                  ).then_inc(c["at_lo"], 1)

            def inverse(item):
                dve.wait_ge(c["at_summed"], number(item) + 3)
                dve.reciprocal(m.at_inv[:], sum_ps).then_inc(c["at_inverse"], 1)

            def rows(item):
                dve.wait_ge(c["at_inv_turned"], number(item) + 1)
                dve.tensor_copy(m.at_rows[0:4, :], turned_ps).then_inc(c["at_inv_rows"], 1)

            def scaled(item):
                dve.wait_ge(c["at_scales"], number(item) + 1)
                dve.wait_ge(c["at_copied"], number(item) + 2)
                dve.tensor_tensor(head(item, m.a), head(item, m.a), scale_ps, ALU.mult
                                  ).then_inc(c["at_out_scaled"], 1)

            def body(item, prev, following):
                for kt in range(kt_n):
                    if following and kt == 0:
                        q(following)
                    if prev and kt == 4:
                        inverse(prev)
                    if prev and kt == 6:
                        rows(prev)
                    lows(item, kt)
                    if following and kt in max_at:
                        maxima(following, max_at[kt])
                    if kt == 7:
                        mod.reduce(dve, number(item), item[2])
                    if prev and kt == 9:
                        scaled(prev)

            def end(item):
                inverse(item)
                rows(item)
                scaled(item)

            q((0, 0, 0))
            for qi in range(4):
                maxima((0, 0, 0), qi)
            all_items(dve, body, end)
            mod.finish(dve, [1, 2, 3])

        @block.gpsimd
        def _(pool):
            def body(item, prev, following):
                g, h, half = item
                n = number(item)
                for kt in range(1, kt_n):
                    pool.wait_ge(c["at_exp"], n * kt_n + (kt + 3))
                    if kt == 1:
                        pool.wait_ge(c["at_summed"], n + 1)
                        first = m.probs[:, 0, :]
                    else:
                        pool.wait_ge(c["at_added"], n * adds + (adds + kt - 1))
                        first = m.added[:, half, :]
                    pool.tensor_tensor(m.added[:, half, :], first, m.probs[:, kt % PROBS, :],
                                       ALU.add).then_inc(c["at_added"], 1)
                    if kt == 1:
                        mod.product(pool, h + GROUP * g, half)

            after.split_first(pool, 0)
            all_items(pool, body, lambda item: None)


def pool_stage(nc, c, m, ins, pre, tail):
    pad = 8
    wide = T + 2 * pad
    split = HALF - pad
    widest = HALF + 4 * pad
    h_pad = m.at("pool_h", XN, [P, KD, wide])
    sums = m.at("pool_sums", XN + 4 * KD * wide, [P, 4, widest])
    inv = m.at("pool_inverse_counts", XN + 4 * KD * wide + 16 * widest, [P, 4, T])
    pre.begin(tail)
    pre.parts[1]["work"] = lambda k: h_pad[:, k, pad + HALF:pad + T]
    aff0 = pre.aff0

    def pooled(eng, name, places, t0, t1, ready):
        done = 0

        def step(ins):
            nonlocal done
            done += 1
            ins.then_inc(c[name], 1)
            eng.wait_ge(c[name], done)

        for k in range(KD):
            ready(k)
            ranges = [(pad + t0, pad + t1)]
            for i in range(k // 2, 0, -1):
                lo, hi = ranges[0]
                ranges.insert(0, (lo - 2 ** (i - 1), hi + 2 ** (i - 1)))
            src, base = h_pad[:, k, :], 0
            for i, (lo, hi) in enumerate(ranges):
                back, ahead = (1, 0) if i == 0 else (2 ** (i - 1), 2 ** (i - 1))
                out = sums[:, places + i % 2, 0:hi - lo]
                step(eng.tensor_tensor(out, src[:, lo - back - base:hi - back - base],
                                       src[:, lo + ahead - base:hi + ahead - base], ALU.add))
                src, base = sums[:, places + i % 2, :], lo
            out = m.a[:, k, t0:t1]
            step(eng.tensor_tensor(out, src[:, 0:t1 - t0], inv[:, k // 2, t0:t1], ALU.mult))
            step(eng.tensor_tensor(out, out, h_pad[:, k, pad + t0:pad + t1], ALU.subtract))

    with nc.Block() as block:
        @block.sync
        def _(sp):
            sp.dma_start(inv[:], ins["k_pool_inverse"].unsqueeze(0).to_broadcast([P, 4, T])
                         ).then_inc(c["pool_counts_in"], 16)

        @block.scalar
        def _(act):
            def copies():
                for k in range(KD):
                    act.activation(h_pad[:, k, pad:pad + HALF], pre.parts[0]["work"](k), ACT.Copy
                                   ).then_inc(c["pool_copied"], 1)

            pre.act(act, copies)

        @block.tensor
        def _(pe):
            for step in pre.pe_steps(pe):
                step()
            pre.pe_sums(pe, 1)
            pre.pe_spread(pe, 1)

        @block.vector
        def _(dve):
            def ready(k):
                if k == 0:
                    dve.wait_ge(c["pool_copied"], KD)
                    dve.wait_ge(c["pool_counts_in"], 16)
                dve.wait_ge(c["pre_shifted"], aff0 + KD + k + 1)

            pre.dve(dve)
            dve.wait_ge(c["pool_zeros"], 2)
            pooled(dve, "pool_second", 2, split, T, ready)

        @block.gpsimd
        def _(pool):
            def ready(k):
                pool.wait_ge(c["pool_copied"], k + 1)
                if k == 0:
                    pool.wait_ge(c["pool_counts_in"], 16)
                    tail.rms.summed(pool)

            pool.memset(h_pad[:, :, 0:pad], 0.0).then_inc(c["pool_zeros"], 1)
            pool.memset(h_pad[:, :, pad + T:wide], 0.0).then_inc(c["pool_zeros"], 1)
            pool.wait_ge(c["pool_zeros"], 2)
            pooled(pool, "pool_first", 0, 0, split, ready)


class Lru:

    def __init__(self, c, m, ins, pre):
        self.c, self.m, self.ins, self.pre = c, m, ins, pre
        self.n = 4
        self.bd = m.at("lru_gates", YX, [P, 2, self.n, P])
        self.small = m.at("lru_small", YX + 4096, [P, 12, self.n])
        squares = m.at("lru_squares", YX + 8192, [P, 4, HALF])
        self.rms = [RootMeanSquare(c, m, f"lru{h}", 1, self.n, 4, self.n * P,
                                   (lambda hh: lambda k: m.a[:, k, hh * HALF:(hh + 1) * HALF])(h),
                                   [squares[:, 2 * h + i, :] for i in range(2)],
                                   m.ps[:, 4 + h, 0:8], m.ps[:, 4 + h, P:2 * P],
                                   [m.ps[:, 6 + h, :]], 4 * h)
                    for h in range(2)]

    def xc(self, k):
        return self.m.a[:, 18 + 3 * (k % 2), :]

    def gi(self, k):
        return self.m.a[:, 19 + 3 * (k % 2), :]

    def mi(self, k):
        return self.m.a[:, 20 + 3 * (k % 2), :]

    def ra(self, k):
        return self.m.a[:, k, :]

    def gate_ps(self, which):
        return self.m.ps[:, 4 + 2 * which:6 + 2 * which, :].rearrange("p b t -> p (b t)")

    def pool(self, pool):
        self.pre.ready(pool, 0)
        pool.memset(self.bd[:], 0.0).then_inc(self.c["lru_zero"], 1)

    def begin(self, act):
        c, small = self.c, self.small
        act.wait_ge(c["lru_zero"], 1)
        for w, name in enumerate(("lru_gate_a_w_2", "lru_gate_x_w_2")):
            for odd in range(2):
                src = self.ins[name][0].rearrange("(b o) i j -> o i b j", o=2)[odd]
                s = slice(odd * 64, odd * 64 + 64)
                act.dma_start(self.bd[s, w, :, s], src).then_inc(c["lru_gates_in"], 16)
        act.wait_ge(c["lru_small"], 3)
        act.activation(small[:, 3, :], small[:, 2, :], ACT.Exp).then_inc(c["lru_u"], 1)

    def act(self, act, u):
        c, m, n, small = self.c, self.m, self.n, self.small
        k, odd = divmod(u - 8, 2)
        if k < n and not odd:
            if k >= 2:
                act.wait_ge(c["lru_y"], k - 1)
            act.activation(self.xc(k), m.a[:, k, :], ACT.Identity, bias=vcol(m, "lru_conv_b", k),
                           scale=vcol(m, "lru_conv_w", 12 + k)).then_inc(c["lru_centre"], 1)
            act.activation(m.a[:, 4 + k, :], m.a[:, 4 + k, :], ACT.Gelu_apprx_tanh
                           ).then_inc(c["lru_gelu"], 1)
        if k < n and odd:
            for w, (name, dst) in enumerate((("gate_a_b", self.ra(k)), ("gate_x_b", self.gi(k)))):
                act.wait_ge(c["lru_gate"], 2 * k + w + 1)
                act.activation(dst, self.gate_ps(w), ACT.Sigmoid, bias=vcol(m, name, k)
                               ).then_inc(c["lru_sigmoid"], 1)
        k -= 1
        if 0 <= k < n and not odd:
            act.wait_ge(c["lru_coefs"], 2)
            act.wait_ge(c["lru_sigmoid"], 2 * k + 2)
            act.activation(self.mi(k), self.ra(k), ACT.Tanh, scale=small[:, 10, k:k + 1]
                           ).then_inc(c["lru_tanh"], 1)
            act.wait_ge(c["lru_tanh"], k + 1)
            act.activation(self.ra(k), self.ra(k), ACT.Exp, scale=small[:, 11, k:k + 1]
                           ).then_inc(c["lru_a"], 1)
            act.wait_ge(c["lru_a"], k + 1)
            act.wait_ge(c["lru_ix"], k + 1)
            act.activation(self.xc(k), self.ra(k), ACT.Square).then_inc(c["lru_a2"], 1)
        if 0 <= k < n and odd:
            act.wait_ge(c["lru_m2"], k + 1)
            act.activation(self.mi(k), self.mi(k), ACT.Sqrt).then_inc(c["lru_m"], 1)
        if u == 18:
            for h in range(2):
                self.rms[h].act_squares(act, lambda i: act.wait_ge(c["lru_y"], i + 1))
        if u == 19:
            for h in range(2):
                self.rms[h].act_root(act)

    def pe(self, pe, u):
        c, n = self.c, self.n
        k, odd = divmod(u - 8, 2)
        if u == 8:
            pe.wait_ge(c["lru_gates_in"], 64)
        if k < n and odd:
            pe.wait_ge(c["lru_side"], 3 * k + 3)
            for w in range(2):
                if k:
                    pe.wait_ge(c["lru_sigmoid"], 2 * k + w - 1)
                for h in range(2):
                    last = pe.matmul(self.m.ps[:, 4 + 2 * w + h, :], self.bd[:, w, k, :],
                                     self.xc(k)[:, h * HALF:(h + 1) * HALF], start=True, stop=True)
                last.then_inc(c["lru_gate"], 1)
        if u == 19:
            for h in range(2):
                self.rms[h].pe_sums(pe)
        if u == 20:
            for h in range(2):
                self.rms[h].pe_turn(pe)
        if u == 21:
            for h in range(2):
                self.rms[h].pe_broadcast(pe, 0)

    def dve(self, dve):
        c, m, n, small = self.c, self.m, self.n, self.small
        lam = m.vt[:, m.col["lambda"]:m.col["lambda"] + n]
        terms, done = 8, 0

        def step(ins):
            nonlocal done
            done += 1
            ins.then_inc(c["lru_small"], 1)
            dve.wait_ge(c["lru_small"], done)

        step(dve.tensor_scalar(small[:, 0, :], lam, -1.0, None, ALU.mult))
        step(dve.tensor_scalar(small[:, 1, :], small[:, 0, :], 0.0, None, ALU.max))
        step(dve.tensor_tensor(small[:, 2, :], small[:, 0, :], lam, ALU.min))
        dve.wait_ge(c["lru_u"], 1)
        step(dve.tensor_scalar(small[:, 4, :], small[:, 3, :], 2.0, None, ALU.add))
        step(dve.reciprocal(small[:, 5, :], small[:, 4, :]))
        step(dve.tensor_tensor(small[:, 6, :], small[:, 3, :], small[:, 5, :], ALU.mult))
        step(dve.tensor_tensor(small[:, 7, :], small[:, 6, :], small[:, 6, :], ALU.mult))
        step(dve.tensor_scalar(small[:, 8, :], small[:, 7, :], 1.0 / (2 * terms + 1), None,
                               ALU.mult))
        for i in range(terms - 1, 0, -1):
            step(dve.scalar_tensor_tensor(out=small[:, 8, :], in0=small[:, 8, :],
                                          scalar=1.0 / (2 * i + 1), in1=small[:, 7, :],
                                          op0=ALU.add, op1=ALU.mult))
        step(dve.scalar_tensor_tensor(out=small[:, 8, :], in0=small[:, 8, :], scalar=1.0,
                                      in1=small[:, 6, :], op0=ALU.add, op1=ALU.mult))
        step(dve.scalar_tensor_tensor(out=small[:, 9, :], in0=small[:, 8, :], scalar=2.0,
                                      in1=small[:, 1, :], op0=ALU.mult, op1=ALU.add))
        dve.tensor_scalar(small[:, 10, :], small[:, 9, :], LRU_C, None, ALU.mult
                          ).then_inc(c["lru_coefs"], 1)
        dve.tensor_scalar(small[:, 11, :], small[:, 9, :], -LRU_C, None, ALU.mult
                          ).then_inc(c["lru_coefs"], 1)

        def sides(k):
            dve.wait_ge(c["lru_centre"], k + 1)
            xc = self.xc(k)
            for tap in range(3):
                back = 3 - tap
                if tap:
                    dve.wait_ge(c["lru_side"], 3 * k + tap)
                dve.scalar_tensor_tensor(
                    out=xc[:, back:T], in0=m.a[:, k, 0:T - back],
                    scalar=vcol(m, "lru_conv_w", 4 * tap + k), in1=xc[:, back:T],
                    op0=ALU.mult, op1=ALU.add).then_inc(c["lru_side"], 1)

        def gated(k):
            dve.wait_ge(c["lru_sigmoid"], 2 * k + 2)
            dve.tensor_tensor(self.gi(k), self.gi(k), self.xc(k), ALU.mult
                              ).then_inc(c["lru_ix"], 1)

        def factor(k):
            dve.wait_ge(c["lru_a2"], k + 1)
            dve.scalar_tensor_tensor(out=self.mi(k), in0=self.xc(k), scalar=1.0, in1=self.mi(k),
                                     op0=ALU.add, op1=ALU.mult).then_inc(c["lru_m2"], 1)

        def scan(k):
            dve.wait_ge(c["lru_m"], k + 1)
            dve.tensor_tensor(self.mi(k), self.mi(k), self.gi(k), ALU.mult
                              ).then_inc(c["lru_in"], 1)
            dve.wait_ge(c["lru_in"], k + 1)
            dve.tensor_tensor_scan(self.xc(k), self.ra(k), self.mi(k), 0.0, ALU.mult, ALU.add
                                   ).then_inc(c["lru_scan"], 1)
            dve.wait_ge(c["lru_gelu"], k + 1)
            dve.wait_ge(c["lru_scan"], k + 1)
            dve.tensor_tensor(m.a[:, k, :], self.xc(k), m.a[:, 4 + k, :], ALU.mult
                              ).then_inc(c["lru_y"], 1)

        for k in range(n + 1):
            if k < n:
                sides(k)
            if k:
                factor(k - 1)
            if k:
                scan(k - 1)
            if k < n:
                gated(k)
        for h in range(2):
            self.rms[h].dve_sums(dve)
        for h in range(2):
            self.rms[h].dve_inverse(dve, sums=False)
        for h in range(2):
            self.rms[h].dve_row(dve)
        for h in range(2):
            bank = self.rms[h].ready(dve, 0)
            for k in range(n):
                y = m.a[:, k, h * HALF:(h + 1) * HALF]
                dve.scalar_tensor_tensor(out=y, in0=y, scalar=vcol(m, "lru_norm", k), in1=bank,
                                         op0=ALU.mult, op1=ALU.mult).then_inc(c["lru_out"], 1)


def retention_stage(nc, c, m, ins):
    nh = RET_HEADS
    q, k, v, gate = (m.a[:, 8 + 4 * i:12 + 4 * i, :] for i in range(4))
    t = m.at("ret_work", XN, [P, 16, T])
    cos, sin = t[:, 0, :], t[:, 1, :]
    direct, swapped = t[:, 2, :], t[:, 3, :]
    v_rows = t[:, 4:8, :].rearrange("p a (b e) -> p (a b) e", b=2)
    k_rows = t[:, 8:12, :].rearrange("p a (b e) -> p (a b) e", b=2)
    decay = t[:, 12, 0:HALF]
    q_decay = t[:, 12, HALF:T]
    state = [t[:, 13, 0:HALF], t[:, 13, HALF:T]]
    masked = [t[:, 14, 0:HALF], t[:, 14, HALF:T]]
    q_scaled = [t[:, 15, 0:HALF], t[:, 15, HALF:T]]
    perm = m.at("ret_perm", YX, [P, P])
    zeta = m.at("ret_zeta", YX + 512, [P, nh])
    squares = m.at("ret_squares", YX + 8192, [P, 4, HALF])
    carry = [float(np.exp(np.float32(P) * np.float32(g))) for g in RET_DECAY]
    items = [(x, h, slice(half * HALF, (half + 1) * HALF)) for h in range(nh)
             for x in (q, k) for half in range(2)]
    outs = [(h, slice(half * HALF, (half + 1) * HALF)) for h in range(nh) for half in range(2)]
    rms = RootMeanSquare(c, m, "ret", len(outs), 1, 4, P, lambda i: v[:, outs[i][0], outs[i][1]],
                         [squares[:, i, :] for i in range(4)], m.ps[:, 4, :], m.ps[:, 5, :],
                         [m.ps[:, 6, :], m.ps[:, 7, :]], 0)

    with nc.Block() as block:
        @block.sync
        def _(sp):
            sp.dma_start(perm[:], ins["k_perm2"]).then_inc(c["ret_in"], 16)
            sp.dma_start(cos, ins["k_cos2"]).then_inc(c["ret_in"], 16)
            sp.dma_start(sin, ins["k_sin2"]).then_inc(c["ret_in"], 16)
            sp.dma_start(decay, ins["k_decay"]).then_inc(c["ret_in"], 16)
            sp.dma_start(q_decay, ins["k_q_decay"].unsqueeze(0).to_broadcast([P, HALF])
                         ).then_inc(c["ret_in"], 16)
            sp.dma_start(zeta[:], ins["k_zeta"]).then_inc(c["ret_in"], 16)

        @block.tensor
        def _(pe):
            pe.wait_ge(c["ret_in"], 96)
            for i, (x, h, s) in enumerate(items):
                if i >= 2:
                    pe.wait_ge(c["ret_sin"], i - 1)
                pe.matmul(m.ps[:, i % 2, :], perm[:], x[:, h, s], start=True, stop=True
                          ).then_inc(c["ret_swapped"], 1)
            for n in range(TT):
                tok = slice(n * P, (n + 1) * P)
                for w, x in enumerate((v, k)):
                    j = 2 * n + w
                    if w == 0 and n == 0:
                        pe.wait_ge(c["ret_rotated"], len(items))
                    if j >= 2:
                        pe.wait_ge(c["ret_rows_v" if w == 0 else "ret_rows_k"], n)
                    for h in range(nh):
                        last = pe.transpose(m.ps[:, 2 + w, h * P:(h + 1) * P], x[:, h, tok],
                                            m.ident[:])
                    last.then_inc(c["ret_turned"], 1)

            def scores(n):
                tok = slice(n * P, (n + 1) * P)
                if n == 1:
                    pe.wait_ge(c["ret_rows_v"], TT)
                    pe.wait_ge(c["ret_rows_k"], TT)
                if n >= 2:
                    pe.wait_ge(c["ret_masked"], n - 1)
                for h in range(nh):
                    last = pe.matmul(m.ps[:, 2 * (n % 2), h * P:(h + 1) * P], k[:, h, tok],
                                     q[:, h, tok], start=True, stop=True)
                last.then_inc(c["ret_scores"], 1)

            def products(n):
                pe.wait_ge(c["ret_rows_v"], n + 1)
                pe.wait_ge(c["ret_rows_k"], n + 1)
                if n >= 2:
                    pe.wait_ge(c["ret_state"], nh * (n - 1))
                for h in range(nh):
                    hs = slice(h * P, (h + 1) * P)
                    last = pe.matmul(m.ps[:, 1 + 2 * (n % 2), hs], k_rows[:, n, hs],
                                     v_rows[:, n, hs], start=True, stop=True)
                last.then_inc(c["ret_kv"], 1)

            scores(0)
            products(0)
            for n in range(TT):
                if n + 1 < TT:
                    scores(n + 1)
                if n + 1 < TT - 1:
                    products(n + 1)
                pe.wait_ge(c["ret_rows_v"], n + 1)
                pe.wait_ge(c["ret_masked"], n + 1)
                if n >= 2:
                    pe.wait_ge(c["ret_copied"], n - 1)
                if n:
                    pe.wait_ge(c["ret_q_scaled"], n)
                    pe.wait_ge(c["ret_state"], nh * n)
                for h in range(nh):
                    hs = slice(h * P, (h + 1) * P)
                    out = m.ps[:, 6 + n % 2, hs]
                    last = pe.matmul(out, v_rows[:, n, hs], masked[n % 2][:, hs], start=True,
                                     stop=(n == 0))
                    if n:
                        last = pe.matmul(out, state[n % 2][:, hs], q_scaled[n % 2][:, hs],
                                         start=False, stop=True)
                last.then_inc(c["ret_out"], 1)
            for i, (h, s) in enumerate(outs):
                if i == 0:
                    pe.wait_ge(c["ret_copied"], TT)
                if i >= 2:
                    pe.wait_ge(c["ret_centred"], i - 1)
                pe.matmul(m.ps[:, i % 2, :], m.ones[:, 0:1].to_broadcast([P, P]), v[:, h, s],
                          start=True, stop=True).then_inc(c["ret_sums"], 1)
            rms.pe_sums(pe)
            rms.pe_turn(pe)
            for g in range(len(outs)):
                rms.pe_broadcast(pe, g)

        @block.scalar
        def _(act):
            for n in range(TT):
                act.wait_ge(c["ret_turned"], 2 * n + 1)
                act.activation(v_rows[:, n, :], m.ps[:, 2, :], ACT.Copy
                               ).then_inc(c["ret_rows_v"], 1)
            for n in range(TT):
                act.wait_ge(c["ret_out"], n + 1)
                act.activation(v[:, :, n * P:(n + 1) * P], two(m.ps[:, 6 + n % 2, :], nh), ACT.Copy
                               ).then_inc(c["ret_copied"], 1)
            for h in range(nh):
                act.activation(gate[:, h, :], gate[:, h, :], ACT.Silu).then_inc(c["ret_silu"], 1)
            rms.act_squares(act, lambda i: act.wait_ge(c["ret_centred"], i + 1))
            rms.act_root(act)

        @block.gpsimd
        def _(pool):
            pool.wait_ge(c["ret_in"], 96)
            for i, (x, h, s) in enumerate(items):
                if i >= 2:
                    pool.wait_ge(c["ret_rotated"], i - 1)
                pool.tensor_tensor(two(direct)[:, i % 2, :], x[:, h, s], cos[:, s], ALU.mult
                                   ).then_inc(c["ret_direct"], 1)
            pool.wait_ge(c["ret_rotated"], len(items))
            for n in range(1, TT):
                if n >= 3:
                    pool.wait_ge(c["ret_out"], n - 1)
                pool.tensor_tensor(two(q_scaled[n % 2], nh), q[:, :, n * P:(n + 1) * P],
                                   two(q_decay, nh), ALU.mult).then_inc(c["ret_q_scaled"], 1)

        @block.vector
        def _(dve):
            dve.wait_ge(c["ret_in"], 96)
            for i, (x, h, s) in enumerate(items):
                dve.wait_ge(c["ret_swapped"], i + 1)
                dve.tensor_tensor(two(swapped)[:, i % 2, :], m.ps[:, i % 2, :], sin[:, s],
                                  ALU.mult).then_inc(c["ret_sin"], 1)
                dve.wait_ge(c["ret_sin"], i + 1)
                dve.wait_ge(c["ret_direct"], i + 1)
                dve.tensor_tensor(x[:, h, s], two(direct)[:, i % 2, :], two(swapped)[:, i % 2, :],
                                  ALU.add).then_inc(c["ret_rotated"], 1)
            for n in range(TT):
                dve.wait_ge(c["ret_turned"], 2 * n + 2)
                dve.tensor_tensor(two(k_rows[:, n, :], nh), two(m.ps[:, 3, :], nh),
                                  zeta[:].unsqueeze(2).to_broadcast([P, nh, P]), ALU.mult
                                  ).then_inc(c["ret_rows_k"], 1)
            for n in range(TT):
                dve.wait_ge(c["ret_scores"], n + 1)
                if n >= 2:
                    dve.wait_ge(c["ret_out"], n - 1)
                dve.tensor_tensor(masked[n % 2], m.ps[:, 2 * (n % 2), :], decay, ALU.mult
                                  ).then_inc(c["ret_masked"], 1)
                if n < TT - 1:
                    dve.wait_ge(c["ret_kv"], n + 1)
                    if n >= 1:
                        dve.wait_ge(c["ret_out"], n)
                        dve.wait_ge(c["ret_state"], nh * n)
                    for h in range(nh):
                        hs = slice(h * P, (h + 1) * P)
                        if n == 0:
                            dve.tensor_copy(state[1][:, hs], m.ps[:, 1 + 2 * (n % 2), hs]
                                            ).then_inc(c["ret_state"], 1)
                        else:
                            dve.scalar_tensor_tensor(
                                out=state[(n + 1) % 2][:, hs], in0=state[n % 2][:, hs],
                                scalar=carry[h], in1=m.ps[:, 1 + 2 * (n % 2), hs], op0=ALU.mult, op1=ALU.add
                                ).then_inc(c["ret_state"], 1)
            for i, (h, s) in enumerate(outs):
                dve.wait_ge(c["ret_sums"], i + 1)
                dve.scalar_tensor_tensor(out=v[:, h, s], in0=m.ps[:, i % 2, :], scalar=-1.0 / P,
                                         in1=v[:, h, s], op0=ALU.mult, op1=ALU.add
                                         ).then_inc(c["ret_centred"], 1)
            rms.dve_inverse(dve)
            rms.dve_row(dve)
            for i, (h, s) in enumerate(outs):
                bank = rms.ready(dve, i)
                rms.used(dve.scalar_tensor_tensor(
                    out=v[:, h, s], in0=v[:, h, s], scalar=vcol(m, "ret_norm", h), in1=bank,
                    op0=ALU.mult, op1=ALU.mult))
                dve.wait_ge(c["rms_broadcast_used"], rms.free0 + i + 1)
                dve.wait_ge(c["ret_silu"], h + 1)
                dve.tensor_tensor(m.a[:, 4 + h, s], v[:, h, s], gate[:, h, s], ALU.mult
                                  ).then_inc(c["ret_done"], 1)


def final_stage(nc, c, m, out, pre, tail):
    pre.begin(tail)
    rows = m.at("out_rows", XN, [P, TT, D])
    out_tiles = out.rearrange("b (t p) d -> (b t) p d", p=P)
    groups = list(enumerate((t, g) for t in range(TT) for g in range(2)))
    with nc.Block() as block:
        @block.scalar
        def _(act):
            pre.act(act)

        @block.tensor
        def _(pe):
            for i, (t, g) in groups:
                if i == 4:
                    pre.pe_sums(pe, 1)
                if i == 8:
                    pre.pe_spread(pe, 1)
                pe.wait_ge(c["pre_shifted"], pre.aff0 + KD * (t // 4 + 1))
                if i >= 4:
                    pe.wait_ge(c["out_copied"], i - 3)
                for q in range(4):
                    k = 4 * g + q
                    last = pe.transpose(m.ps[:, i % 4, q * P:(q + 1) * P],
                                        pre.parts[t // 4]["work"](k)[:, t % 4 * P:(t % 4 + 1) * P],
                                        m.ident[:])
                last.then_inc(c["out_turned"], 1)

        @block.vector
        def _(dve):
            def copies(tiles):
                for i, (t, g) in groups[tiles]:
                    dve.wait_ge(c["out_turned"], i + 1)
                    dve.tensor_copy(rows[:, t, g * HALF:(g + 1) * HALF], m.ps[:, i % 4, :]
                                    ).then_inc(c["out_copied"], 1)

            for step in tail.dve_steps(dve):
                step()
            tail.dve(dve)
            pre.rms[1].dve_sums(dve)
            copies(slice(0, TT))
            pre.rms[1].dve_inverse(dve, sums=False)
            pre.rms[1].dve_row(dve)
            tail.wait(dve, KD - 1)
            pre.dve_scale(dve, 1)
            copies(slice(TT, 2 * TT))

        @block.sync
        def _(sp):
            for t in range(TT):
                sp.wait_ge(c["out_copied"], 2 * t + 2)
                sp.dma_start(out_tiles[t], rows[:, t, :]).then_inc(c["out_stored"], 16)
            sp.wait_ge(c["out_stored"], 16 * TT)


def qkv_norm(c, m):
    parts = halves_parts(m, lambda k: m.coef[:, 0, 0, k:k + 1], lambda k: mod_col(m, 0, 0, k),
                         squares=5)
    parts.append(dict(
        source=lambda k: m.ctx_cm[:, k, :], work=lambda k: m.ctx_cm[:, k, :],
        hi=lambda k: m.xnc_hi[:, k, :], lo=lambda k: m.xnc_lo[:, k, :],
        scale=lambda k: m.coef_ctx[:, k:k + 1], shift=lambda k: mod_col(m, 0, 0, k, 1), tiles=2,
        stat=m.ps[:, 1, 72:74], turned=m.ps[:, 1, P:2 * P], bank=m.ps[:, 1, 256:512], small=8,
        squares=[m.a[:, 23, i * CTX:(i + 1) * CTX] for i in range(4)]))
    for h, part in enumerate(parts[:2]):
        bank = 1 - h
        part.update(stat=m.ps[:, bank, 64:68], turned=m.ps[:, bank, P:2 * P],
                    bank=m.ps[:, 2 + h, :])
    return PreNorm(c, m, "qkv", parts, early=3)


def weight_streams(c, m, ins):
    def wide(w, first, second):
        v = w.rearrange("(k p) n -> p k n", p=P)
        return [v[:, :, first:first + P], v[:, :, second:second + P]]

    def tall(w):
        v = w.rearrange("(k p) n -> p k n", p=P)
        return [v[:, 0:8, 0:P], v[:, 8:16, 0:P]]

    streams = {}

    def add(name, units, first):
        streams[name] = WeightStream(c, m, units, first)

    add("qkv", 12, wide(ins["w_qkv"][0], 0, P))
    add("w_o", 2 * KD, wide(ins["w_o"][0], 0, P))
    add("up0", 2 * FF1, wide(ins["w_up"][0], 0, FF1 * P))
    add("down0", 6 * KD, tall(ins["w_down"][0]))
    add("w_pool", 2 * KD, wide(ins["w_pool"][0, 0], 0, P))
    add("up1", 2 * FF1, wide(ins["w_up"][1], 0, FF1 * P))
    add("down1", 6 * KD, tall(ins["w_down"][1]))
    add("w_in", 24, wide(ins["w_in_2"][0], 0, P))
    add("w_out", 2 * KD, wide(ins["w_out_2"][0], 0, P))
    add("up2", 2 * FF2, wide(ins["ffn_up_w_2"][0], 0, FF2 * P))
    add("down2", 6 * KD, tall(ins["ffn_down_w_2"][0]))
    return streams


def build(nc, ins, out):
    c = Counters(nc)
    m = Memory(nc)
    x_dram = nc.dram_tensor("x_scratch", [P, KD, T], F32).ap()
    streams = weight_streams(c, m, ins)
    load_vectors(nc, c, m, ins, streams["qkv"], qkv_norm)
    m.gains_sw = m.vec("gains_sw", [P, 2])
    m.at_max, m.at_inv = m.vec("at_max", [P, 4]), m.vec("at_inv", [P, 4])
    m.at_rows = m.rms_row[0]
    m.mod_acc = m.vec("mod_acc", [P, 2 * P])
    attention_memory(m)

    project_stage(nc, c, m, "qkv", m.qkv_norm, None, streams["qkv"], None,
                  ins["w_qkv"][0], 12, HEADS,
                  lambda u: (m.a[:, bass.ds(u, 1), :].rearrange("p o t -> p (o t)")
                             if not isinstance(u, int) or u < HEADS
                             else m.kv_raw[:, u - HEADS, CTX:KEYS]),
                  lambda u: m.kv_raw[:, u - HEADS, 0:CTX])
    rotate_stage(nc, c, m, ins)
    attention_stage(nc, c, m, Modulation(c, m, ins["w_mod"], 0, 16, 16, m.mod_buf, m.mod_acc,
                                         m.ps[:, 7, 0:32]), streams["w_o"])

    def ffn_pre(layer):
        return PreNorm(c, m, f"up{layer}", halves_parts(
            m, lambda k: m.coef[:, layer, 2, k:k + 1], lambda k: mod_col(m, layer, 3, k),
            squares=6, early=True), early=1)

    w_o = ins["w_o"][0].rearrange("(k p) n -> p k n", p=P)
    pre = ffn_pre(0)
    tail = down_stage(nc, c, m, "w_o", KD, [KD], streams["w_o"], streams["up0"], pre,
               lambda i, b, g: w_o[:, :, bass.ds(i * 256 + b * P, P)],
               lambda i, b: 0, None, lambda k: m.coef[:, 0, 1, k:k + 1], x_dram, False, True)

    def ffn(layer, pre, tail, after, after_stream, x_store):
        cw, cb = m.col[f"conv_w{layer}"], m.col["conv_b"] + layer * FF1
        ffn_up_stage(nc, c, m, f"up{layer}", pre, tail, streams[f"up{layer}"],
                     streams[f"down{layer}"], ins["w_up"][layer], FF1,
                     lambda tap, j: m.vt[:, bass.ds(j + (cw + tap * FF1), 1)],
                     lambda j: m.vt[:, bass.ds(j + cb, 1)], False,
                     None if layer else Modulation(
                         c, m, ins["w_mod"], 1, 0, 24,
                         [m.at("mod_buf_up0", A0 + 22 * 4096, [P, KD, 2 * P]),
                          m.at("mod_buf_up1", YX + 8192, [P, KD, 2 * P])], m.mod_acc,
                         m.ps[:, 4, 64:112]))
        w = ins["w_down"][layer].rearrange("(k p) n -> p k n", p=P)
        sizes = [8, 8, 6]
        after = after()
        tail = down_stage(nc, c, m, f"down{layer}", FF1, sizes, streams[f"down{layer}"], after_stream,
                   after,
                   lambda i, b, g: w[:, 8 * g:8 * g + sizes[g], bass.ds(i * 256 + b * P, P)],
                   lambda i, b: 0, None, lambda k: m.coef[:, layer, 3, k:k + 1], x_dram, True,
                   x_store)
        return after, tail

    pre, tail = ffn(0, pre, tail, lambda: PreNorm(c, m, "pool", halves_parts(
        m, lambda k: m.coef[:, 1, 0, k:k + 1], lambda k: mod_col(m, 1, 0, k), early=True),
        split=False, early=1), streams["w_pool"], False)
    pool_stage(nc, c, m, ins, pre, tail)
    w_pool = ins["w_pool"][0].rearrange("g (k p) n -> p g k n", p=P)
    bps = m.vec("pool_bias", [P, KD])
    with nc.Block() as block:
        @block.vector
        def _(dve):
            dve.tensor_tensor(bps[:], m.vt[:, m.col["b_pool"]:m.col["b_pool"] + KD],
                              m.vt[:, m.col["pool_scale"]:m.col["pool_scale"] + KD], ALU.mult
                              ).then_inc(c["pool_bias"], 1)
    pre = ffn_pre(1)
    tail = down_stage(nc, c, m, "w_pool", KD, [2], streams["w_pool"], streams["up1"], pre,
               lambda i, b, g: w_pool[:, bass.ds(i, 1), :, b * P:(b + 1) * P].rearrange(
                   "p g k n -> p (g k) n"),
               lambda i, b: 2 * i,
               (lambda n: m.vt[:, bass.ds(n + m.col["pool_scale"], 1)],
                lambda n: bps[:, bass.ds(n, 1)]),
               lambda k: m.coef[:, 1, 1, k:k + 1], x_dram, False, True)
    pre, tail = ffn(1, pre, tail, lambda: PreNorm(c, m, "w_in", halves_parts(
        m, lambda k: vcol(m, "norm1", k), lambda k: 0.0, early=True), early=1),
        streams["w_in"], True)
    project_stage(nc, c, m, "w_in", pre, tail, streams["w_in"], streams["w_out"], ins["w_in_2"][0], 24, 24,
                  lambda u: m.a[:, bass.ds(u, 1), :].rearrange("p o t -> p (o t)"), None,
                  lambda: Lru(c, m, ins, pre))
    retention_stage(nc, c, m, ins)
    w_out = ins["w_out_2"][0].rearrange("(k p) n -> p k n", p=P)
    pre = PreNorm(c, m, "up2", halves_parts(m, lambda k: vcol(m, "norm2", k), lambda k: 0.0,
                                            early=True), early=1)
    tail = down_stage(nc, c, m, "w_out", KD, [KD], streams["w_out"], streams["up2"], pre,
               lambda i, b, g: w_out[:, :, bass.ds(i * 256 + b * P, P)],
               lambda i, b: 0, None, None, x_dram, True, True)
    ffn_w = [m.col[f"ffn_w{tap}"] for tap in range(3)]
    ffn_up_stage(nc, c, m, "up2", pre, tail, streams["up2"], streams["down2"], ins["ffn_up_w_2"][0], FF2,
                 lambda tap, j: m.vt[:, bass.ds(j + ffn_w[tap], 1)],
                 lambda j: m.vt[:, bass.ds(j + m.col["ffn_b"], 1)], True)
    w_d = ins["ffn_down_w_2"][0].rearrange("(k p) n -> p k n", p=P)
    pre = PreNorm(c, m, "final", halves_parts(m, lambda k: vcol(m, "final", k), lambda k: 0.0,
                                              early=True), split=False, early=1)
    tail = down_stage(nc, c, m, "down2", FF2, [8, 8, 8], streams["down2"], None, pre,
               lambda i, b, g: w_d[:, 8 * g:8 * g + 8, bass.ds(i * 256 + b * P, P)],
               lambda i, b: 0, None, None, x_dram, True, False)
    final_stage(nc, c, m, out, pre, tail)


_INS = ["x", "c", "ctx", "c_ctx", "w_mod", "b_mod", "g_pre_mix", "g_post_mix", "g_pre_ffn",
        "g_post_ffn", "w_qkv", "g_q", "g_k", "w_o", "w_pool", "b_pool", "pool_scale", "w_up",
        "conv_w", "conv_b", "w_down", "norm1_gain_2", "w_in_2", "lru_conv_w_2", "lru_conv_b_2",
        "lru_gate_a_w_2", "lru_gate_a_b_2", "lru_gate_x_w_2", "lru_gate_x_b_2", "lru_lambda_2",
        "lru_norm_gain_2", "ret_norm_gain_2", "w_out_2", "norm2_gain_2", "ffn_up_w_2",
        "ffn_conv_w_2", "ffn_conv_b_2", "ffn_down_w_2", "final_norm_gain_2"]


def constants():
    f = np.float32
    t = np.arange(T)
    d = np.arange(P)
    inv = (f(10000.0) ** (-np.arange(32, dtype=f) / f(32))).astype(f)
    pos = np.where((d // 64)[:, None] == 0, (t // 64)[None], (t % 64)[None]).astype(f)
    ang = (pos * inv[d % 32][:, None]).astype(f)
    sign = np.where(d % 64 < 32, -1, 1).astype(f)[:, None]
    k = {"k_ident": np.eye(P, dtype=f), "k_cos1": np.cos(ang), "k_sin1": sign * np.sin(ang),
         "k_perm1": np.eye(P, dtype=f)[d ^ 32]}
    inv = (f(10000.0) ** (-np.arange(0, P, 2, dtype=f) / f(P))).astype(f)
    ang = (t.astype(f)[None] * inv[d % 64][:, None]).astype(f)
    sign = np.where(d < 64, -1, 1).astype(f)[:, None]
    k.update(k_cos2=np.cos(ang), k_sin2=sign * np.sin(ang), k_perm2=np.eye(P, dtype=f)[d ^ 64])
    k["k_pool_inverse"] = np.stack([
        1.0 / (np.minimum(t + w - w // 2, T) - np.maximum(t - w // 2, 0)) for w in (2, 4, 8, 16)])
    log_g = np.log1p(-np.exp2(f(-5.0) - np.arange(RET_HEADS, dtype=f))).astype(f)
    diff = (d[None, :] - d[:, None]).astype(f)
    decay = np.where(diff >= 0, np.exp(np.maximum(diff, 0)[:, None, :] * log_g[None, :, None])
                     .transpose(1, 0, 2), 0.0)
    k["k_decay"] = (decay.transpose(1, 0, 2) * RET_SCALE).reshape(P, RET_HEADS * P)
    k["k_zeta"] = np.exp((P - 1 - d).astype(f)[:, None] * log_g[None, :]) * RET_SCALE
    k["k_q_decay"] = np.exp((d + 1).astype(f)[None, :] * log_g[:, None]).reshape(-1)
    return {name: np.ascontiguousarray(v.astype(f)) for name, v in k.items()}


def kernel(**inputs):
    import concourse.bacc as bacc
    from concourse.bass_utils import run_bass_kernel_spmd as run

    nc = bacc.Bacc("TRN2", target_bir_lowering=False, num_devices=1)
    arrays, ins = {}, {}
    for name, a in [(n, np.ascontiguousarray(inputs[n])) for n in _INS] + list(constants().items()):
        arrays[f"in_{name}"] = a
        ins[name] = nc.dram_tensor(f"in_{name}", a.shape, mybir.dt.from_np(a.dtype),
                                   kind="ExternalInput").ap()
    out = nc.dram_tensor("out_x", [1, T, D], F32, kind="ExternalOutput").ap()
    build(nc, ins, out)
    r = run(nc, [arrays], core_ids=[0])
    return r.results[0]["out_x"]
```
